# Optimizing a Trainium2 kernel written in Bass

```python
import functools
import jax, jax.numpy as jnp
from jax import lax
import numpy as np

D_MODEL = 1024
BATCH = 1
SEQ = 256
DEPTH = 2

CHUNK = 64
Q_BLOCK = 128
MLA_HEADS = 8
MLA_NOPE = 64
MLA_ROPE = 32
MLA_V = 64
Q_LORA = 384
KV_LORA = 256
ROPE_THETA = 10000.0
SB_HEADS = 8
SB_DIM = 64
C_HEADS = 16
C_DIM = 64
LEFT_CHUNKS = 8
BAND = (LEFT_CHUNKS + 1) * CHUNK
REL_CLIP = 256
D_FF = -(-8 * D_MODEL // (3 * 256)) * 256
EVEN_IN = Q_LORA + KV_LORA + MLA_ROPE + 3 * SB_HEADS * SB_DIM
MIX_EVEN = MLA_HEADS * MLA_V + SB_HEADS * SB_DIM
MIX_ODD = C_HEADS * C_DIM
N_EVEN = (DEPTH + 1) // 2
N_ODD = DEPTH // 2
RMS_EPS = 1e-6


def rms_norm(x, g):
    x32 = x.astype(jnp.float32)
    y = x32 * lax.rsqrt(jnp.mean(x32 * x32, axis=-1, keepdims=True) + RMS_EPS)
    return (y * g.astype(jnp.float32)).astype(x.dtype)

def rope_tables(seq, dim):
    pos = jnp.arange(seq, dtype=jnp.float32)
    inv_freq = ROPE_THETA ** (-jnp.arange(0, dim, 2, dtype=jnp.float32) / dim)
    ang = pos[:, None] * inv_freq[None, :]
    return jnp.cos(ang), jnp.sin(ang)

def apply_rope(x, cos, sin):
    half = x.shape[-1] // 2
    c, s = cos.astype(x.dtype), sin.astype(x.dtype)
    x1, x2 = x[..., :half], x[..., half:]
    return jnp.concatenate([x1 * c - x2 * s, x2 * c + x1 * s], axis=-1)

def swiglu(u, w_gate, w_up, w_down):
    return (jax.nn.silu(u @ w_gate) * (u @ w_up)) @ w_down

def mla_stick_breaking_mixer(u, w_in, g_cq, w_uq, g_ckv, w_ukv, w_out):
    bsz, seq, _ = u.shape
    proj = u @ w_in
    o1 = Q_LORA
    o2 = o1 + KV_LORA
    o3 = o2 + MLA_ROPE
    nb = SB_HEADS * SB_DIM
    c_q, c_kv, k_r = proj[..., :o1], proj[..., o1:o2], proj[..., o2:o3]
    q_b = proj[..., o3:o3 + nb].reshape(bsz, seq, SB_HEADS, SB_DIM)
    k_b = proj[..., o3 + nb:o3 + 2 * nb].reshape(bsz, seq, SB_HEADS, SB_DIM)
    v_b = proj[..., o3 + 2 * nb:].reshape(bsz, seq, SB_HEADS, SB_DIM)

    cos, sin = rope_tables(seq, MLA_ROPE)
    q_a = (rms_norm(c_q, g_cq) @ w_uq).reshape(bsz, seq, MLA_HEADS, MLA_NOPE + MLA_ROPE)
    q_a = jnp.concatenate([q_a[..., :MLA_NOPE],
                           apply_rope(q_a[..., MLA_NOPE:], cos[:, None, :], sin[:, None, :])], axis=-1)
    kv = (rms_norm(c_kv, g_ckv) @ w_ukv).reshape(bsz, seq, MLA_HEADS, MLA_NOPE + MLA_V)
    k_rope = apply_rope(k_r, cos, sin)
    k_a = jnp.concatenate([kv[..., :MLA_NOPE],
                           jnp.broadcast_to(k_rope[:, :, None, :], (bsz, seq, MLA_HEADS, MLA_ROPE))], axis=-1)
    v_a = kv[..., MLA_NOPE:]
    scale_a = (MLA_NOPE + MLA_ROPE) ** -0.5
    scale_b = SB_DIM ** -0.5

    outs_a, outs_b = [], []
    for blk in range(seq // Q_BLOCK):
        t0 = blk * Q_BLOCK
        kend = t0 + Q_BLOCK
        t_pos = t0 + jnp.arange(Q_BLOCK)[:, None]
        s_pos = jnp.arange(kend)[None, :]
        s_a = jnp.einsum('bqhd,bkhd->bhqk', q_a[:, t0:kend], k_a[:, :kend]).astype(jnp.float32) * scale_a
        chunk_ok = (s_pos // CHUNK) <= (t_pos // CHUNK)
        p_a = jax.nn.softmax(jnp.where(chunk_ok, s_a, -jnp.inf), axis=-1)
        outs_a.append(jnp.einsum('bhqk,bkhd->bqhd', p_a.astype(v_a.dtype), v_a[:, :kend]))
        z = jnp.einsum('bqhd,bkhd->bhqk', q_b[:, t0:kend], k_b[:, :kend]).astype(jnp.float32) * scale_b
        before = s_pos < t_pos
        log_keep = jnp.where(before, jax.nn.log_sigmoid(-z), 0.0)
        log_between = lax.cumsum(log_keep, axis=3, reverse=True) - log_keep
        w_b = jnp.where(before, jnp.exp(jax.nn.log_sigmoid(z) + log_between), 0.0)
        outs_b.append(jnp.einsum('bhqk,bkhd->bqhd', w_b.astype(v_b.dtype), v_b[:, :kend]))

    o_a = jnp.concatenate(outs_a, axis=1).reshape(bsz, seq, MLA_HEADS * MLA_V)
    o_b = jnp.concatenate(outs_b, axis=1).reshape(bsz, seq, SB_HEADS * SB_DIM)
    return jnp.concatenate([o_a, o_b], axis=-1) @ w_out

def chunk_band_mixer(u, w_qkv, rel_bias, w_out):
    bsz, seq, _ = u.shape
    n_chunks = seq // CHUNK
    qkv = (u @ w_qkv).reshape(bsz, n_chunks, CHUNK, 3, C_HEADS, C_DIM)
    q, k, v = qkv[:, :, :, 0], qkv[:, :, :, 1], qkv[:, :, :, 2]
    pad = ((0, 0), (LEFT_CHUNKS, 0), (0, 0), (0, 0), (0, 0))
    k_p = jnp.pad(k, pad)
    v_p = jnp.pad(v, pad)
    scores = jnp.concatenate(
        [jnp.einsum('bnqhd,bnkhd->bnhqk', q, k_p[:, i:i + n_chunks]) for i in range(LEFT_CHUNKS + 1)],
        axis=-1).astype(jnp.float32) * (C_DIM ** -0.5)
    q_in = jnp.arange(CHUNK)[:, None]
    j = jnp.arange(BAND)[None, :]
    rel = (LEFT_CHUNKS - j // CHUNK) * CHUNK + q_in - j % CHUNK
    bias = rel_bias[:, jnp.clip(rel, -REL_CLIP, REL_CLIP) + REL_CLIP]
    valid = (jnp.arange(n_chunks)[:, None] - LEFT_CHUNKS + j // CHUNK) >= 0
    scores = scores + bias.astype(jnp.float32)[None, None]
    p = jax.nn.softmax(jnp.where(valid[None, :, None, None, :], scores, -jnp.inf), axis=-1).astype(v.dtype)
    parts = [jnp.einsum('bnhqk,bnkhd->bnqhd', p[..., i * CHUNK:(i + 1) * CHUNK], v_p[:, i:i + n_chunks])
             for i in range(LEFT_CHUNKS + 1)]
    o = functools.reduce(jnp.add, parts)
    return o.reshape(bsz, seq, MIX_ODD) @ w_out

def first_inputs(seed: int = 0) -> dict:
    key = jax.random.key(seed)
    ks = jax.random.split(key, 17)
    f32 = jnp.float32

    def nrm(k, shape, fan_in):
        return jax.random.normal(k, shape, f32) * (fan_in ** -0.5)

    def gain(k, shape):
        return 1.0 + 0.05 * jax.random.normal(k, shape, f32)

    return {
        "x": jax.random.normal(ks[0], (BATCH, SEQ, D_MODEL), f32),
        "ev_w_in": nrm(ks[1], (N_EVEN, D_MODEL, EVEN_IN), D_MODEL),
        "ev_g_cq": gain(ks[2], (N_EVEN, Q_LORA)),
        "ev_w_uq": nrm(ks[3], (N_EVEN, Q_LORA, MLA_HEADS * (MLA_NOPE + MLA_ROPE)), Q_LORA),
        "ev_g_ckv": gain(ks[4], (N_EVEN, KV_LORA)),
        "ev_w_ukv": nrm(ks[5], (N_EVEN, KV_LORA, MLA_HEADS * (MLA_NOPE + MLA_V)), KV_LORA),
        "ev_w_out": nrm(ks[6], (N_EVEN, MIX_EVEN, D_MODEL), MIX_EVEN),
        "od_w_qkv": nrm(ks[7], (N_ODD, D_MODEL, 3 * MIX_ODD), D_MODEL),
        "od_rel_bias": 0.1 * jax.random.normal(ks[8], (N_ODD, C_HEADS, 2 * REL_CLIP + 1), f32),
        "od_w_out": nrm(ks[9], (N_ODD, MIX_ODD, D_MODEL), MIX_ODD),
        "g_mix": gain(ks[10], (DEPTH, D_MODEL)),
        "g_ffn": gain(ks[11], (DEPTH, D_MODEL)),
        "w_gate": nrm(ks[12], (DEPTH, D_MODEL, D_FF), D_MODEL),
        "w_up": nrm(ks[13], (DEPTH, D_MODEL, D_FF), D_MODEL),
        "w_down": nrm(ks[14], (DEPTH, D_FF, D_MODEL), D_FF),
        "g_final": gain(ks[15], (D_MODEL,)),
    }

def first_block(x, ev_w_in, ev_g_cq, ev_w_uq, ev_g_ckv, ev_w_ukv, ev_w_out,
              od_w_qkv, od_rel_bias, od_w_out, g_mix, g_ffn, w_gate, w_up, w_down, g_final):
    h = x
    for layer in range(DEPTH):
        u = rms_norm(h, g_mix[layer])
        if layer % 2 == 0:
            i = layer // 2
            h = h + mla_stick_breaking_mixer(u, ev_w_in[i], ev_g_cq[i], ev_w_uq[i],
                                             ev_g_ckv[i], ev_w_ukv[i], ev_w_out[i])
        else:
            i = layer // 2
            h = h + chunk_band_mixer(u, od_w_qkv[i], od_rel_bias[i], od_w_out[i])
        u = rms_norm(h, g_ffn[layer])
        h = h + swiglu(u, w_gate[layer], w_up[layer], w_down[layer])
    return rms_norm(h, g_final)


N_META = 16
HEAD_DIM = 64
A_Q_HEADS = D_MODEL // HEAD_DIM
A_KV_HEADS = A_Q_HEADS // 4
IDX_HEADS = 8
IDX_DIM = 64
B_HEADS = D_MODEL // HEAD_DIM
D_FF_2 = 4 * D_MODEL
BLOCK = 128
TOPK_MAX = 256
EPS = 1e-6
N_A = DEPTH // 2
N_B = DEPTH - N_A

A_Q_W = A_Q_HEADS * HEAD_DIM
A_KV_W = A_KV_HEADS * HEAD_DIM
IDX_Q_W = IDX_HEADS * IDX_DIM
A_SPLITS = (A_Q_W, A_Q_W + A_KV_W, A_Q_W + 2 * A_KV_W,
            A_Q_W + 2 * A_KV_W + IDX_Q_W, A_Q_W + 2 * A_KV_W + IDX_Q_W + IDX_DIM)
A_IN_W = A_SPLITS[-1] + IDX_HEADS
B_W = B_HEADS * HEAD_DIM
KV_IN_W = 2 * B_W + B_HEADS


def rms_norm_2(x, g):
    xf = x.astype(jnp.float32)
    y = xf * lax.rsqrt(jnp.mean(xf * xf, axis=-1, keepdims=True) + EPS)
    return (y * g.astype(jnp.float32)).astype(x.dtype)

def rope_tables_2(T, dim):
    inv = 1.0 / (ROPE_THETA ** (jnp.arange(0, dim, 2, dtype=jnp.float32) / dim))
    ang = jnp.arange(T, dtype=jnp.float32)[:, None] * inv[None, :]
    return jnp.cos(ang), jnp.sin(ang)

def rope(x, cos, sin):
    x1, x2 = jnp.split(x, 2, axis=-1)
    c = cos[None, :, None, :]
    s = sin[None, :, None, :]
    return jnp.concatenate([x1 * c - x2 * s, x1 * s + x2 * c], axis=-1).astype(x.dtype)

def sq_relu_mlp(x, w1, w2):
    h = jax.nn.relu(x @ w1)
    return (h * h) @ w2

def dsa_attention(h, w_in, q_gain, k_gain, w_out, cos, sin, topk):
    B, T, _ = h.shape
    R = A_Q_HEADS // A_KV_HEADS
    nblk = T // BLOCK
    q, k, v, qi, ki, wi = jnp.split(h @ w_in, list(A_SPLITS), axis=-1)
    q = rope(rms_norm_2(q.reshape(B, T, A_Q_HEADS, HEAD_DIM), q_gain), cos, sin)
    k = rope(rms_norm_2(k.reshape(B, T, A_KV_HEADS, HEAD_DIM), k_gain), cos, sin)
    v = v.reshape(B, T, A_KV_HEADS, HEAD_DIM)
    qi = rope(qi.reshape(B, T, IDX_HEADS, IDX_DIM), cos, sin)
    ki = rope(ki[:, :, None, :], cos, sin)[:, :, 0, :]
    wi = wi.astype(jnp.float32) * (IDX_HEADS ** -0.5 * IDX_DIM ** -0.5)
    qb = q.reshape(B, nblk, BLOCK, A_KV_HEADS, R, HEAD_DIM)
    qib = qi.reshape(B, nblk, BLOCK, IDX_HEADS, IDX_DIM)
    wib = wi.reshape(B, nblk, BLOCK, IDX_HEADS)
    key_pos = jnp.arange(T)
    scale = HEAD_DIM ** -0.5

    def per_seq(args):
        qb_s, qib_s, wib_s, k_s, v_s, ki_s = args

        def per_block(bargs):
            blk, q_blk, qi_blk, w_blk = bargs
            qpos = blk * BLOCK + jnp.arange(BLOCK)
            causal = key_pos[None, :] <= qpos[:, None]
            logits = jnp.einsum('qhd,sd->qhs', qi_blk, ki_s,
                                preferred_element_type=jnp.float32)
            score = jnp.einsum('qh,qhs->qs', w_blk, jax.nn.relu(logits))
            score = jnp.where(causal, score, -jnp.inf)
            _, idx = lax.top_k(score, topk)
            valid = idx <= qpos[:, None]
            k_sel = k_s[idx]
            v_sel = v_s[idx]
            s = jnp.einsum('qgrd,qkgd->qgrk', q_blk, k_sel,
                           preferred_element_type=jnp.float32) * scale
            s = jnp.where(valid[:, None, None, :], s, -jnp.inf)
            p = jax.nn.softmax(s, axis=-1).astype(v_s.dtype)
            return jnp.einsum('qgrk,qkgd->qgrd', p, v_sel)

        return lax.map(per_block, (jnp.arange(nblk), qb_s, qib_s, wib_s))

    o = lax.map(per_seq, (qb, qib, wib, k, v, ki))
    return o.reshape(B, T, A_Q_W) @ w_out

def shared_kv(h, w_kv, f_bias, k_gain):
    B, T, _ = h.shape
    k, v, fl = jnp.split(h @ w_kv, [B_W, 2 * B_W], axis=-1)
    k = rms_norm_2(k.reshape(B, T, B_HEADS, HEAD_DIM), k_gain)
    v = v.reshape(B, T, B_HEADS, HEAD_DIM)
    log_f = jax.nn.log_sigmoid(fl.astype(jnp.float32) + f_bias.astype(jnp.float32))
    c = jnp.cumsum(log_f, axis=1).transpose(0, 2, 1)
    return k, v, c

def fox_attention(h, w_q, q_gain, w_out, k, v, c):
    B, T, _ = h.shape
    q = rms_norm_2((h @ w_q).reshape(B, T, B_HEADS, HEAD_DIM), q_gain)
    scale = HEAD_DIM ** -0.5
    outs = []
    for blk in range(T // BLOCK):
        q0, q1 = blk * BLOCK, (blk + 1) * BLOCK
        s = jnp.einsum('bqhd,bshd->bhqs', q[:, q0:q1], k[:, :q1],
                       preferred_element_type=jnp.float32) * scale
        decay = c[:, :, q0:q1, None] - c[:, :, None, :q1]
        causal = jnp.arange(q0, q1)[:, None] >= jnp.arange(q1)[None, :]
        s = jnp.where(causal, s + decay, -jnp.inf)
        p = jax.nn.softmax(s, axis=-1).astype(v.dtype)
        outs.append(jnp.einsum('bhqs,bshd->bqhd', p, v[:, :q1]))
    o = jnp.concatenate(outs, axis=1)
    return o.reshape(B, T, B_W) @ w_out

def second_inputs(seed: int = 0) -> dict:
    key = jax.random.key(seed)
    ks = jax.random.split(key, 18)

    def dense(k, shape, fan_in, scale=1.0):
        return jax.random.normal(k, shape, jnp.float32) * (scale * fan_in ** -0.5)

    def gain(k, shape):
        return 1.0 + 0.02 * jax.random.normal(k, shape, jnp.float32)

    kv_kv = dense(ks[11], (D_MODEL, 2 * B_W), D_MODEL)
    kv_f = dense(ks[17], (D_MODEL, B_HEADS), D_MODEL, 0.25)
    return {
        "x": jax.random.normal(ks[0], (BATCH, SEQ, D_MODEL), jnp.float32),
        "meta_tokens": jax.random.normal(ks[1], (N_META, D_MODEL), jnp.float32),
        "attn_norm": gain(ks[2], (DEPTH, D_MODEL)),
        "mlp_norm": gain(ks[3], (DEPTH, D_MODEL)),
        "mlp_w1": dense(ks[4], (DEPTH, D_MODEL, D_FF_2), D_MODEL),
        "mlp_w2": dense(ks[5], (DEPTH, D_FF_2, D_MODEL), D_FF_2),
        "a_w_in": dense(ks[6], (N_A, D_MODEL, A_IN_W), D_MODEL),
        "a_q_gain": gain(ks[7], (N_A, HEAD_DIM)),
        "a_k_gain": gain(ks[8], (N_A, HEAD_DIM)),
        "a_w_out": dense(ks[9], (N_A, A_Q_W, D_MODEL), A_Q_W),
        "kv_norm": gain(ks[10], (D_MODEL,)),
        "kv_w": jnp.concatenate([kv_kv, kv_f], axis=1),
        "kv_f_bias": jax.random.uniform(ks[12], (B_HEADS,), jnp.float32, 1.0, 4.0),
        "kv_k_gain": gain(ks[13], (HEAD_DIM,)),
        "b_w_q": dense(ks[14], (N_B, D_MODEL, B_W), D_MODEL),
        "b_q_gain": gain(ks[15], (N_B, HEAD_DIM)),
        "b_w_out": dense(ks[16], (N_B, B_W, D_MODEL), B_W),
    }

def second_block(x, meta_tokens, attn_norm, mlp_norm, mlp_w1, mlp_w2,
              a_w_in, a_q_gain, a_k_gain, a_w_out,
              kv_norm, kv_w, kv_f_bias, kv_k_gain,
              b_w_q, b_q_gain, b_w_out):
    B, S, D = x.shape
    T = S + N_META
    Tp = -(-T // BLOCK) * BLOCK
    meta = jnp.broadcast_to(meta_tokens.astype(x.dtype)[None], (B, N_META, D))
    h = jnp.concatenate([meta, x], axis=1)
    h = jnp.pad(h, ((0, 0), (0, Tp - T), (0, 0)))
    cos, sin = rope_tables_2(Tp, HEAD_DIM)
    topk = min(TOPK_MAX, S // 4)
    shared = None
    for i in range(DEPTH):
        hn = rms_norm_2(h, attn_norm[i])
        if i < N_A:
            h = h + dsa_attention(hn, a_w_in[i], a_q_gain[i], a_k_gain[i], a_w_out[i],
                                  cos, sin, topk)
        else:
            if i == N_A:
                shared = shared_kv(rms_norm_2(h, kv_norm), kv_w, kv_f_bias, kv_k_gain)
            j = i - N_A
            h = h + fox_attention(hn, b_w_q[j], b_q_gain[j], b_w_out[j],
                                  shared[0], shared[1], shared[2])
        h = h + sq_relu_mlp(rms_norm_2(h, mlp_norm[i]), mlp_w1[i], mlp_w2[i])
    return h[:, N_META:N_META + S]


def setup_inputs(seed=0):
    out = dict(first_inputs(seed))
    for name, value in second_inputs(seed + 1).items():
        if name != "x":
            out[name + "_2"] = value
    return out


def reference(
    x, ev_w_in, ev_g_cq, ev_w_uq, ev_g_ckv, ev_w_ukv, ev_w_out, od_w_qkv, od_rel_bias, od_w_out,
    g_mix, g_ffn, w_gate, w_up, w_down, g_final, meta_tokens_2, attn_norm_2, mlp_norm_2,
    mlp_w1_2, mlp_w2_2, a_w_in_2, a_q_gain_2, a_k_gain_2, a_w_out_2, kv_norm_2, kv_w_2,
    kv_f_bias_2, kv_k_gain_2, b_w_q_2, b_q_gain_2, b_w_out_2,
):
    x = first_block(
        x, ev_w_in, ev_g_cq, ev_w_uq, ev_g_ckv, ev_w_ukv, ev_w_out, od_w_qkv, od_rel_bias,
        od_w_out, g_mix, g_ffn, w_gate, w_up, w_down, g_final,
    )
    return second_block(
        x, meta_tokens_2, attn_norm_2, mlp_norm_2, mlp_w1_2, mlp_w2_2, a_w_in_2, a_q_gain_2,
        a_k_gain_2, a_w_out_2, kv_norm_2, kv_w_2, kv_f_bias_2, kv_k_gain_2, b_w_q_2, b_q_gain_2,
        b_w_out_2,
    )


_drawn_inputs = setup_inputs


def setup_inputs(seed=0):
    import zlib

    import numpy as np

    out = dict(_drawn_inputs(seed))
    spreads = {}
    factors = {'ev_g_cq': 3.222,
     'ev_g_ckv': 2.731,
     'a_q_gain_2': 8.0,
     'a_k_gain_2': 8.0,
     'kv_norm_2': 8.0,
     'kv_k_gain_2': 8.0,
     'b_q_gain_2': 8.0}
    for name, (base, spread) in spreads.items():
        noise = np.random.default_rng([zlib.crc32(name.encode()), seed]).standard_normal(out[name].shape)
        drawn = base * np.exp(spread * noise) if base else spread * noise
        out[name] = __import__('jax').numpy.asarray(drawn.astype(out[name].dtype))
    for name, factor in factors.items():
        out[name] = (out[name] * factor).astype(out[name].dtype)
    return out
```

```python
from contextlib import ExitStack

import concourse.bass as bass
import numpy as np
from concourse import mybir

ALU = mybir.AluOpType
ACT = mybir.ActivationFunctionType
AX = mybir.AxisListType
F32 = mybir.dt.float32
F32R = mybir.dt.float32r
BF16 = mybir.dt.bfloat16

P = 128
D = 1024
DC = D // P
META = 16
SEQ = 256
T = META + SEQ
QL, KVL = 384, 256
QC, KVC = QL // P, KVL // P
ROPE = 32
NOPE = 64
HD = 64
FF1 = 2816
FC1 = FF1 // P
FF2 = 4096
FC2 = FF2 // P
TOPK = 64
EPS = 1e-6
NEG = -1e30
TAKEN = -3e38
RING = 4
AHEAD = RING - 1
UNIT = DC * P

PHASES = [
    ("cq", 3), ("ckv", 2), ("kr", 1), ("sv", 4), ("sq", 4), ("sk", 4), ("mla", 8), ("out0", 8),
    ("gu0", 44), ("dn0", 24),
    ("bv", 8), ("bq", 8), ("bk", 8), ("out1", 8), ("gu1", 44), ("dn1", 24),
    ("ki", 1), ("wi", 1), ("qi", 4), ("dk", 4), ("dv", 2), ("dq", 8), ("out2", 8), ("up2", 32), ("dn2", 32),
    ("ff", 1), ("fv", 8), ("fk", 8), ("fq", 8), ("out3", 8), ("up3", 32), ("dn3", 32),
    ("end", AHEAD),
]
START = {}
_n = 0
for _name, _k in PHASES:
    START[_name] = _n
    _n += _k
UNITS = _n

BSTART = {}
_n = 0
for _name, _k in PHASES:
    BSTART[_name] = _n
    _n += {"dn": 8, "ml": 16, "en": 0}.get(_name[:2], _k)

GAINS = ["mix0", "ffn0", "mix1", "ffn1", "final", "attn0", "mlp0", "kvn", "attn1", "mlp1"]
GCOL = {name: DC * i for i, name in enumerate(GAINS)}
GCOL.update(cq=80, ckv=83, aq=85, ak=86, kk=87, bq=88, fb=89)
NG = 90

CONSTS = [("ident", 128), ("rev", 128), ("ones", 128), ("headones", 128), ("laterneg", 128), ("allneg", 128),
          ("rot", 128), ("rotm", 128), ("before", 128), ("causal", 128), ("cos", T), ("sin", T),
          ("cosm", SEQ), ("sinm", SEQ), ("upper", 128), ("late", 64), ("rep", 128)]
CCOL = {}
_n = 0
for _name, _k in CONSTS:
    CCOL[_name] = (_n, _n + _k)
    _n += _k
NCONST = _n


class At:

    def __init__(self, c, it=None, m=0):
        self.c, self.it, self.m = c, it, m

    def __add__(self, k):
        return At(self.c + k, self.it, self.m)

    def times(self, k):
        return At(self.c * k, self.it, self.m * k)

    def mod(self, k):
        assert self.m % k == 0
        return self.c % k

    def div(self, k):
        assert self.m % k == 0
        return At(self.c // k, self.it, self.m // k)

    def value(self):
        assert self.c > 0
        return self.c if self.it is None else self.it * self.m + self.c


class Chain:

    def __init__(self, sem):
        self.sem, self.done, self.it, self.per, self.here = sem, 0, None, 0, 0

    def enter(self, it, per):
        self.it, self.per, self.here = it, per, 0

    def leave(self, trips):
        assert self.here == self.per, (self.here, self.per)
        self.done += self.per * trips
        self.it, self.per, self.here = None, 0, 0

    def next(self):
        if self.it is None:
            self.done += 1
            return self.done
        self.here += 1
        return At(self.done + self.here, self.it, self.per).value()


def program(nc, stream, xT, metaT, gains, consts, relh, sel, out):
    with ExitStack() as ctx:
        def sb(name, cols, dt=F32):
            return ctx.enter_context(nc.sbuf_tensor(name, [P, cols], dt))

        def sem(name):
            return ctx.enter_context(nc.semaphore(name))

        def sems(names):
            return [sem(name) for name in names.split()]

        raw = sb("raw", RING * UNIT)[:, :].rearrange("p (s n) -> p s n", s=RING)
        whi = sb("whi", RING * UNIT, F32R)[:, :].rearrange("p (s n) -> p s n", s=RING)
        wlo = sb("wlo", RING * UNIT, F32R)[:, :].rearrange("p (s n) -> p s n", s=RING)
        uhi = sb("uhi", DC * T, F32R)[:, :].rearrange("p (c t) -> p c t", t=T)
        ulo = sb("ulo", DC * T, F32R)[:, :].rearrange("p (c t) -> p c t", t=T)
        ahi_t = sb("ahi", FC2 * T, F32R)
        alo_t = sb("alo", FC2 * T, F32R)
        ahi = ahi_t[:, :].rearrange("p (c t) -> p c t", t=T)
        alo = alo_t[:, :].rearrange("p (c t) -> p c t", t=T)
        h = sb("h", DC * T)[:, :].rearrange("p (c t) -> p c t", t=T)
        g_t = sb("gain_columns", NG)
        c_t = sb("constants", NCONST)
        rstd = sb("rstd", 3 * T)[:, :].rearrange("p (c t) -> p c t", t=T)
        lg = sb("log_mean", T)
        acc = sb("sum_of_squares", T)
        bias = sb("bias_columns", 2)
        gains8 = sb("gains_over_8", 2)
        identb = sb("identb", 128, BF16)
        causalb = sb("causalb", 128, BF16)
        rowsb = sb("rowsb", 128 + 64 + 128, BF16)
        selmask = sb("selmask", 128 + 256 + T, BF16)
        wi = sb("wi", 3 * 8)
        SCR = 12208
        scr = sb("scratch", SCR)
        upperb, lateb, repb = rowsb[0:1, 0:128], rowsb[0:1, 128:192], rowsb[0:16, 192:320]

        def area(at, cols):
            assert at + cols <= SCR, (at, cols)
            return scr[:, at:at + cols]

        Q0, K0, V0 = 0, DC * T, 2 * DC * T
        q_all = area(Q0, DC * T).rearrange("p (c t) -> p c t", t=T)
        k_all = area(K0, DC * T).rearrange("p (c t) -> p c t", t=T)
        sq_all = q_all
        S0 = V0 + 3 * D
        prob = area(S0, 832).rearrange("p (b n) -> p b n", b=2)
        probT = area(S0 + 832, 768).rearrange("p (b n) -> p b n", b=2)
        probTA = area(S0 + 1600, 512).rearrange("p (b n) -> p b n", b=2)
        small = area(S0 + 2112, 64)
        yb = area(S0, 4 * T).rearrange("p (b t) -> p b t", b=4)
        y2 = area(S0 + 4 * T, 2 * T).rearrange("p (b t) -> p b t", b=2)
        ysq = area(S0 + 6 * T, 2 * T).rearrange("p (b t) -> p b t", b=2)
        E0 = S0 + 8 * T
        hr = area(E0 + 1760, 2 * T).rearrange("p (b t) -> p b t", b=2)
        relb = area(E0, 1024).rearrange("p (s b n) -> p s b n", s=2, b=2)
        selb = area(E0, 1024).bitcast(BF16).rearrange("p (h n) -> p h n", n=128)
        csplit = area(E0 + 1024, T // 2).bitcast(BF16)
        score = [area(E0, 128), area(E0 + 128, 256), area(E0 + 384, T)]
        best = area(E0 + 384 + T, 8)
        relu_t = area(E0 + 664, 2 * T).rearrange("p (b t) -> p b t", b=2)
        mc = area(E0 + 664 + 2 * T, 2 * T).rearrange("p (b t) -> p b t", b=2)
        relu = area(K0 + 4 * T, 768).rearrange("p (b n) -> p b n", b=2)
        gate, egate, tgate, mval = (
            area(K0 + 2 * T * i, 2 * T).rearrange("p (b t) -> p b t", b=2) for i in range(4))
        mq = area(8 * T, 8 * SEQ).rearrange("p (c t) -> p c t", t=SEQ)
        mk = area(8 * T + 8 * SEQ, 8 * SEQ).rearrange("p (c t) -> p c t", t=SEQ)
        sbq, sbk = q_all[:, 0:4, :], q_all[:, 4:8, :]
        L0 = 8 * T + 16 * SEQ
        zlog, nlk, ls = (area(L0 + 2048 + 768 * i, 768).rearrange("p (b n) -> p b n", b=2) for i in range(3))
        kro = area(L0 + 2048 + 2304, T)
        mprob = area(L0 + 2048 + 2304, 768).rearrange("p (b n) -> p b n", b=2)
        mprobT = area(L0 + 2048 + 2304 + 768, 768).rearrange("p (b n) -> p b n", b=2)
        msmall = area(L0 + 2048 + 2304 + 1536, 16)
        lyb = area(L0 + 2048, 4 * T).rearrange("p (b t) -> p b t", b=4)
        lat = area(8 * T, 5 * T).rearrange("p (b t) -> p b t", b=5)
        latsq = area(8 * T + 5 * T, 5 * T).rearrange("p (b t) -> p b t", b=5)

        def const(name):
            a, b = CCOL[name]
            return c_t[:, a:b]

        def gain(name, m=0):
            return g_t[:, GCOL[name] + m:GCOL[name] + m + 1]

        def chunk_at(first, at, cols):
            w = cols.stop - cols.start
            if at.it is None:
                return scr[:, first + at.c * T + cols.start:first + at.c * T + cols.stop]
            return scr[:, bass.ds(at.it * (at.m * T) + (first + at.c * T + cols.start), w)]

        def hidden_at(t, at, cols):
            w = cols.stop - cols.start
            if at.it is None:
                return t[:, at.c * T + cols.start:at.c * T + cols.stop]
            return t[:, bass.ds(at.it * (at.m * T) + (at.c * T + cols.start), w)]

        bank = [ctx.enter_context(nc.psum_tensor(f"bank{i}", [P, 512], F32)) for i in range(8)]
        STAT = 4

        loaded, consts_cast, bias_set, stored = sems("inputs_loaded consts_cast bias_set stored")
        w_loaded = sems("w_loaded0 w_loaded1 w_loaded2 w_loaded3")
        w_hi, w_lo, w_used, evac = sems("w_hi w_lo w_used evacuated")
        u_hi, u_lo, squares, acc_done, stat_ready, rstd_ready = sems(
            "u_hi u_lo squares acc_done stat_ready rstd_ready")
        x2_ready, u2_hi, u2_lo = sems("x2_ready u2_hi u2_lo")
        e_ready, t_ready, a_hi, a_lo, a_sq = sems("e_ready t_ready a_hi a_lo a_sq")
        v_turned, v_stored = sems("v_turned v_stored")
        y_sq, y_stat, y_rstd, y_norm, y_rot, y_cos, y_done = sems(
            "y_sq y_stat y_rstd y_norm y_rot y_cos y_done")
        s_ready, s_max, p_exp, p_norm, pt_ready, pt_copied, o_ready, o_hi, o_lo = sems(
            "s_ready s_max p_exp p_norm pt_ready pt_copied o_ready o_hi o_lo")
        z_ready, z_log, z_split, z_masked, z_sum, z_arg, z_exp, z_w, z_o, z_ohi, z_olo = sems(
            "z_ready z_log z_split z_masked z_sum z_arg z_exp z_w z_o z_ohi z_olo")
        sel_loaded = sem("sel_loaded")
        rel_loaded = sems("rel_loaded0 rel_loaded1")
        lat_hi, lat_lo, lat_sq, lat_stat, lat_rstd, kr_rot, kr_done = sems(
            "lat_hi lat_lo lat_sq lat_stat lat_rstd kr_rot kr_done")
        m_q, m_rot, m_qdone, m_kv, m_turned, m_vstored, m_kdone = sems(
            "m_q m_rot m_qdone m_kv m_turned m_vstored m_kdone")
        wi_ready, wi_turned, wi_done, ix_ready, ix_relu, ix_acc, ix_mask = sems(
            "wi_ready wi_turned wi_done ix_ready ix_relu ix_acc ix_mask")
        f_exp, f_log, f_split = sems("f_exp f_log f_split")
        t_q, t_s, t_max, t_exp, t_p, t_pt, t_pts, t_o, t_ohi, t_olo = sems(
            "t_q t_s t_max t_exp t_p t_pt t_pts t_o t_ohi t_olo")
        out_turned, out_copied = sems("out_turned out_copied")
        dve_chain, act_chain = sems("dve_chain act_chain")

        FIRST, WHOLE = slice(META, T), slice(0, T)
        UIDX = {0: 0, 1: 1, 2: 2, 3: 3, 5: 4, 6: 5, 7: 6, 8: 7}

        def width(cols):
            return cols.stop - cols.start

        def split_hi(act, n):
            s = n.mod(RING)
            act.wait_ge(w_loaded[s], (n.div(RING) + 1).times(16).value())
            if (n + (1 - RING)).c > 0:
                act.wait_ge(w_used, (n + (1 - RING)).value())
            act.activation(whi[:, s, :], raw[:, s, :], ACT.Copy).then_inc(w_hi, 1)

        def split_lo(dve, n):
            s = n.mod(RING)
            dve.wait_ge(w_hi, (n + 1).value())
            dve.tensor_tensor(wlo[:, s, :], raw[:, s, :], whi[:, s, :].bitcast(F32),
                              ALU.subtract).then_inc(w_lo, 1)

        def unit_mm(pe, n, dst, xhi, xlo, cols, chunks=DC, at=0, first=True, last=True, x=None, used=True):
            s = n.mod(RING)
            pe.wait_ge(w_lo, (n + 1).value())
            for i in range(chunks):
                if x is not None:
                    ready, count = x(i)
                    pe.wait_ge(ready, count)
                hi, lo = (w[:, s, (at + i) * P:(at + i + 1) * P] for w in (whi, wlo))
                a, b = xhi[:, i, cols], xlo[:, i, cols]
                pe.matmul(dst, hi, a, start=first and i == 0, stop=False)
                pe.matmul(dst, hi, b, start=False, stop=False)
                mm = pe.matmul(dst, lo, a, start=False, stop=last and i == chunks - 1)
            if used:
                mm.then_inc(w_used, 1)

        def u_chunk(norm):
            return lambda i: (u_lo, 8 * UIDX[norm] + i + 1)

        def norm_act(act, k, m, cols, name):
            if name != "final":
                act.activation(uhi[:, m, cols], h[:, m, cols], ACT.Copy, scale=gain(name, m)).then_inc(u_hi, 1)
            if m == 0:
                if 7 * k > 0:
                    act.wait_ge(acc_done, 7 * k)
            act.activation(sq_all[:, m, cols], h[:, m, cols], ACT.Square).then_inc(squares, 1)

        def norm_dve(dve, k, m, cols, name):
            if name == "final":
                return
            dve.wait_ge(u_hi, 8 * UIDX[k] + m + 1)
            dve.scalar_tensor_tensor(out=ulo[:, m, cols], in0=h[:, m, cols], scalar=gain(name, m),
                                     in1=uhi[:, m, cols].bitcast(F32), op0=ALU.mult,
                                     op1=ALU.subtract).then_inc(u_lo, 1)

        def norm_pool(pool, k, cols):
            for m in range(1, DC):
                pool.wait_ge(squares, 8 * k + m + 1)
                if m == 1:
                    if k > 0:
                        pool.wait_ge(stat_ready, k)
                else:
                    pool.wait_ge(acc_done, 7 * k + m - 1)
                first = sq_all[:, 0, cols] if m == 1 else acc[:, cols]
                pool.tensor_tensor(acc[:, cols], first, sq_all[:, m, cols], ALU.add).then_inc(acc_done, 1)

        def norm_pe(pe, k, cols):
            pe.wait_ge(acc_done, 7 * (k + 1))
            if k > 0:
                pe.wait_ge(rstd_ready, k)
            pe.matmul(bank[STAT][:, 0:width(cols)], const("ones"), acc[:, cols], start=True,
                      stop=True).then_inc(stat_ready, 1)

        def norm_rstd(act, link, k, cols):
            act.wait_ge(stat_ready, k + 1)
            if k > 0:
                act.wait_ge(rstd_ready, k)
            act.activation(lg[:, cols], bank[STAT][:, 0:width(cols)], ACT.Ln, scale=1.0 / D, bias=bias[:, 0:1]).then_inc(link.sem, 1)
            act.wait_ge(link.sem, link.next())
            act.activation(rstd[:, 0, cols], lg[:, cols], ACT.Exp, scale=-0.5).then_inc(rstd_ready, 1)

        def resid_pe(pe, name, kc, cols, x):
            per = -(-kc // DC)

            def group(it):
                n0, b0 = At(START[name], it, 4 * per), At(BSTART[name], it, 4)
                for j in range(4):
                    pe.wait_ge(evac, (b0 + (j - 3)).value())
                    dst = bank[(b0 + j).mod(4)][:, 0:width(cols)]
                    for u in range(per):
                        wait_x = it is None and j == 0
                        unit_mm(pe, n0 + (j * per + u), dst, ahi[:, u * DC:, :], alo[:, u * DC:, :], cols,
                                chunks=min(DC, kc - u * DC), first=u == 0, last=u == per - 1,
                                x=(lambda i, u=u: x(u * DC + i)) if wait_x else None)
            group(None)
            with pe.Fori(1, DC // 4) as it:
                group(it)

        def resid_act(act, link, name, kc, cols, norm, gname):
            per = -(-kc // DC)
            for m in range(DC + 1):
                for u in range(per if m < DC else 1):
                    if m < DC:
                        split_hi(act, At(START[name] + m * per + u + AHEAD))
                    if u == 0 and m > 0 and gname is not None:
                        act.wait_ge(evac, BSTART[name] + m)
                        norm_act(act, norm, m - 1, cols, gname)
            if norm is not None:
                norm_rstd(act, link, norm, cols)

        def resid_dve(dve, name, kc, cols, norm, gname):
            per = -(-kc // DC)
            for m in range(DC):
                for u in range(per):
                    split_lo(dve, At(START[name] + m * per + u + AHEAD))
                    if m > 0 and u == 0 and gname is not None:
                        norm_dve(dve, norm, m - 1, cols, gname)
                b = BSTART[name] + m
                dve.wait_ge(w_used, START[name] + (m + 1) * per)
                dve.tensor_tensor(h[:, m, cols], bank[b % 4][:, 0:width(cols)], h[:, m, cols],
                                  ALU.add).then_inc(evac, 1)
            if gname is not None:
                norm_dve(dve, norm, DC - 1, cols, gname)

        def hidden_pe(pe, name, cols, norm, groups):
            def group(it):
                n0, b0 = At(START[name], it, 4), At(BSTART[name], it, 4)
                for j in range(4):
                    pe.wait_ge(evac, (b0 + (j - 3)).value())
                    unit_mm(pe, n0 + j, bank[(b0 + j).mod(4)][:, 0:width(cols)], uhi, ulo, cols,
                            x=u_chunk(norm) if it is None and j == 0 else None)
                    if it is None and j == 0:
                        norm_pe(pe, norm, cols)
            group(None)
            with pe.Fori(1, groups) as it:
                group(it)

        def swiglu_pe(pe, name, cols, norm):
            hidden_pe(pe, name, cols, norm, FC1 // 2)

        def swiglu_act(act, link, name, cols):
            with act.Fori(0, FC1 // 2) as it:
                link.enter(it, 4)
                n0, b0 = At(START[name], it, 4), At(BSTART[name], it, 4)
                for j in range(2):
                    split_hi(act, n0 + (2 * j + AHEAD))
                    act.wait_ge(evac, (b0 + (2 * j + 1)).value())
                    e = egate[:, j, cols]
                    act.activation(e, gate[:, j, cols], ACT.Exp, scale=-1.0).then_inc(link.sem, 1)
                    act.wait_ge(link.sem, link.next())
                    act.activation(e, e, ACT.Ln, bias=bias[:, 1:2]).then_inc(link.sem, 1)
                    act.wait_ge(link.sem, link.next())
                    act.activation(e, e, ACT.Exp, scale=-1.0).then_inc(e_ready, 1)
                    split_hi(act, n0 + (2 * j + 1 + AHEAD))
                    act.wait_ge(evac, (b0 + (2 * j + 2)).value())
                    act.activation(hidden_at(ahi_t, At(j, it, 2), cols), mval[:, j, cols], ACT.Copy).then_inc(a_hi, 1)
                link.leave(FC1 // 2)

        def swiglu_dve(dve, name, cols, norm, i0):
            dve.wait_ge(rstd_ready, norm + 1)
            with dve.Fori(0, FC1 // 2) as it:
                n0, b0 = At(START[name], it, 4), At(BSTART[name], it, 4)
                for j in range(2):
                    i = At(i0 + j, it, 2)
                    dve.wait_ge(w_used, (n0 + (2 * j + 1)).value())
                    dve.tensor_tensor(gate[:, j, cols], bank[(b0 + 2 * j).mod(4)][:, 0:width(cols)],
                                      rstd[:, 0, cols], ALU.mult).then_inc(evac, 1)
                    split_lo(dve, n0 + (2 * j + AHEAD))
                    split_lo(dve, n0 + (2 * j + 1 + AHEAD))
                    dve.wait_ge(w_used, (n0 + (2 * j + 2)).value())
                    dve.wait_ge(t_ready, (i + 1).times(2).value())
                    dve.tensor_tensor(mval[:, j, cols], bank[(b0 + 2 * j + 1).mod(4)][:, 0:width(cols)],
                                      tgate[:, j, cols], ALU.mult).then_inc(evac, 1)

        def swiglu_pool(pool, name, cols, norm, i0):
            pool.wait_ge(rstd_ready, norm + 1)
            with pool.Fori(0, FC1 // 2) as it:
                for j in range(2):
                    i = At(i0 + j, it, 2)
                    pool.wait_ge(e_ready, (i + 1).value())
                    pool.tensor_tensor(tgate[:, j, cols], gate[:, j, cols], egate[:, j, cols], ALU.mult).then_inc(t_ready, 1)
                    pool.wait_ge(t_ready, (i.times(2) + 1).value())
                    pool.tensor_tensor(tgate[:, j, cols], tgate[:, j, cols], rstd[:, 0, cols], ALU.mult).then_inc(t_ready, 1)
                    pool.wait_ge(a_hi, (i + 1).value())
                    pool.tensor_tensor(hidden_at(alo_t, At(j, it, 2), cols), mval[:, j, cols],
                                       hidden_at(ahi_t, At(j, it, 2), cols).bitcast(F32), ALU.subtract).then_inc(a_lo, 1)

        def sqrelu_pe(pe, name, cols, norm):
            hidden_pe(pe, name, cols, norm, FC2 // 4)

        def sqrelu_act(act, name, cols):
            with act.Fori(0, FC2 // 4) as it:
                n0, b0 = At(START[name], it, 4), At(BSTART[name], it, 4)
                for j in range(4):
                    split_hi(act, n0 + (j + AHEAD))
                    act.wait_ge(evac, (b0 + (j + 1)).value())
                    act.activation(hidden_at(ahi_t, At(j, it, 4), cols), gate[:, j % 2, cols], ACT.Square).then_inc(a_hi, 1)

        def sqrelu_dve(dve, name, cols, norm, i0):
            dve.wait_ge(rstd_ready, norm + 1)
            with dve.Fori(0, FC2 // 4) as it:
                n0, b0 = At(START[name], it, 4), At(BSTART[name], it, 4)
                for j in range(4):
                    i = At(i0 + j, it, 4)
                    dve.wait_ge(w_used, (n0 + (j + 1)).value())
                    dve.wait_ge(a_lo, (i + (-1)).value())
                    dve.scalar_tensor_tensor(out=gate[:, j % 2, cols], in0=bank[(b0 + j).mod(4)][:, 0:width(cols)],
                                             scalar=0.0, in1=rstd[:, 0, cols], op0=ALU.max,
                                             op1=ALU.mult).then_inc(evac, 1)
                    split_lo(dve, n0 + (j + AHEAD))

        def sqrelu_pool(pool, name, cols, i0, k0):
            with pool.Fori(0, FC2 // 4) as it:
                b0 = At(BSTART[name], it, 4)
                for j in range(4):
                    i, k = At(i0 + j, it, 4), At(k0 + j, it, 4)
                    pool.wait_ge(evac, (b0 + (j + 1)).value())
                    pool.tensor_tensor(mval[:, j % 2, cols], gate[:, j % 2, cols], gate[:, j % 2, cols],
                                       ALU.mult).then_inc(a_sq, 1)
                    pool.wait_ge(a_sq, (k + 1).value())
                    pool.wait_ge(a_hi, (i + 1).value())
                    pool.tensor_tensor(hidden_at(alo_t, At(j, it, 4), cols), mval[:, j % 2, cols],
                                       hidden_at(ahi_t, At(j, it, 4), cols).bitcast(F32), ALU.subtract).then_inc(a_lo, 1)


        VFIRST = {"sv": 0, "bv": 4, "dv": 12, "fv": 14}
        RFIRST = {"dk": 0, "dq": 4, "fk": 12, "fq": 20}
        OFIRST = {"ki": 0, "qi": 1, "dk": 5, "dq": 9, "fk": 17, "fq": 25}
        VTILES = {"sv": (META, META + 128, None), "bv": (META, META + 128, None), "dv": (0, 128, 256), "fv": (META, META + 128, 0)}
        COUNT = dict(PHASES)

        def in_groups(eng, name, body, peel=False):
            n = COUNT[name]
            if n <= 4:
                body(At(0), n, None, 1)
            else:
                if peel:
                    body(At(0), 4, None, 1)
                with eng.Fori(1 if peel else 0, n // 4) as it:
                    body(At(0, it, 4), 4, it, n // 4)

        def proj_pe(pe, name, kind, cols, norm, second=False, sum_norm=None):
            xhi, xlo = (ahi[:, DC:, :], alo[:, DC:, :]) if second else (uhi, ulo)
            ready = (lambda i: (u2_lo, i + 1)) if second else u_chunk(norm)
            vy = lyb if name == "sv" else yb
            n_cols = width(cols)

            def body(g, k, it, trips):
                def turn(j):
                    v = g + (VFIRST[name] + j)
                    pe.wait_ge(evac, (g + (BSTART[name] + j + 1)).value())
                    if (v + (-1)).c > 0:
                        pe.wait_ge(v_stored, (v + (-1)).value())
                    t0, t1, ta = VTILES[name]
                    dst = bank[5 + j % 2]
                    if ta is not None:
                        pe.transpose(dst[0:META, 256:384], vy[:, j, ta:ta + META], const("ident"))
                    pe.transpose(dst[:, 0:128], vy[:, j, t0:t0 + 128], const("ident"))
                    pe.transpose(dst[:, 128:256], vy[:, j, t1:t1 + 128], const("ident")).then_inc(v_turned, 1)

                def stat(j):
                    r = g + (RFIRST[name] + j)
                    pe.wait_ge(y_sq, (r + 1).value())
                    if (r + (-1)).c > 0:
                        pe.wait_ge(y_rstd, (r + (-1)).value())
                    pe.matmul(bank[5 + j % 2][:, 0:n_cols], const("headones"), ysq[:, j % 2, cols],
                              start=True, stop=True).then_inc(y_stat, 1)

                def rot(j):
                    o = g + (OFIRST[name] + j)
                    if kind == "rope":
                        pe.wait_ge(evac, (g + (BSTART[name] + j + 1)).value())
                    else:
                        pe.wait_ge(y_norm, (g + (RFIRST[name] + j + 1)).value())
                    if o.c > 0:
                        pe.wait_ge(y_done, o.value())
                    src = yb[:, (OFIRST[name] + j) % 4, cols] if kind == "rope" else y2[:, j % 2, cols]
                    pe.matmul(bank[7][:, 0:n_cols], const("rot"), src, start=True, stop=True).then_inc(y_rot, 1)

                for j in range(k):
                    b = g + (BSTART[name] + j)
                    pe.wait_ge(evac, (b + (-3)).value())
                    unit_mm(pe, g + (START[name] + j), bank[b.mod(4)][:, 0:n_cols], xhi, xlo, cols,
                            x=ready if j == 0 else None)
                    if sum_norm is not None and it is None and j == 0:
                        norm_pe(pe, sum_norm, cols)
                    if kind == "v" and j >= 1:
                        turn(j - 1)
                    if "rms" in kind and j >= 1:
                        stat(j - 1)
                    if "rope" in kind and j >= 2:
                        rot(j - 2)
                if kind == "v":
                    turn(k - 1)
                if "rms" in kind:
                    stat(k - 1)
                if "rope" in kind:
                    for j in range(max(0, k - 2), k):
                        rot(j)
            in_groups(pe, name, body, peel=sum_norm is not None)

        def proj_act(act, link, name, kind, cols):
            n_cols = width(cols)

            def body(g, k, it, trips):
                if it is not None:
                    link.enter(it, k if "rms" in kind or name == "fv" else 0)

                def rms(j):
                    act.wait_ge(y_stat, (g + (RFIRST[name] + j + 1)).value())
                    if kind == "rms":
                        act.wait_ge(y_done, (g + (OFIRST[name] + j - 1)).value())
                    else:
                        if (g + (RFIRST[name] + j - 1)).c > 0:
                            act.wait_ge(y_norm, (g + (RFIRST[name] + j - 1)).value())
                    if (g + (RFIRST[name] + j)).c > 0:
                        act.wait_ge(y_rstd, (g + (RFIRST[name] + j)).value())
                    act.activation(lg[:, cols], bank[5 + j % 2][:, 0:n_cols], ACT.Ln, scale=1.0 / HD, bias=bias[:, 0:1]).then_inc(link.sem, 1)
                    act.wait_ge(link.sem, link.next())
                    act.activation(hr[:, j % 2, cols], lg[:, cols], ACT.Exp, scale=-0.5).then_inc(y_rstd, 1)

                def store_v(j):
                    act.wait_ge(v_turned, (g + (VFIRST[name] + j + 1)).value())
                    if VTILES[name][2] is not None:
                        act.activation(v_cols(g + j, 256, 128, META), bank[5 + j % 2][0:META, 256:384], ACT.Copy).then_inc(link.sem, 1)
                        act.wait_ge(link.sem, link.next())
                    dst = v_cols(g + j, 0, 256, P) if name != "sv" else mv_cols(g + j)
                    act.activation(dst, bank[5 + j % 2][:, 0:256], ACT.Copy).then_inc(v_stored, 1)

                for j in range(k):
                    split_hi(act, g + (START[name] + j + AHEAD))
                    if "rms" in kind:
                        act.wait_ge(evac, (g + (BSTART[name] + j + 1)).value())
                        if (g + (RFIRST[name] + j - 1)).c > 0:
                            act.wait_ge(y_stat, (g + (RFIRST[name] + j - 1)).value())
                        act.activation(ysq[:, j % 2, cols], yb[:, j, cols], ACT.Square).then_inc(y_sq, 1)
                        if j >= 1:
                            rms(j - 1)
                    if kind == "v" and j >= 1:
                        store_v(j - 1)
                if "rms" in kind:
                    rms(k - 1)
                if kind == "v":
                    store_v(k - 1)
                if it is not None:
                    link.leave(trips)
            in_groups(act, name, body)

        def v_cols(at, off, w, rows):
            if at.it is None:
                return scr[0:rows, V0 + at.c * 384 + off:V0 + at.c * 384 + off + w]
            return scr[0:rows, bass.ds(at.it * (at.m * 384) + (V0 + at.c * 384 + off), w)]

        def mv_cols(at):
            return scr[:, L0 + at.c * 256:L0 + at.c * 256 + 256]

        def proj_dve(dve, link, name, kind, cols, first=None, scale=1.0, gcol=None, norm=0):
            n_cols = width(cols)
            vy = lyb if name == "sv" else yb
            dve.wait_ge(rstd_ready, norm + 1)

            def body(g, k, it, trips):
                if it is not None:
                    link.enter(it, k if "rope" in kind else 0)

                def normed(j):
                    r = g + (RFIRST[name] + j)
                    dve.wait_ge(y_rstd, (r + 1).value())
                    if kind == "rms":
                        dst, done = chunk_at(first, g + j, cols), y_done
                    else:
                        dst, done = y2[:, j % 2, cols], y_norm
                        dve.wait_ge(y_rot, (g + (OFIRST[name] + j - 1)).value())
                        dve.wait_ge(y_cos, (g + (OFIRST[name] + j - 1)).value())
                    dve.scalar_tensor_tensor(out=dst, in0=yb[:, j, cols], scalar=gcol, in1=hr[:, j % 2, cols],
                                             op0=ALU.mult, op1=ALU.mult).then_inc(done, 1)

                def rotated(j):
                    o = g + (OFIRST[name] + j)
                    dst = chunk_at(first, g + j, cols)
                    dve.wait_ge(y_rot, (o + 1).value())
                    dve.tensor_tensor(dst, bank[7][:, 0:n_cols], const("sin")[:, cols], ALU.mult).then_inc(link.sem, 1)
                    dve.wait_ge(link.sem, link.next())
                    dve.wait_ge(y_cos, (o + 1).value())
                    dve.tensor_tensor(dst, dst, mc[:, (OFIRST[name] + j) % 2, cols], ALU.add).then_inc(y_done, 1)

                for j in range(k):
                    b = g + (BSTART[name] + j)
                    dve.wait_ge(w_used, (g + (START[name] + j + 1)).value())
                    src = bank[b.mod(4)][:, 0:n_cols]
                    if kind == "plain":
                        dve.scalar_tensor_tensor(out=chunk_at(first, g + j, cols), in0=src, scalar=scale, in1=rstd[:, 0, cols],
                                                 op0=ALU.mult, op1=ALU.mult).then_inc(evac, 1)
                        split_lo(dve, g + (START[name] + j + AHEAD))
                        continue
                    if kind == "v":
                        if (g + (VFIRST[name] + j - 3)).c > 0:
                            dve.wait_ge(v_turned, (g + (VFIRST[name] + j - 3)).value())
                        dst = vy[:, j, cols]
                    elif kind == "rope":
                        if (g + (OFIRST[name] + j - 3)).c > 0:
                            dve.wait_ge(y_rot, (g + (OFIRST[name] + j - 3)).value())
                        if (g + (OFIRST[name] + j - 3)).c > 0:
                            dve.wait_ge(y_cos, (g + (OFIRST[name] + j - 3)).value())
                        dst = yb[:, (OFIRST[name] + j) % 4, cols]
                    else:
                        if (g + (RFIRST[name] + j - 3)).c > 0:
                            dve.wait_ge(y_sq, (g + (RFIRST[name] + j - 3)).value())
                        dst = yb[:, j, cols]
                    dve.tensor_tensor(dst, src, rstd[:, 0, cols], ALU.mult).then_inc(evac, 1)
                    split_lo(dve, g + (START[name] + j + AHEAD))
                    if "rms" in kind and j >= 1:
                        normed(j - 1)
                    if "rope" in kind and j >= 2:
                        rotated(j - 2)
                if "rms" in kind:
                    normed(k - 1)
                if "rope" in kind:
                    for j in range(max(0, k - 2), k):
                        rotated(j)
                if it is not None:
                    link.leave(trips)
            in_groups(dve, name, body)

        def proj_pool(pool, name, kind, cols):
            def body(g, k, it, trips):
                for j in range(k):
                    o = g + (OFIRST[name] + j)
                    oo = OFIRST[name] + j
                    if kind == "rope":
                        pool.wait_ge(evac, (g + (BSTART[name] + j + 1)).value())
                    else:
                        pool.wait_ge(y_norm, (g + (RFIRST[name] + j + 1)).value())
                    if (o + (-1)).c > 0:
                        pool.wait_ge(y_done, (o + (-1)).value())
                    src = yb[:, oo % 4, cols] if kind == "rope" else y2[:, j % 2, cols]
                    pool.tensor_tensor(mc[:, oo % 2, cols], src, const("cos")[:, cols], ALU.mult).then_inc(y_cos, 1)
            in_groups(pool, name, body)

        class Heads:
            def __init__(self, name, head0, pairs, pre, q, k, v, va, add, chunk0, cols, p, pt, sm):
                self.name, self.head0, self.pairs, self.pre = name, head0, pairs, pre
                self.q, self.k, self.v, self.va, self.add = q, k, v, va, add
                self.chunk0, self.cols, self.p, self.pt = chunk0, cols, p, pt
                self.nmx = sm[:, 0:4].rearrange("p (b n) -> p b n", b=2)
                self.ssum = sm[:, 4:8].rearrange("p (b n) -> p b n", b=2)
                self.rinv = sm[:, 8:12].rearrange("p (b n) -> p b n", b=2)
                self.w0, self.w1 = pre + 128, pre + 256

        def scores_pe(pe, a, i):
            hd, s = a.head0 + i, bank[4 + i % 2]
            if 2 * (hd - 1) > 0:
                pe.wait_ge(p_exp, 2 * (hd - 1))
            q, k = a.q(i), a.k(i)
            more = a.add is not None
            pe.matmul(s[:, 0:a.w0], q[:, 0:128], k[:, 0:a.w0], start=True, stop=not more, skip_group_check=True)
            mm = pe.matmul(s[:, a.w0:a.w0 + a.w1], q[:, 128:256], k[:, 0:a.w1], start=not more, stop=not more, skip_group_check=True)
            if more:
                mm = a.add(pe, i, s)
            mm.then_inc(s_ready, 1)

        def turn_pe(pe, a, i):
            hd, p, dst = a.head0 + i, a.p[:, i % 2, :], bank[6 + i % 2]
            pe.wait_ge(p_norm, 2 * (hd + 1))
            if hd - 1 > 0:
                pe.wait_ge(pt_copied, hd - 1)
            idn = const("ident")
            c0, c1 = a.pre, a.w0 + a.pre
            if a.pre:
                pe.transpose(bank[2 + i % 2][0:a.pre, 0:128], p[:, 0:a.pre], idn)
                pe.transpose(bank[2 + i % 2][0:a.pre, 128:256], p[:, a.w0:a.w0 + a.pre], idn)
            pe.transpose(dst[:, 0:128], p[:, c0:c0 + 128], idn)
            pe.transpose(dst[:, 128:256], p[:, c1:c1 + 128], idn)
            pe.transpose(dst[:, 256:384], p[:, c1 + 128:c1 + 256], idn).then_inc(pt_ready, 1)

        def values_pe(pe, a, s):
            pr = a.head0 // 2 + s
            o = bank[pr % 2]
            if pr - 1 > 0:
                pe.wait_ge(o_lo, pr - 1)
            for i in (2 * s, 2 * s + 1):
                pe.wait_ge(pt_copied, a.head0 + i + 1)
                dst, pt = o[64 * (i % 2):64 * (i % 2) + 64, :], a.pt[:, i % 2, :]
                if a.pre:
                    pe.matmul(dst[:, 0:256], a.va(i), probTA[0:META, i % 2, :], start=True, stop=False, skip_group_check=True)
                pe.matmul(dst[:, 0:256], a.v(i, 0), pt[:, 0:256], start=not a.pre, stop=False, skip_group_check=True)
                mm = pe.matmul(dst[:, 128:256], a.v(i, 1), pt[:, 256:384], start=False, stop=True, skip_group_check=True)
            mm.then_inc(o_ready, 1)

        def att_pe(pe, a, hook=None):
            for s in range(a.pairs + 1):
                if hook:
                    hook(0, s)
                for i in (2 * s, 2 * s + 1):
                    if s < a.pairs:
                        scores_pe(pe, a, i)
                    if s > 0:
                        turn_pe(pe, a, i - 2)
                if hook:
                    hook(1, s)
                if s > 0:
                    values_pe(pe, a, s - 1)

        def att_act(act, link, a, hook=None):
            for s in range(a.pairs + 1):
                if hook:
                    hook(0, s)
                for i in (2 * s, 2 * s + 1):
                    if s < a.pairs:
                        hd, sc = a.head0 + i, bank[4 + i % 2]
                        act.wait_ge(s_max, 2 * (hd + 1))
                        if hd - 1 > 0:
                            act.wait_ge(pt_ready, hd - 1)
                        for t, (c0, w) in enumerate(((0, a.w0), (a.w0, a.w1))):
                            act.activation(a.p[:, i % 2, c0:c0 + w], sc[:, c0:c0 + w], ACT.Exp, bias=a.nmx[:, i % 2, t:t + 1],
                                           accum_out=a.ssum[:, i % 2, t:t + 1]).then_inc(p_exp, 1)
                    if s > 0:
                        hd = a.head0 + i - 2
                        act.wait_ge(pt_ready, hd + 1)
                        if a.head0 // 2 + s - 1 > 0:
                            act.wait_ge(o_ready, a.head0 // 2 + s - 1)
                        if a.pre:
                            act.activation(probTA[0:a.pre, i % 2, :], bank[2 + i % 2][0:a.pre, 0:256], ACT.Copy).then_inc(link.sem, 1)
                            act.wait_ge(link.sem, link.next())
                        act.activation(a.pt[:, i % 2, 0:384], bank[6 + i % 2][:, 0:384], ACT.Copy).then_inc(pt_copied, 1)
                if hook:
                    hook(1, s)
                if s > 0:
                    pr = a.head0 // 2 + s - 1
                    act.wait_ge(o_ready, pr + 1)
                    act.activation(ahi[:, a.chunk0 + s - 1, a.cols], bank[pr % 2][:, 0:256], ACT.Copy).then_inc(o_hi, 1)

        def att_dve(dve, link, a, hook=None):
            for s in range(a.pairs + 1):
                if hook:
                    hook(0, s)
                if s < a.pairs:
                    for i in (2 * s, 2 * s + 1):
                        sc = bank[4 + i % 2]
                        dve.wait_ge(s_ready, a.head0 + i + 1)
                        for t, (c0, w) in enumerate(((0, a.w0), (a.w0, a.w1))):
                            dve.tensor_reduce(a.nmx[:, i % 2, t:t + 1], sc[:, c0:c0 + w], AX.X, ALU.max,
                                              negate=True).then_inc(s_max, 1)
                    if s > 0:
                        out_lo(dve, a, s - 1)
                    for i in (2 * s, 2 * s + 1):
                        dve.wait_ge(p_exp, 2 * (a.head0 + i + 1))
                        dve.reciprocal(a.rinv[:, i % 2, :], a.ssum[:, i % 2, :]).then_inc(link.sem, 1)
                        dve.wait_ge(link.sem, link.next())
                        for t, (c0, w) in enumerate(((0, a.w0), (a.w0, a.w1))):
                            p = a.p[:, i % 2, c0:c0 + w]
                            dve.tensor_scalar(p, p, a.rinv[:, i % 2, t:t + 1], None, ALU.mult).then_inc(p_norm, 1)
                else:
                    out_lo(dve, a, s - 1)
                if hook:
                    hook(1, s)

        def out_lo(dve, a, s):
            pr = a.head0 // 2 + s
            dve.wait_ge(o_hi, pr + 1)
            dst = a.chunk0 + s
            dve.tensor_tensor(alo[:, dst, a.cols], bank[pr % 2][:, 0:256], ahi[:, dst, a.cols].bitcast(F32),
                              ALU.subtract).then_inc(o_lo, 1)

        def half(ap, i):
            return ap[64 * (i % 2):64 * (i % 2) + 64]

        def v_of(i, tile, rows=P):
            c = V0 + (i // 2) * 384 + tile * 128 + 64 * (i % 2)
            return scr[0:rows, c:c + 64]

        def late_mask(pe, s):
            pe.matmul(s[:, 64:128], upperb, lateb, start=False, stop=True, skip_group_check=True)
            return pe.matmul(s[:, 128 + 192:128 + 256], upperb, lateb, start=False, stop=True, skip_group_check=True)

        def band_add(pe, i, s):
            pe.wait_ge(rel_loaded[i // 2 % 2], 16 * (i // 4 + 1))
            b, rev = relb[:, (i // 2) % 2, i % 2, :], const("rev")
            pe.matmul(s[:, 0:128], b[:, 0:128], rev, start=False, stop=False, skip_group_check=True)
            pe.matmul(s[:, 128:256], b[:, 128:256], rev, start=False, stop=False, skip_group_check=True)
            pe.matmul(s[:, 256:384], b[:, 0:128], rev, start=False, stop=False, skip_group_check=True)
            return late_mask(pe, s)

        def fox_add(pe, i, s):
            pe.matmul(s[:, 0:144], selb[0:96, i, :], csplit[0:96, 0:144], start=False, stop=False, skip_group_check=True)
            pe.matmul(s[:, 144:416], selb[0:96, i, :], csplit[0:96, 0:272], start=False, stop=False, skip_group_check=True)
            pe.matmul(s[:, 16:144], identb[:, :], causalb[:, :], start=False, stop=True, skip_group_check=True)
            return pe.matmul(s[:, 144 + 144:416], identb[:, :], causalb[:, :], start=False, stop=True, skip_group_check=True)

        def dsa_add(pe, i, s):
            pe.matmul(s[:, 0:128], identb[:, :], selmask[:, 0:128], start=False, stop=True, skip_group_check=True)
            return pe.matmul(s[:, 128:384], identb[:, :], selmask[:, 128:384], start=False, stop=True, skip_group_check=True)

        mla = Heads("mla", 0, 4, 0, lambda i: mq[0:96, i, :], lambda i: mk[0:96, i, :],
                    lambda i, t: scr[:, L0 + (4 + i // 2) * 256 + t * 128 + 64 * (i % 2):][:, 0:64], None,
                    lambda pe, i, s: late_mask(pe, s), 0, FIRST, mprob, mprobT, msmall)
        band = Heads("band", 8, 8, 0, lambda i: half(q_all[:, i // 2, FIRST], i), lambda i: half(k_all[:, i // 2, FIRST], i),
                     v_of, None, band_add, 0, FIRST, prob, probT, small)
        dsa = Heads("dsa", 24, 8, 0, lambda i: half(q_all[:, i // 2, 0:256], i), lambda i: half(k_all[:, i // 4, 0:256], i),
                    lambda i, t: scr[:, V0 + (i // 8) * 384 + t * 128 + 64 * ((i // 4) % 2):][:, 0:64], None,
                    dsa_add, 0, slice(0, 256), prob, probT, small)
        fox = Heads("fox", 40, 8, META, lambda i: half(q_all[:, i // 2, FIRST], i), lambda i: half(k_all[:, i // 2, WHOLE], i),
                    v_of, lambda i: v_of(i, 2, META), fox_add, 0, FIRST, prob, probT, small)

        SCALE_A = (NOPE + ROPE) ** -0.5

        def first_pe(pe):
            for i in range(QC + KVC + 1):
                if i - 3 > 0:
                    pe.wait_ge(evac, i - 3)
                unit_mm(pe, At(i), bank[i % 4][:, 0:SEQ], uhi, ulo, FIRST, x=u_chunk(0) if i == 0 else None)
                if i == 0:
                    norm_pe(pe, 0, FIRST)
            for s, (a, k) in enumerate(((0, QC), (QC, KVC))):
                pe.wait_ge(lat_sq, a + k)
                for i in range(k):
                    mm = pe.matmul(bank[5 + s][:, 0:SEQ], const("ones"), latsq[:, a + i, FIRST], start=i == 0, stop=i == k - 1)
                mm.then_inc(lat_stat, 1)
            pe.wait_ge(evac, BSTART["kr"] + 1)
            pe.matmul(bank[7][:, 0:SEQ], const("rotm"), lyb[:, 0, FIRST], start=True, stop=True).then_inc(kr_rot, 1)
            pe.wait_ge(lat_rstd, 2)
            pe.wait_ge(kr_done, 1)
            proj_pe(pe, "sv", "v", FIRST, 0)
            proj_pe(pe, "sq", "plain", FIRST, 0)
            proj_pe(pe, "sk", "plain", FIRST, 0)
            pe.wait_ge(v_stored, 4)
            pe.wait_ge(lat_lo, QC + KVC)

            def turn_and_rotate(i):
                b = BSTART["mla"] + 2 * i
                pe.wait_ge(evac, b + 1)
                if i > 0:
                    pe.wait_ge(m_qdone, i)
                pe.matmul(bank[7][:, 0:SEQ], const("rotm"), mq[:, i, :], start=True, stop=True).then_inc(m_rot, 1)
                pe.wait_ge(evac, b + 2)
                if i - 1 > 0:
                    pe.wait_ge(m_vstored, i - 1)
                for t in range(2):
                    mm = pe.transpose(bank[5 + i % 2][:, 64 * t:64 * t + 64], mk[64:128, i, 128 * t:128 * t + 128],
                                      const("ident")[64:128, 64:128])
                mm.then_inc(m_turned, 1)

            for i in range(8):
                b, n = BSTART["mla"] + 2 * i, At(START["mla"] + i)
                pe.wait_ge(evac, b - 2)
                unit_mm(pe, n, bank[b % 4][:, 0:SEQ], ahi[:, 16:, :], alo[:, 16:, :], FIRST, chunks=QC, used=False)
                unit_mm(pe, n, bank[(b + 1) % 4][:, 0:SEQ], ahi[:, 16 + QC:, :], alo[:, 16 + QC:, :], FIRST, chunks=KVC, at=QC)
                if i:
                    turn_and_rotate(i - 1)
            turn_and_rotate(7)

        def first_act(act, link):
            for n in range(AHEAD):
                split_hi(act, At(n))
            act.wait_ge(loaded, 16 * 4)
            act.wait_ge(bias_set, 2)
            for m in range(DC):
                norm_act(act, 0, m, FIRST, "mix0")
            norm_rstd(act, link, 0, FIRST)
            for i in range(QC + KVC + 1):
                split_hi(act, At(i + AHEAD))
                if i < QC + KVC:
                    act.wait_ge(evac, i + 1)
                    act.activation(latsq[:, i, FIRST], lat[:, i, FIRST], ACT.Square).then_inc(lat_sq, 1)
                    g = gain("cq", i) if i < QC else gain("ckv", i - QC)
                    act.activation(ahi[:, 16 + i, FIRST], lat[:, i, FIRST], ACT.Copy, scale=g).then_inc(lat_hi, 1)
            for s, w in enumerate((QL, KVL)):
                act.wait_ge(lat_stat, s + 1)
                act.wait_ge(rstd_ready, 1)
                if s > 0:
                    act.wait_ge(lat_rstd, s)
                act.activation(lg[:, FIRST], bank[5 + s][:, 0:SEQ], ACT.Ln, scale=1.0 / w, bias=bias[:, 0:1]).then_inc(link.sem, 1)
                act.wait_ge(link.sem, link.next())
                act.activation(rstd[:, 1 + s, FIRST], lg[:, FIRST], ACT.Exp, scale=-0.5).then_inc(lat_rstd, 1)
            proj_act(act, link, "sv", "v", FIRST)
            proj_act(act, link, "sq", "plain", FIRST)
            proj_act(act, link, "sk", "plain", FIRST)

            def store(i):
                act.wait_ge(m_turned, i + 1)
                c = L0 + (4 + i // 2) * 256 + 64 * (i % 2)
                for t in range(2):
                    ins = act.activation(scr[:, c + 128 * t:c + 128 * t + 64], bank[5 + i % 2][:, 64 * t:64 * t + 64], ACT.Copy)
                ins.then_inc(m_vstored, 1)
                act.wait_ge(kr_done, 1)
                act.activation(mk[64:96, i, :], kro[64:96, FIRST], ACT.Copy).then_inc(m_kdone, 1)

            for i in range(8):
                split_hi(act, At(START["mla"] + i + AHEAD))
                if i:
                    store(i - 1)
            store(7)

        def first_dve(dve, link):
            dve.wait_ge(loaded, 16 * 4)
            for c, (dst, name) in enumerate(((identb[:, :], "ident"), (causalb[:, :], "causal"))):
                dve.tensor_copy(dst, const(name)).then_inc(consts_cast, 1)
            dve.tensor_copy(rowsb[:, :], c_t[:, CCOL["upper"][0]:CCOL["rep"][1]]).then_inc(consts_cast, 1)
            dve.tensor_scalar(gains8[:, 0:1], gain("aq"), HD ** -0.5, None, ALU.mult).then_inc(consts_cast, 1)
            dve.tensor_scalar(gains8[:, 1:2], gain("bq"), HD ** -0.5, None, ALU.mult).then_inc(consts_cast, 1)
            for m in range(DC):
                norm_dve(dve, 0, m, FIRST, "mix0")
                if m < AHEAD:
                    split_lo(dve, At(m))

            def latent_lo(i):
                g = gain("cq", i) if i < QC else gain("ckv", i - QC)
                dve.wait_ge(lat_hi, i + 1)
                dve.scalar_tensor_tensor(out=alo[:, 16 + i, FIRST], in0=lat[:, i, FIRST], scalar=g,
                                         in1=ahi[:, 16 + i, FIRST].bitcast(F32), op0=ALU.mult, op1=ALU.subtract).then_inc(lat_lo, 1)

            dve.wait_ge(rstd_ready, 1)
            for i in range(QC + KVC + 1):
                dve.wait_ge(w_used, i + 1)
                dst = lat[:, i, FIRST] if i < QC + KVC else lyb[:, 0, FIRST]
                dve.tensor_tensor(dst, bank[i % 4][:, 0:SEQ], rstd[:, 0, FIRST], ALU.mult).then_inc(evac, 1)
                split_lo(dve, At(i + AHEAD))
                if i:
                    latent_lo(i - 1)
            dve.wait_ge(kr_rot, 1)
            dve.tensor_tensor(kro[64:96, FIRST], bank[7][64:96, 0:SEQ], const("sinm")[64:96, :], ALU.mult).then_inc(link.sem, 1)
            dve.wait_ge(link.sem, link.next())
            dve.tensor_tensor(lyb[64:96, 1, FIRST], lyb[64:96, 0, FIRST], const("cosm")[64:96, :], ALU.mult).then_inc(link.sem, 1)
            dve.wait_ge(link.sem, link.next())
            dve.tensor_tensor(kro[64:96, FIRST], kro[64:96, FIRST], lyb[64:96, 1, FIRST], ALU.add).then_inc(kr_done, 1)
            proj_dve(dve, link, "sv", "v", FIRST)
            proj_dve(dve, link, "sq", "plain", FIRST, first=0, scale=HD ** -0.5)
            proj_dve(dve, link, "sk", "plain", FIRST, first=4 * T)

            def rotate(i):
                dve.wait_ge(m_rot, i + 1)
                dve.tensor_tensor(lyb[64:96, 0, FIRST], mq[64:96, i, :], const("cosm")[64:96, :], ALU.mult).then_inc(link.sem, 1)
                dve.wait_ge(link.sem, link.next())
                dve.tensor_tensor(mq[64:96, i, :], bank[7][64:96, 0:SEQ], const("sinm")[64:96, :], ALU.mult).then_inc(link.sem, 1)
                dve.wait_ge(link.sem, link.next())
                dve.tensor_tensor(mq[64:96, i, :], mq[64:96, i, :], lyb[64:96, 0, FIRST], ALU.add).then_inc(m_qdone, 1)

            dve.wait_ge(lat_rstd, 2)
            for i in range(8):
                n, b = START["mla"] + i, BSTART["mla"] + 2 * i
                dve.wait_ge(w_used, n + 1)
                dve.scalar_tensor_tensor(out=mq[:, i, :], in0=bank[b % 4][:, 0:SEQ], scalar=SCALE_A, in1=rstd[:, 1, FIRST],
                                         op0=ALU.mult, op1=ALU.mult).then_inc(evac, 1)
                dve.tensor_tensor(mk[:, i, :], bank[(b + 1) % 4][:, 0:SEQ], rstd[:, 2, FIRST], ALU.mult).then_inc(evac, 1)
                split_lo(dve, At(n + AHEAD))
                if i:
                    rotate(i - 1)
            rotate(7)

        def diag(buf, b):
            return buf[:, b, :].rearrange("p (k n) -> p k n", k=3)[:, 0:3:2, :]

        def stick_pe(pe):
            def z(s):
                for b in range(2):
                    q, k = half(sbq[:, s, FIRST], b), half(sbk[:, s, FIRST], b)
                    if 2 * s > 0:
                        pe.wait_ge(z_arg, 2 * s)
                    pe.matmul(bank[2 + b][:, 0:256], k[:, 0:128], q, start=True, stop=True)
                    mm = pe.matmul(bank[2 + b][:, 256:384], k[:, 128:256], q[:, 128:256], start=True, stop=True)
                mm.then_inc(z_ready, 1)

            def sums(s):
                pe.wait_ge(z_masked, 4 * (s + 1))
                pe.wait_ge(z_split, 4 * (s + 1))
                for b in range(2):
                    dst, x = bank[2 + b], nlk[:, b, :]
                    pe.matmul(dst[:, 0:256], const("laterneg"), x[:, 0:256], start=True, stop=False, skip_group_check=True)
                    pe.matmul(dst[:, 128:256], const("allneg"), x[:, 256:384], start=False, stop=True, skip_group_check=True)
                    mm = pe.matmul(dst[:, 256:384], const("laterneg"), x[:, 256:384], start=True, stop=True, skip_group_check=True)
                mm.then_inc(z_sum, 1)

            def values(s):
                pe.wait_ge(z_w, 4 * (s + 1))
                for b in range(2):
                    v = [scr[:, L0 + s * 256 + t * 128 + 64 * b:][:, 0:64] for t in range(2)]
                    dst, w = bank[7][64 * b:64 * b + 64, :], zlog[:, b, :]
                    pe.matmul(dst[:, 0:256], v[0], w[:, 0:256], start=True, stop=False, skip_group_check=True)
                    mm = pe.matmul(dst[:, 128:256], v[1], w[:, 256:384], start=False, stop=True, skip_group_check=True)
                mm.then_inc(z_o, 1)
            for s in range(4):
                z(s)
                sums(s)
                if s > 0:
                    pe.wait_ge(z_olo, s)
                values(s)

        def stick_act(act, link):
            for s in range(4):
                for b in range(2):
                    act.wait_ge(z_ready, s + 1)
                    z = zlog[:, b, :]
                    if s > 0:
                        act.wait_ge(z_o, s)
                    act.activation(z, bank[2 + b][:, 0:384], ACT.Abs).then_inc(link.sem, 1)
                    act.wait_ge(link.sem, link.next())
                    act.activation(z, z, ACT.Exp, scale=-1.0).then_inc(link.sem, 1)
                    act.wait_ge(link.sem, link.next())
                    act.activation(z, z, ACT.Ln, bias=bias[:, 1:2]).then_inc(z_log, 1)
                for b in range(2):
                    act.wait_ge(z_arg, 2 * s + b + 1)
                    act.activation(zlog[:, b, :], ls[:, b, :], ACT.Exp).then_inc(z_exp, 1)
                act.wait_ge(z_o, s + 1)
                act.activation(ahi[:, 4 + s, FIRST], bank[7][:, 0:256], ACT.Copy).then_inc(z_ohi, 1)

        def stick_dve(dve):
            for s in range(4):
                for b in range(2):
                    dve.wait_ge(z_log, 2 * s + b + 1)
                    z = bank[2 + b][:, 0:384]
                    dve.scalar_tensor_tensor(out=nlk[:, b, :], in0=z, scalar=0.0, in1=zlog[:, b, :], op0=ALU.max, op1=ALU.add).then_inc(z_split, 1)
                    dve.scalar_tensor_tensor(out=ls[:, b, :], in0=z, scalar=0.0, in1=zlog[:, b, :], op0=ALU.min,
                                             op1=ALU.subtract).then_inc(z_split, 1)
                dve.wait_ge(z_sum, s + 1)
                for b in range(2):
                    dve.tensor_tensor(ls[:, b, :], ls[:, b, :], bank[2 + b][:, 0:384], ALU.add).then_inc(z_arg, 1)
                dve.wait_ge(z_ohi, s + 1)
                dve.tensor_tensor(alo[:, 4 + s, FIRST], bank[7][:, 0:256], ahi[:, 4 + s, FIRST].bitcast(F32), ALU.subtract).then_inc(z_olo, 1)

        def stick_pool(pool):
            before = const("before")
            for s in range(4):
                for b in range(2):
                    pool.wait_ge(z_split, 4 * s + 2 * b + 1)
                    for c in (0, 256):
                        pool.tensor_tensor(nlk[:, b, c:c + 128], nlk[:, b, c:c + 128], before, ALU.mult).then_inc(z_masked, 1)
                for b in range(2):
                    pool.wait_ge(z_exp, 2 * s + b + 1)
                    for c in (0, 256):
                        pool.tensor_tensor(zlog[:, b, c:c + 128], zlog[:, b, c:c + 128], before, ALU.mult).then_inc(z_w, 1)

        def wi_pe(pe):
            n, b = START["wi"], BSTART["wi"]
            pe.wait_ge(evac, b - 3)
            unit_mm(pe, At(n), bank[b % 4][:, 0:T], uhi, ulo, WHOLE)
            pe.wait_ge(evac, b + 1)
            for t in range(3):
                w = min(128, T - 128 * t)
                mm = pe.transpose(bank[6][0:w, 8 * t:8 * t + 8], relu_t[0:8, 0, 128 * t:128 * t + w], const("ident")[0:8, 0:8])
            mm.then_inc(wi_turned, 1)

        def wi_dve(dve):
            n, b = START["wi"], BSTART["wi"]
            split_lo(dve, At(n + AHEAD))
            dve.wait_ge(w_used, n + 1)
            dve.tensor_tensor(relu_t[0:8, 0, :], bank[b % 4][0:8, 0:T], rstd[0:8, 0, :], ALU.mult).then_inc(evac, 1)
            dve.wait_ge(wi_turned, 1)
            k = 8 ** -0.5 * HD ** -0.5
            dve.tensor_scalar(wi[:, 0:16], bank[6][:, 0:16], k, None, ALU.mult).then_inc(wi_done, 1)
            dve.tensor_scalar(wi[0:META, 16:24], bank[6][0:META, 16:24], k, None, ALU.mult).then_inc(wi_done, 1)

        def index_pe(pe):
            pe.wait_ge(y_done, 5)
            pe.wait_ge(wi_done, 2)
            for i in range(8):
                q, k = half(q_all[:, i // 2, :], i), half(q_all[:, 4, :], i)
                big, tail = (bank[5], bank[7]) if i % 2 == 0 else (bank[6], bank[4])
                if 2 * (i - 1) > 0:
                    pe.wait_ge(ix_relu, 2 * (i - 1))
                pe.matmul(big[:, 0:128], q[:, 0:128], k[:, 0:128], start=True, stop=True)
                pe.matmul(big[:, 128:384], q[:, 128:256], k[:, 0:256], start=True, stop=True)
                pe.matmul(tail[0:META, 0:T], q[:, 256:T], k[:, 0:T], start=True, stop=True).then_inc(ix_ready, 1)

        def index_act(act):
            for i in range(8):
                big, tail = (bank[5], bank[7]) if i % 2 == 0 else (bank[6], bank[4])
                act.wait_ge(ix_ready, i + 1)
                if 3 * (i - 1) > 0:
                    act.wait_ge(ix_acc, 3 * (i - 1))
                act.activation(relu[:, i % 2, 0:384], big[:, 0:384], ACT.Relu).then_inc(ix_relu, 1)
                act.activation(relu_t[0:META, i % 2, :], tail[0:META, 0:T], ACT.Relu).then_inc(ix_relu, 1)

        def index_dve(dve):
            for i in range(8):
                dve.wait_ge(ix_relu, 2 * (i + 1))
                for t, (src, rows) in enumerate(((relu[:, i % 2, 0:128], P), (relu[:, i % 2, 128:384], P), (relu_t[0:META, i % 2, :], META))):
                    w, dst = wi[0:rows, 8 * t + i:8 * t + i + 1], score[t][0:rows]
                    if i == 0:
                        dve.tensor_scalar(dst, src, w, None, ALU.mult).then_inc(ix_acc, 1)
                    else:
                        dve.wait_ge(ix_acc, 3 * (i - 1) + t + 1)
                        dve.scalar_tensor_tensor(out=dst, in0=src, scalar=w, in1=dst, op0=ALU.mult, op1=ALU.add).then_inc(ix_acc, 1)

        def topk_dve(dve, link, t):
            rows, w = (P, P, META)[t], (128, 256, T)[t]
            sc = score[t][0:rows]
            d0 = w - rows
            cm = const("causal")[0:rows, 0:rows]
            dve.wait_ge(ix_acc, 24)
            dve.tensor_tensor(sc[:, d0:w], sc[:, d0:w], cm, ALU.add).then_inc(link.sem, 1)
            dve.wait_ge(link.sem, link.next())
            for _ in range(TOPK // 8):
                dve.max(out=best[0:rows], in_=sc).then_inc(link.sem, 1)
                dve.wait_ge(link.sem, link.next())
                dve.match_replace(out=sc, in_to_replace=best[0:rows], in_values=sc, imm_value=TAKEN).then_inc(link.sem, 1)
                dve.wait_ge(link.sem, link.next())
            dve.tensor_scalar(sc, sc, TAKEN * 0.9, NEG, ALU.is_gt, ALU.mult).then_inc(link.sem, 1)
            dve.wait_ge(link.sem, link.next())
            dve.tensor_tensor(sc[:, d0:w], sc[:, d0:w], cm, ALU.add).then_inc(link.sem, 1)
            dve.wait_ge(link.sem, link.next())
            c0 = (0, 128, 384)[t]
            dve.tensor_copy(selmask[0:rows, c0:c0 + w], sc).then_inc(ix_mask, 1)

        tailq = area(E0 + 1760, 128)

        def tail_pe(pe):
            idn = const("ident")
            pe.wait_ge(t_q, 1)
            for t in range(2):
                s, pt, o = bank[2], bank[3], bank[5]
                if t > 0:
                    pe.wait_ge(t_exp, t)
                for r in range(4):
                    g, par = 2 * t + r // 2, r % 2
                    q = tailq[64 * par:64 * par + 64, 32 * g:32 * g + 32]
                    pe.matmul(s[32 * r:32 * r + 32, 0:T], q, k_all[64 * par:64 * par + 64, g, 0:T], start=True, stop=False, skip_group_check=True)
                pe.matmul(s[:, 0:T], repb, selmask[0:META, 384:384 + T], start=False, stop=True, skip_group_check=True).then_inc(t_s, 1)
                pe.wait_ge(t_p, t + 1)
                if 2 * t > 0:
                    pe.wait_ge(t_pts, 2 * t)
                p = prob[:, 0, 0:T]
                pe.transpose(pt[0:META, 256:384], p[:, 256:T], idn)
                pe.transpose(pt[:, 0:128], p[:, 0:128], idn)
                pe.transpose(pt[:, 128:256], p[:, 128:256], idn).then_inc(t_pt, 1)
                pe.wait_ge(t_pts, 2 * (t + 1))
                if t > 0:
                    pe.wait_ge(t_olo, t)
                for r in range(4):
                    g, par = 2 * t + r // 2, r % 2
                    dst = o[64 * par:64 * par + 64, 32 * (r // 2):32 * (r // 2) + 32]
                    for tile, rows in ((0, P), (1, P), (2, META)):
                        c = V0 + (g // 2) * 384 + tile * 128 + 64 * (g % 2)
                        mm = pe.matmul(dst, scr[0:rows, c:c + 64], probT[0:rows, 0, 128 * tile + 32 * r:128 * tile + 32 * r + 32],
                                       start=tile == 0, stop=tile == 2, skip_group_check=True)
                mm.then_inc(t_o, 1)

        def tail_act(act):
            for t in range(2):
                act.wait_ge(t_max, t + 1)
                if t > 0:
                    act.wait_ge(t_pt, t)
                act.activation(prob[:, 0, 0:T], bank[2][:, 0:T], ACT.Exp, bias=small[:, 16:17], accum_out=small[:, 17:18]).then_inc(t_exp, 1)
                act.wait_ge(t_pt, t + 1)
                if t > 0:
                    act.wait_ge(t_o, t)
                act.activation(probT[0:META, 0, 256:384], bank[3][0:META, 256:384], ACT.Copy).then_inc(t_pts, 1)
                act.activation(probT[:, 0, 0:256], bank[3][:, 0:256], ACT.Copy).then_inc(t_pts, 1)
                act.wait_ge(t_o, t + 1)
                act.activation(ahi[:, 4 * t:4 * t + 4, 256:T], bank[5][:, 0:64].rearrange("p (c n) -> p c n", n=META),
                               ACT.Copy).then_inc(t_ohi, 1)

        def tail_dve(dve, link):
            dve.tensor_copy(tailq.rearrange("p (c n) -> p c n", n=META), q_all[:, :, 256:T]).then_inc(t_q, 1)
            for t in range(2):
                dve.wait_ge(t_s, t + 1)
                dve.tensor_reduce(small[:, 16:17], bank[2][:, 0:T], AX.X, ALU.max, negate=True).then_inc(t_max, 1)
                dve.wait_ge(t_exp, t + 1)
                dve.reciprocal(small[:, 18:19], small[:, 17:18]).then_inc(link.sem, 1)
                dve.wait_ge(link.sem, link.next())
                dve.tensor_scalar(prob[:, 0, 0:T], prob[:, 0, 0:T], small[:, 18:19], None, ALU.mult).then_inc(t_p, 1)
                dve.wait_ge(t_ohi, t + 1)
                dve.tensor_tensor(alo[:, 4 * t:4 * t + 4, 256:T], bank[5][:, 0:64].rearrange("p (c n) -> p c n", n=META),
                                  ahi[:, 4 * t:4 * t + 4, 256:T].bitcast(F32), ALU.subtract).then_inc(t_olo, 1)

        fx, fe, fc = area(E0 + 1760, T), area(E0 + 1760 + T, T), area(S0, T)

        def forget_pe(pe):
            n, b = START["ff"], BSTART["ff"]
            pe.wait_ge(evac, b - 3)
            unit_mm(pe, At(n), bank[b % 4][:, 0:T], uhi, ulo, WHOLE, x=u_chunk(7))
            norm_pe(pe, 7, WHOLE)

        def forget_act(act, link):
            split_hi(act, At(START["ff"] + AHEAD))
            x = fx[0:16]
            act.wait_ge(f_exp, 1)
            act.activation(fe[0:16], x, ACT.Abs).then_inc(link.sem, 1)
            act.wait_ge(link.sem, link.next())
            act.activation(fe[0:16], fe[0:16], ACT.Exp, scale=-1.0).then_inc(link.sem, 1)
            act.wait_ge(link.sem, link.next())
            act.activation(fe[0:16], fe[0:16], ACT.Ln, bias=bias[0:16, 1:2]).then_inc(f_log, 1)

        def forget_dve(dve, link):
            n, b = START["ff"], BSTART["ff"]
            split_lo(dve, At(n + AHEAD))
            dve.wait_ge(rstd_ready, 8)
            dve.wait_ge(w_used, n + 1)
            dve.memset(csplit[:, :], 0.0).then_inc(link.sem, 1)
            dve.wait_ge(link.sem, link.next())
            x, l = fx[0:16], fe[0:16]
            dve.tensor_tensor(x, bank[b % 4][0:16, 0:T], rstd[0:16, 0, :], ALU.mult).then_inc(evac, 1)
            dve.wait_ge(evac, b + 1)
            dve.tensor_scalar(x, x, gain("fb")[0:16], None, ALU.add).then_inc(f_exp, 1)
            dve.wait_ge(f_log, 1)
            dve.scalar_tensor_tensor(out=x, in0=x, scalar=0.0, in1=l, op0=ALU.min, op1=ALU.subtract).then_inc(link.sem, 1)
            dve.wait_ge(link.sem, link.next())
            dve.memset(l, 1.0).then_inc(link.sem, 1)
            dve.wait_ge(link.sem, link.next())
            c = fc[0:16]
            dve.tensor_tensor_scan(c, l, x, 0.0, ALU.mult, ALU.add).then_inc(link.sem, 1)
            dve.wait_ge(link.sem, link.next())
            dve.tensor_scalar(c, c, -1.0, None, ALU.mult).then_inc(link.sem, 1)
            dve.wait_ge(link.sem, link.next())
            for k in range(3):
                part = csplit[32 * k:32 * k + 16, :]
                dve.tensor_copy(part, c).then_inc(f_split, 1)
                dve.wait_ge(f_split, k + 1)
                if k < 2:
                    dve.tensor_copy(l, part).then_inc(link.sem, 1)
                    dve.wait_ge(link.sem, link.next())
                    dve.tensor_tensor(c, c, l, ALU.subtract).then_inc(link.sem, 1)
                    dve.wait_ge(link.sem, link.next())

        def second_u_act(act):
            for m in range(DC):
                act.activation(ahi[:, 8 + m, :], h[:, m, :], ACT.Copy, scale=gain("attn1", m)).then_inc(u2_hi, 1)

        def second_u_dve(dve):
            for m in range(DC):
                dve.wait_ge(u2_hi, m + 1)
                dve.scalar_tensor_tensor(out=alo[:, 8 + m, :], in0=h[:, m, :], scalar=gain("attn1", m),
                                         in1=ahi[:, 8 + m, :].bitcast(F32), op0=ALU.mult, op1=ALU.subtract).then_inc(u2_lo, 1)

        block = ctx.enter_context(nc.Block())

        @block.sync
        def _(sp):
            sp.dma_start(h[:, :, META:T], xT).then_inc(loaded, 16)
            sp.dma_start(g_t[:, :], gains).then_inc(loaded, 16)
            sp.dma_start(c_t[:, :], consts).then_inc(loaded, 16)
            sp.dma_start(h[:, :, 0:META], metaT).then_inc(loaded, 16)
            for s in range(RING):
                sp.dma_start(raw[:, s, :], stream[s]).then_inc(w_loaded[s], 16)
            with sp.Fori(1, UNITS // RING) as it:
                for s in range(RING):
                    sp.wait_ge(w_lo, it * RING + (s - RING + 1))
                    sp.dma_start(raw[:, s, :], stream[bass.ds(it * RING + s, 1)].rearrange("a p n -> (a p) n")).then_inc(w_loaded[s], 16)
            for s in range(UNITS % RING):
                n = UNITS // RING * RING + s
                sp.wait_ge(w_lo, n - RING + 1)
                sp.dma_start(raw[:, s, :], stream[n]).then_inc(w_loaded[s], 16)
            for m in range(DC):
                sp.wait_ge(evac, BSTART["dn3"] + m + 1)
                sp.dma_start(out[:, m, :], h[:, m, META:T]).then_inc(stored, 16)
            sp.wait_ge(stored, 16 * DC)

        @block.tensor
        def _(pe):
            pe.wait_ge(loaded, 16 * 4)
            pe.wait_ge(consts_cast, 5)
            first_pe(pe)
            pe.wait_ge(m_qdone, 8)
            pe.wait_ge(m_kdone, 8)
            pe.wait_ge(evac, BSTART["out0"])
            stick_pe(pe)
            pe.wait_ge(z_olo, 4)
            att_pe(pe, mla)
            resid_pe(pe, "out0", DC, FIRST, lambda i: (o_lo, i + 1) if i < 4 else (z_olo, i - 3))
            swiglu_pe(pe, "gu0", FIRST, 1)
            resid_pe(pe, "dn0", FC1, FIRST, lambda i: (a_lo, i + 1))
            proj_pe(pe, "bv", "v", FIRST, 2, sum_norm=2)
            proj_pe(pe, "bq", "plain", FIRST, 2)
            proj_pe(pe, "bk", "plain", FIRST, 2)
            pe.wait_ge(evac, BSTART["out1"])
            pe.wait_ge(v_stored, VFIRST["dv"])
            att_pe(pe, band)
            resid_pe(pe, "out1", DC, FIRST, lambda i: (o_lo, 4 + i + 1))
            swiglu_pe(pe, "gu1", FIRST, 3)
            resid_pe(pe, "dn1", FC1, FIRST, lambda i: (a_lo, FC1 + i + 1))
            norm_pe(pe, 4, FIRST)
            proj_pe(pe, "ki", "rope", WHOLE, 5, sum_norm=5)
            wi_pe(pe)
            proj_pe(pe, "qi", "rope", WHOLE, 5)
            index_pe(pe)
            pe.wait_ge(ix_relu, 16)
            proj_pe(pe, "dk", "rmsrope", WHOLE, 5)
            pe.wait_ge(y_done, 9)
            pe.wait_ge(y_rstd, 4)
            proj_pe(pe, "dv", "v", WHOLE, 5)
            pe.wait_ge(v_stored, VFIRST["fv"])
            proj_pe(pe, "dq", "rmsrope", WHOLE, 5)
            pe.wait_ge(y_done, 17)
            pe.wait_ge(ix_mask, 3)
            att_pe(pe, dsa)
            tail_pe(pe)
            pe.wait_ge(t_olo, 2)
            resid_pe(pe, "out2", DC, WHOLE, lambda i: (o_lo, 12 + i + 1))
            sqrelu_pe(pe, "up2", WHOLE, 6)
            resid_pe(pe, "dn2", FC2, WHOLE, lambda i: (a_lo, 2 * FC1 + i + 1))
            forget_pe(pe)
            proj_pe(pe, "fv", "v", WHOLE, 7)
            pe.wait_ge(v_stored, 22)
            proj_pe(pe, "fk", "rms", WHOLE, 7)
            proj_pe(pe, "fq", "rms", FIRST, 7, second=True)
            pe.wait_ge(y_done, 33)
            pe.wait_ge(f_split, 3)
            pe.wait_ge(sel_loaded, 16)
            att_pe(pe, fox)
            resid_pe(pe, "out3", DC, FIRST, lambda i: (o_lo, 20 + i + 1))
            sqrelu_pe(pe, "up3", FIRST, 8)
            resid_pe(pe, "dn3", FC2, FIRST, lambda i: (a_lo, 2 * FC1 + FC2 + i + 1))

        @block.scalar
        def _(act):
            act.preload_act_table_set("natural_log_exp_and_others")
            link = Chain(act_chain)
            first_act(act, link)
            stick_act(act, link)
            att_act(act, link, mla)
            resid_act(act, link, "out0", DC, FIRST, 1, "ffn0")
            swiglu_act(act, link, "gu0", FIRST)
            resid_act(act, link, "dn0", FC1, FIRST, 2, "mix1")
            proj_act(act, link, "bv", "v", FIRST)
            proj_act(act, link, "bq", "plain", FIRST)
            proj_act(act, link, "bk", "plain", FIRST)

            def relh_load(where, s):
                if where == 0 and s < band.pairs:
                    if s == 0:
                        act.wait_ge(evac, BSTART["out1"])
                        for n in (0, 1):
                            act.dma_start(relb[:, n, :, :], relh[n]).then_inc(rel_loaded[n], 16)
                if where == 1 and s + 2 < band.pairs:
                    act.wait_ge(s_ready, band.head0 + 2 * s + 2)
                    act.dma_start(relb[:, s % 2, :, :], relh[s + 2]).then_inc(rel_loaded[s % 2], 16)
            att_act(act, link, band, relh_load)
            resid_act(act, link, "out1", DC, FIRST, 3, "ffn1")
            swiglu_act(act, link, "gu1", FIRST)
            resid_act(act, link, "dn1", FC1, FIRST, 4, "final")
            for m in range(DC):
                act.wait_ge(x2_ready, m + 1)
                norm_act(act, 5, m, WHOLE, "attn0")
            norm_rstd(act, link, 5, WHOLE)
            proj_act(act, link, "ki", "rope", WHOLE)
            split_hi(act, At(START["wi"] + AHEAD))
            proj_act(act, link, "qi", "rope", WHOLE)
            index_act(act)
            proj_act(act, link, "dk", "rmsrope", WHOLE)
            proj_act(act, link, "dv", "v", WHOLE)
            proj_act(act, link, "dq", "rmsrope", WHOLE)
            att_act(act, link, dsa)
            tail_act(act)
            resid_act(act, link, "out2", DC, WHOLE, 6, "mlp0")
            sqrelu_act(act, "up2", WHOLE)
            resid_act(act, link, "dn2", FC2, WHOLE, 7, "kvn")
            act.dma_start(area(E0, 1024)[0:96, :], sel).then_inc(sel_loaded, 16)
            forget_act(act, link)
            proj_act(act, link, "fv", "v", WHOLE)
            second_u_act(act)
            proj_act(act, link, "fk", "rms", WHOLE)
            proj_act(act, link, "fq", "rms", FIRST)
            att_act(act, link, fox)
            resid_act(act, link, "out3", DC, FIRST, 8, "mlp1")
            sqrelu_act(act, "up3", FIRST)
            resid_act(act, link, "dn3", FC2, FIRST, None, None)

        @block.vector
        def _(dve):
            link = Chain(dve_chain)
            first_dve(dve, link)
            stick_dve(dve)
            att_dve(dve, link, mla)
            resid_dve(dve, "out0", DC, FIRST, 1, "ffn0")
            swiglu_dve(dve, "gu0", FIRST, 1, 0)
            resid_dve(dve, "dn0", FC1, FIRST, 2, "mix1")
            proj_dve(dve, link, "bv", "v", FIRST, norm=2)
            proj_dve(dve, link, "bq", "plain", FIRST, first=Q0, scale=HD ** -0.5, norm=2)
            proj_dve(dve, link, "bk", "plain", FIRST, first=K0, norm=2)
            att_dve(dve, link, band)
            resid_dve(dve, "out1", DC, FIRST, 3, "ffn1")
            swiglu_dve(dve, "gu1", FIRST, 3, FC1)
            resid_dve(dve, "dn1", FC1, FIRST, 4, "final")
            dve.wait_ge(rstd_ready, 5)
            for m in range(DC):
                dve.scalar_tensor_tensor(out=h[:, m, FIRST], in0=h[:, m, FIRST], scalar=gain("final", m), in1=rstd[:, 0, FIRST],
                                         op0=ALU.mult, op1=ALU.mult).then_inc(x2_ready, 1)
            for m in range(DC):
                norm_dve(dve, 5, m, WHOLE, "attn0")
            proj_dve(dve, link, "ki", "rope", WHOLE, first=4 * T, norm=5)
            wi_dve(dve)
            proj_dve(dve, link, "qi", "rope", WHOLE, first=0, norm=5)
            index_dve(dve)
            proj_dve(dve, link, "dk", "rmsrope", WHOLE, first=K0, gcol=gain("ak"), norm=5)
            topk_dve(dve, link, 0)
            proj_dve(dve, link, "dv", "v", WHOLE, norm=5)
            topk_dve(dve, link, 1)
            proj_dve(dve, link, "dq", "rmsrope", WHOLE, first=Q0, gcol=gains8[:, 0:1], norm=5)
            topk_dve(dve, link, 2)
            att_dve(dve, link, dsa)
            tail_dve(dve, link)
            resid_dve(dve, "out2", DC, WHOLE, 6, "mlp0")
            sqrelu_dve(dve, "up2", WHOLE, 6, 2 * FC1)
            resid_dve(dve, "dn2", FC2, WHOLE, 7, "kvn")
            forget_dve(dve, link)
            proj_dve(dve, link, "fv", "v", WHOLE, norm=7)
            second_u_dve(dve)
            proj_dve(dve, link, "fk", "rms", WHOLE, first=K0, gcol=gain("kk"), norm=7)
            proj_dve(dve, link, "fq", "rms", FIRST, first=Q0, gcol=gains8[:, 1:2], norm=7)
            att_dve(dve, link, fox)
            resid_dve(dve, "out3", DC, FIRST, 8, "mlp1")
            sqrelu_dve(dve, "up3", FIRST, 8, 2 * FC1 + FC2)
            resid_dve(dve, "dn3", FC2, FIRST, None, None)

        @block.gpsimd
        def _(pool):
            pool.memset(bias[:, 0:1], EPS).then_inc(bias_set, 1)
            pool.memset(bias[:, 1:2], 1.0).then_inc(bias_set, 1)
            norm_pool(pool, 0, FIRST)
            stick_pool(pool)
            norm_pool(pool, 1, FIRST)
            swiglu_pool(pool, "gu0", FIRST, 1, 0)
            norm_pool(pool, 2, FIRST)
            norm_pool(pool, 3, FIRST)
            swiglu_pool(pool, "gu1", FIRST, 3, FC1)
            norm_pool(pool, 4, FIRST)
            norm_pool(pool, 5, WHOLE)
            proj_pool(pool, "ki", "rope", WHOLE)
            proj_pool(pool, "qi", "rope", WHOLE)
            proj_pool(pool, "dk", "rmsrope", WHOLE)
            proj_pool(pool, "dq", "rmsrope", WHOLE)
            norm_pool(pool, 6, WHOLE)
            sqrelu_pool(pool, "up2", WHOLE, 2 * FC1, 0)
            norm_pool(pool, 7, WHOLE)
            norm_pool(pool, 8, FIRST)
            sqrelu_pool(pool, "up3", FIRST, 2 * FC1 + FC2, FC2)


def unit_of(w, cols, chunks=None):
    u = np.zeros((P, DC, P), w.dtype)
    k = w.shape[0] // P
    u[:, :k, :len(cols)] = w[:, cols].reshape(k, P, len(cols)).transpose(1, 0, 2)
    return u.reshape(P, UNIT)


def blocks_of(w, first, last):
    units = []
    for c in range(first, last, P):
        for r in range(0, w.shape[0], UNIT):
            units.append(unit_of(w[r:r + UNIT], np.arange(c, c + P)))
    return units


def stream_of(a):
    w_in = a["ev_w_in"][0]
    o = QL + KVL + ROPE
    nb = 8 * HD
    s = blocks_of(w_in, 0, QL) + blocks_of(w_in, QL, QL + KVL)
    kr = unit_of(w_in, np.arange(QL + KVL, o)).reshape(P, DC, P)
    moved = np.zeros_like(kr)
    moved[:, :, NOPE:NOPE + ROPE] = kr[:, :, 0:ROPE]
    s.append(moved.reshape(P, UNIT))
    s += blocks_of(w_in, o + 2 * nb, o + 3 * nb) + blocks_of(w_in, o, o + nb) + blocks_of(w_in, o + nb, o + 2 * nb)
    uq, ukv = a["ev_w_uq"][0], a["ev_w_ukv"][0]
    for i in range(8):
        u = np.zeros((P, DC, P), uq.dtype)
        u[:, :QC] = unit_of(uq, np.arange(96 * i, 96 * i + 96)).reshape(P, DC, P)[:, :QC]
        u[:, QC:QC + KVC] = unit_of(ukv, np.arange(128 * i, 128 * i + 128)).reshape(P, DC, P)[:, :KVC]
        s.append(u.reshape(P, UNIT))
    s += blocks_of(a["ev_w_out"][0], 0, D)

    def swiglu(layer):
        g, u = blocks_of(a["w_gate"][layer], 0, FF1), blocks_of(a["w_up"][layer], 0, FF1)
        return [x for pair in zip(g, u) for x in pair] + blocks_of(a["w_down"][layer], 0, D)

    s += swiglu(0)
    qkv = a["od_w_qkv"][0]
    s += blocks_of(qkv, 2 * D, 3 * D) + blocks_of(qkv, 0, D) + blocks_of(qkv, D, 2 * D) + blocks_of(a["od_w_out"][0], 0, D)
    s += swiglu(1)
    w = a["a_w_in_2"][0]
    q, k, v, qi, ki = D, D + 256, D + 512, D + 1024, D + 1088
    two = np.arange(HD)
    s.append(unit_of(w, np.concatenate([qi + two, qi + two])))
    s.append(unit_of(w, np.arange(ki, ki + 8)))
    s += blocks_of(w, v, qi)
    for g in range(4):
        s.append(unit_of(w, np.concatenate([q + HD * g + two, q + HD * g + two])))
    s += blocks_of(w, k, v) + blocks_of(w, 0, D)
    s += blocks_of(a["a_w_out_2"][0], 0, D) + blocks_of(a["mlp_w1_2"][0], 0, FF2) + blocks_of(a["mlp_w2_2"][0], 0, D)
    w = a["kv_w_2"]
    s.append(unit_of(w, np.arange(2 * D, 2 * D + 16)))
    s += blocks_of(w, D, 2 * D) + blocks_of(w, 0, D) + blocks_of(a["b_w_q_2"][0], 0, D)
    s += blocks_of(a["b_w_out_2"][0], 0, D) + blocks_of(a["mlp_w1_2"][1], 0, FF2) + blocks_of(a["mlp_w2_2"][1], 0, D)
    s += [np.zeros((P, UNIT), w.dtype)] * AHEAD
    assert len(s) == UNITS
    return np.stack(s)


def gains_of(a):
    g = np.zeros((P, NG), np.float32)

    def put(name, v):
        v = np.asarray(v)
        g[:, GCOL[name]:GCOL[name] + v.size // P] = v.reshape(-1, P).T

    for name, v in (("mix0", a["g_mix"][0]), ("ffn0", a["g_ffn"][0]), ("mix1", a["g_mix"][1]), ("ffn1", a["g_ffn"][1]),
                    ("final", a["g_final"]), ("attn0", a["attn_norm_2"][0]), ("mlp0", a["mlp_norm_2"][0]), ("kvn", a["kv_norm_2"]),
                    ("attn1", a["attn_norm_2"][1]), ("mlp1", a["mlp_norm_2"][1]), ("cq", a["ev_g_cq"][0]), ("ckv", a["ev_g_ckv"][0])):
        put(name, v)
    for name, v in (("aq", a["a_q_gain_2"][0]), ("ak", a["a_k_gain_2"][0]), ("kk", a["kv_k_gain_2"]), ("bq", a["b_q_gain_2"][0])):
        put(name, np.concatenate([v, v]))
    g[0:16, GCOL["fb"]] = a["kv_f_bias_2"]
    return g


def constants():
    c = np.zeros((P, NCONST), np.float32)

    def put(name, v):
        v = np.asarray(v, np.float32)
        c[:v.shape[0], CCOL[name][0]:CCOL[name][0] + v.shape[1]] = v

    i, j = np.arange(P)[:, None], np.arange(P)[None, :]
    put("ident", i == j)
    put("rev", i + j == P - 1)
    put("ones", np.ones((P, P)))
    put("headones", i // HD == j // HD)
    put("laterneg", -(i > j).astype(np.float32))
    put("allneg", -np.ones((P, P)))
    put("before", i < j)
    put("causal", np.where(j > i, NEG, 0.0))

    def rotation(first, heads, dim):
        r = np.zeros((P, P), np.float32)
        for hd in range(heads):
            for d in range(dim // 2):
                lo = first + hd * dim + d
                r[lo + dim // 2, lo] = -1.0
                r[lo, lo + dim // 2] = 1.0
        return r

    put("rot", rotation(0, 2, HD))
    put("rotm", rotation(NOPE, 1, ROPE))

    def tables(n, dim, inv):
        ang = np.arange(n, dtype=np.float32)[:, None] * inv[None, :]
        return np.cos(ang).T.astype(np.float32), np.sin(ang).T.astype(np.float32)

    e = np.arange(0, HD, 2, dtype=np.float32) / np.float32(HD)
    cos, sin = tables(T, HD, (np.float32(1.0) / (np.float32(10000.0) ** e)).astype(np.float32))
    put("cos", np.tile(cos, (4, 1)))
    put("sin", np.tile(sin, (4, 1)))
    e = -np.arange(0, ROPE, 2, dtype=np.float32) / np.float32(ROPE)
    cos, sin = tables(SEQ, ROPE, (np.float32(10000.0) ** e).astype(np.float32))
    z = np.zeros((NOPE, SEQ), np.float32)
    put("cosm", np.concatenate([z, cos, cos]))
    put("sinm", np.concatenate([z, sin, sin]))
    put("upper", (np.arange(P) < 64)[None, :])
    put("late", np.full((1, 64), NEG))
    put("rep", (np.arange(P)[None, :] % META) == np.arange(META)[:, None])
    return c


def selection():
    s = np.zeros((96, 16, P), np.uint16)
    for k in range(3):
        for hd in range(16):
            s[32 * k + hd, hd, :] = 0x3F80
    return s.reshape(96, -1).view(np.float32)


def bias_tiles(rb):
    at = 129 + np.arange(P)[:, None] + np.arange(2 * P)[None, :]
    return np.ascontiguousarray(rb[:, at].reshape(8, 2, P, 2 * P).transpose(0, 2, 1, 3))


def kernel(**inputs):
    from concourse import bacc
    from concourse.bass_utils import run_bass_kernel_spmd

    a = {k: np.asarray(v) for k, v in inputs.items()}
    nc = bacc.Bacc("TRN2", target_bir_lowering=False, num_devices=1)

    def chunked(x):
        return np.ascontiguousarray(x.T.reshape(DC, P, x.shape[0]).transpose(1, 0, 2))

    arrays = {
        "stream": stream_of(a), "xT": chunked(a["x"][0]), "metaT": chunked(a["meta_tokens_2"]),
        "gains": gains_of(a), "consts": constants(), "relh": bias_tiles(a["od_rel_bias"][0]), "sel": selection(),
    }
    aps = [nc.dram_tensor(n, v.shape, mybir.dt.from_np(v.dtype), kind="ExternalInput").ap() for n, v in arrays.items()]
    out = nc.dram_tensor("out", (P, DC, SEQ), F32, kind="ExternalOutput").ap()
    program(nc, *aps, out)
    r = run_bass_kernel_spmd(nc, [arrays], core_ids=[0])
    got = np.asarray(r.results[0]["out"])
    return np.ascontiguousarray(got.transpose(1, 0, 2).reshape(D, SEQ).T)[None]
```

```python
from contextlib import ExitStack

import concourse.bass as bass
import numpy as np
from concourse import mybir

ALU = mybir.AluOpType
ACT = mybir.ActivationFunctionType
AX = mybir.AxisListType
F32 = mybir.dt.float32
F32R = mybir.dt.float32r
BF16 = mybir.dt.bfloat16

P = 128
D = 1024
DC = D // P
META = 16
SEQ = 256
T = META + SEQ
QL, KVL = 384, 256
QC, KVC = QL // P, KVL // P
ROPE = 32
NOPE = 64
HD = 64
FF1 = 2816
FC1 = FF1 // P
FF2 = 4096
FC2 = FF2 // P
TOPK = 64
EPS = 1e-6
NEG = -1e30
TAKEN = -3e38
RING = 4
AHEAD = RING - 1
UNIT = DC * P

PHASES = [
    ("cq", 3), ("ckv", 2), ("kr", 1), ("sv", 4), ("sq", 4), ("sk", 4), ("mla", 8), ("out0", 8),
    ("gu0", 44), ("dn0", 24),
    ("bv", 8), ("bq", 8), ("bk", 8), ("out1", 8), ("gu1", 44), ("dn1", 24),
    ("ki", 1), ("wi", 1), ("qi", 4), ("dk", 4), ("dv", 2), ("dq", 8), ("out2", 8), ("up2", 32), ("dn2", 32),
    ("ff", 1), ("fv", 8), ("fk", 8), ("fq", 8), ("out3", 8), ("up3", 32), ("dn3", 32),
    ("end", AHEAD),
]
START = {}
_n = 0
for _name, _k in PHASES:
    START[_name] = _n
    _n += _k
UNITS = _n

BSTART = {}
_n = 0
for _name, _k in PHASES:
    BSTART[_name] = _n
    _n += {"dn": 8, "ml": 16, "en": 0}.get(_name[:2], _k)

GAINS = ["mix0", "ffn0", "mix1", "ffn1", "final", "attn0", "mlp0", "kvn", "attn1", "mlp1"]
GCOL = {name: DC * i for i, name in enumerate(GAINS)}
GCOL.update(cq=80, ckv=83, aq=85, ak=86, kk=87, bq=88, fb=89)
NG = 90

CONSTS = [("ident", 128), ("rev", 128), ("headones", 128), ("laterneg", 128), ("allneg", 128),
          ("rot", 128), ("rotm", 128), ("before", 128), ("causal", 128), ("cos", T), ("sin", T),
          ("cosm", SEQ), ("sinm", SEQ), ("upper", 128), ("late", 64), ("rep", 128)]
CCOL = {}
_n = 0
for _name, _k in CONSTS:
    CCOL[_name] = (_n, _n + _k)
    _n += _k
NCONST = _n


class At:

    def __init__(self, c, it=None, m=0):
        self.c, self.it, self.m = c, it, m

    def __add__(self, k):
        return At(self.c + k, self.it, self.m)

    def times(self, k):
        return At(self.c * k, self.it, self.m * k)

    def mod(self, k):
        assert self.m % k == 0
        return self.c % k

    def div(self, k):
        assert self.m % k == 0
        return At(self.c // k, self.it, self.m // k)

    def value(self):
        assert self.c > 0
        return self.c if self.it is None else self.it * self.m + self.c


class Chain:

    def __init__(self, sem):
        self.sem, self.done, self.it, self.per, self.here = sem, 0, None, 0, 0

    def enter(self, it, per):
        self.it, self.per, self.here = it, per, 0

    def leave(self, trips):
        assert self.here == self.per, (self.here, self.per)
        self.done += self.per * trips
        self.it, self.per, self.here = None, 0, 0

    def next(self):
        if self.it is None:
            self.done += 1
            return self.done
        self.here += 1
        return At(self.done + self.here, self.it, self.per).value()


def program(nc, stream, xT, metaT, gains, consts, relh, sel, out):
    with ExitStack() as ctx:
        def sb(name, cols, dt=F32):
            return ctx.enter_context(nc.sbuf_tensor(name, [P, cols], dt))

        def sem(name):
            return ctx.enter_context(nc.semaphore(name))

        def sems(names):
            return [sem(name) for name in names.split()]

        raw = sb("raw", RING * UNIT)[:, :].rearrange("p (s n) -> p s n", s=RING)
        whi = sb("whi", RING * UNIT, F32R)[:, :].rearrange("p (s n) -> p s n", s=RING)
        wlo = sb("wlo", RING * UNIT, F32R)[:, :].rearrange("p (s n) -> p s n", s=RING)
        uhi = sb("uhi", DC * T, F32R)[:, :].rearrange("p (c t) -> p c t", t=T)
        ulo = sb("ulo", DC * T, F32R)[:, :].rearrange("p (c t) -> p c t", t=T)
        ahi_t = sb("ahi", FC2 * T, F32R)
        alo_t = sb("alo", FC2 * T, F32R)
        ahi = ahi_t[:, :].rearrange("p (c t) -> p c t", t=T)
        alo = alo_t[:, :].rearrange("p (c t) -> p c t", t=T)
        h = sb("h", DC * T)[:, :].rearrange("p (c t) -> p c t", t=T)
        g_t = sb("gain_columns", NG)
        c_t = sb("constants", NCONST)
        rstd = sb("rstd", 3 * T)[:, :].rearrange("p (c t) -> p c t", t=T)
        lg = sb("log_mean", T)
        acc = sb("sum_of_squares", T)
        bias = sb("bias_columns", 2)
        gains8 = sb("gains_over_8", 2)
        ones = sb("ones", 128)
        identb = sb("identb", 128, BF16)
        causalb = sb("causalb", 128, BF16)
        rowsb = sb("rowsb", 128 + 64 + 128, BF16)
        selmask = sb("selmask", 128 + 256 + T, BF16)
        wi = sb("wi", 3 * 8)
        SCR = 12208
        scr = sb("scratch", SCR)
        upperb, lateb, repb = rowsb[0:1, 0:128], rowsb[0:1, 128:192], rowsb[0:16, 192:320]

        def area(at, cols):
            assert at + cols <= SCR, (at, cols)
            return scr[:, at:at + cols]

        Q0, K0, V0 = 0, DC * T, 2 * DC * T
        q_all = area(Q0, DC * T).rearrange("p (c t) -> p c t", t=T)
        k_all = area(K0, DC * T).rearrange("p (c t) -> p c t", t=T)
        sq_all = q_all
        S0 = V0 + 3 * D
        prob = area(S0, 832).rearrange("p (b n) -> p b n", b=2)
        probT = area(S0 + 832, 768).rearrange("p (b n) -> p b n", b=2)
        probTA = area(S0 + 1600, 512).rearrange("p (b n) -> p b n", b=2)
        small = area(S0 + 2112, 64)
        yb = area(S0, 4 * T).rearrange("p (b t) -> p b t", b=4)
        y2 = area(S0 + 4 * T, 2 * T).rearrange("p (b t) -> p b t", b=2)
        ysq = area(S0 + 6 * T, 2 * T).rearrange("p (b t) -> p b t", b=2)
        E0 = S0 + 8 * T
        hr = area(E0 + 1760, 2 * T).rearrange("p (b t) -> p b t", b=2)
        relb = area(E0, 1024).rearrange("p (s b n) -> p s b n", s=2, b=2)
        selb = area(E0, 1024).bitcast(BF16).rearrange("p (h n) -> p h n", n=128)
        csplit = area(E0 + 1024, T // 2).bitcast(BF16)
        score = [area(E0, 128), area(E0 + 128, 256), area(E0 + 384, T)]
        best = area(E0 + 384 + T, 8)
        relu_t = area(E0 + 664, 2 * T).rearrange("p (b t) -> p b t", b=2)
        mc = area(E0 + 664 + 2 * T, 2 * T).rearrange("p (b t) -> p b t", b=2)
        relu = area(K0 + 4 * T, 768).rearrange("p (b n) -> p b n", b=2)
        gate, egate, tgate, mval = (
            area(K0 + 2 * T * i, 2 * T).rearrange("p (b t) -> p b t", b=2) for i in range(4))
        mq = area(8 * T, 8 * SEQ).rearrange("p (c t) -> p c t", t=SEQ)
        mk = area(8 * T + 8 * SEQ, 8 * SEQ).rearrange("p (c t) -> p c t", t=SEQ)
        sbq, sbk = q_all[:, 0:4, :], q_all[:, 4:8, :]
        L0 = 8 * T + 16 * SEQ
        zlog, nlk, ls = (area(L0 + 2048 + 768 * i, 768).rearrange("p (b n) -> p b n", b=2) for i in range(3))
        kro = area(L0 + 2048 + 2304, T)
        mprob = area(L0 + 2048 + 2304, 768).rearrange("p (b n) -> p b n", b=2)
        mprobT = area(L0 + 2048 + 2304 + 768, 768).rearrange("p (b n) -> p b n", b=2)
        msmall = area(L0 + 2048 + 2304 + 1536, 16)
        lyb = area(L0 + 2048, 4 * T).rearrange("p (b t) -> p b t", b=4)
        lat = area(8 * T, 5 * T).rearrange("p (b t) -> p b t", b=5)
        latsq = area(8 * T + 5 * T, 5 * T).rearrange("p (b t) -> p b t", b=5)

        def const(name):
            a, b = CCOL[name]
            return c_t[:, a:b]

        def gain(name, m=0):
            return g_t[:, GCOL[name] + m:GCOL[name] + m + 1]

        def chunk_at(first, at, cols):
            w = cols.stop - cols.start
            if at.it is None:
                return scr[:, first + at.c * T + cols.start:first + at.c * T + cols.stop]
            return scr[:, bass.ds(at.it * (at.m * T) + (first + at.c * T + cols.start), w)]

        def hidden_at(t, at, cols):
            w = cols.stop - cols.start
            if at.it is None:
                return t[:, at.c * T + cols.start:at.c * T + cols.stop]
            return t[:, bass.ds(at.it * (at.m * T) + (at.c * T + cols.start), w)]

        bank = [ctx.enter_context(nc.psum_tensor(f"bank{i}", [P, 512], F32)) for i in range(8)]
        STAT = 4

        gains_loaded, consts_loaded, meta_loaded = sems("gains_loaded consts_loaded meta_loaded")
        x_loaded = sems("x_loaded0 x_loaded1 x_loaded2 x_loaded3")
        consts_cast, bias_set, stored = sems("consts_cast bias_set stored")
        w_loaded = sems("w_loaded0 w_loaded1 w_loaded2 w_loaded3")
        w_hi, w_lo, w_used, evac = sems("w_hi w_lo w_used evacuated")
        u_hi, u_lo, squares, acc_done, stat_ready, rstd_ready = sems(
            "u_hi u_lo squares acc_done stat_ready rstd_ready")
        x2_ready, u2_hi, u2_lo = sems("x2_ready u2_hi u2_lo")
        e_ready, t_ready, a_hi, a_lo, a_sq = sems("e_ready t_ready a_hi a_lo a_sq")
        v_turned, v_stored = sems("v_turned v_stored")
        y_sq, y_stat, y_rstd, y_norm, y_rot, y_cos, y_done = sems(
            "y_sq y_stat y_rstd y_norm y_rot y_cos y_done")
        s_ready, s_max, p_exp, p_norm, pt_ready, pt_copied, o_ready, o_hi, o_lo = sems(
            "s_ready s_max p_exp p_norm pt_ready pt_copied o_ready o_hi o_lo")
        z_ready, z_log, z_split, z_masked, z_sum, z_arg, z_exp, z_w, z_o, z_ohi, z_olo = sems(
            "z_ready z_log z_split z_masked z_sum z_arg z_exp z_w z_o z_ohi z_olo")
        sel_loaded = sem("sel_loaded")
        rel_loaded = sems("rel_loaded0 rel_loaded1")
        lat_hi, lat_lo, lat_sq, lat_stat, lat_rstd, kr_rot, kr_done = sems(
            "lat_hi lat_lo lat_sq lat_stat lat_rstd kr_rot kr_done")
        m_q, m_rot, m_qdone, m_kv, m_turned, m_vstored, m_kdone = sems(
            "m_q m_rot m_qdone m_kv m_turned m_vstored m_kdone")
        wi_ready, wi_turned, wi_done, ix_ready, ix_relu, ix_acc, ix_mask = sems(
            "wi_ready wi_turned wi_done ix_ready ix_relu ix_acc ix_mask")
        f_exp, f_log, f_split = sems("f_exp f_log f_split")
        t_q, t_s, t_max, t_exp, t_p, t_pt, t_pts, t_o, t_ohi, t_olo = sems(
            "t_q t_s t_max t_exp t_p t_pt t_pts t_o t_ohi t_olo")
        out_turned, out_copied = sems("out_turned out_copied")
        dve_chain, act_chain = sems("dve_chain act_chain")

        FIRST, WHOLE = slice(META, T), slice(0, T)
        UIDX = {0: 0, 1: 1, 2: 2, 3: 3, 5: 4, 6: 5, 7: 6, 8: 7}

        def width(cols):
            return cols.stop - cols.start

        def split_hi(act, n):
            s = n.mod(RING)
            act.wait_ge(w_loaded[s], (n.div(RING) + 1).times(16).value())
            if (n + (1 - RING)).c > 0:
                act.wait_ge(w_used, (n + (1 - RING)).value())
            act.activation(whi[:, s, :], raw[:, s, :], ACT.Copy).then_inc(w_hi, 1)

        def split_lo(dve, n):
            s = n.mod(RING)
            dve.wait_ge(w_hi, (n + 1).value())
            dve.tensor_tensor(wlo[:, s, :], raw[:, s, :], whi[:, s, :].bitcast(F32),
                              ALU.subtract).then_inc(w_lo, 1)

        def unit_mm(pe, n, dst, xhi, xlo, cols, chunks=DC, at=0, first=True, last=True, x=None, used=True):
            s = n.mod(RING)
            pe.wait_ge(w_lo, (n + 1).value())
            for i in range(chunks):
                if x is not None:
                    ready, count = x(i)
                    pe.wait_ge(ready, count)
                hi, lo = (w[:, s, (at + i) * P:(at + i + 1) * P] for w in (whi, wlo))
                a, b = xhi[:, i, cols], xlo[:, i, cols]
                pe.matmul(dst, hi, a, start=first and i == 0, stop=False)
                pe.matmul(dst, hi, b, start=False, stop=False)
                mm = pe.matmul(dst, lo, a, start=False, stop=last and i == chunks - 1)
            if used:
                mm.then_inc(w_used, 1)

        def u_chunk(norm):
            return lambda i: (u_lo, 8 * UIDX[norm] + i + 1)

        def norm_act(act, k, m, cols, name):
            if name != "final":
                act.activation(uhi[:, m, cols], h[:, m, cols], ACT.Copy, scale=gain(name, m)).then_inc(u_hi, 1)
            if m == 0:
                if 7 * k > 0:
                    act.wait_ge(acc_done, 7 * k)
            act.activation(sq_all[:, m, cols], h[:, m, cols], ACT.Square).then_inc(squares, 1)

        def norm_dve(dve, k, m, cols, name):
            if name == "final":
                return
            dve.wait_ge(u_hi, 8 * UIDX[k] + m + 1)
            dve.scalar_tensor_tensor(out=ulo[:, m, cols], in0=h[:, m, cols], scalar=gain(name, m),
                                     in1=uhi[:, m, cols].bitcast(F32), op0=ALU.mult,
                                     op1=ALU.subtract).then_inc(u_lo, 1)

        def norm_pool(pool, k, cols):
            for m in range(1, DC):
                pool.wait_ge(squares, 8 * k + m + 1)
                if m == 1:
                    if k > 0:
                        pool.wait_ge(stat_ready, k)
                else:
                    pool.wait_ge(acc_done, 7 * k + m - 1)
                first = sq_all[:, 0, cols] if m == 1 else acc[:, cols]
                pool.tensor_tensor(acc[:, cols], first, sq_all[:, m, cols], ALU.add).then_inc(acc_done, 1)

        def norm_pe(pe, k, cols):
            pe.wait_ge(acc_done, 7 * (k + 1))
            if k > 0:
                pe.wait_ge(rstd_ready, k)
            pe.matmul(bank[STAT][:, 0:width(cols)], ones[:, :], acc[:, cols], start=True,
                      stop=True).then_inc(stat_ready, 1)

        def norm_rstd(act, link, k, cols):
            act.wait_ge(stat_ready, k + 1)
            if k > 0:
                act.wait_ge(rstd_ready, k)
            act.activation(lg[:, cols], bank[STAT][:, 0:width(cols)], ACT.Ln, scale=1.0 / D, bias=bias[:, 0:1]).then_inc(link.sem, 1)
            act.wait_ge(link.sem, link.next())
            act.activation(rstd[:, 0, cols], lg[:, cols], ACT.Exp, scale=-0.5).then_inc(rstd_ready, 1)

        def resid_pe(pe, name, kc, cols, x):
            per = -(-kc // DC)

            def group(it):
                n0, b0 = At(START[name], it, 4 * per), At(BSTART[name], it, 4)
                for j in range(4):
                    pe.wait_ge(evac, (b0 + (j - 3)).value())
                    dst = bank[(b0 + j).mod(4)][:, 0:width(cols)]
                    for u in range(per):
                        wait_x = it is None and j == 0
                        unit_mm(pe, n0 + (j * per + u), dst, ahi[:, u * DC:, :], alo[:, u * DC:, :], cols,
                                chunks=min(DC, kc - u * DC), first=u == 0, last=u == per - 1,
                                x=(lambda i, u=u: x(u * DC + i)) if wait_x else None)
            group(None)
            with pe.Fori(1, DC // 4) as it:
                group(it)

        def resid_act(act, link, name, kc, cols, norm, gname):
            per = -(-kc // DC)
            for m in range(DC + 1):
                for u in range(per if m < DC else 1):
                    if m < DC:
                        split_hi(act, At(START[name] + m * per + u + AHEAD))
                    if u == 0 and m > 0 and gname is not None:
                        act.wait_ge(evac, BSTART[name] + m)
                        norm_act(act, norm, m - 1, cols, gname)
            if norm is not None:
                norm_rstd(act, link, norm, cols)

        def resid_dve(dve, name, kc, cols, norm, gname):
            per = -(-kc // DC)
            for m in range(DC):
                for u in range(per):
                    split_lo(dve, At(START[name] + m * per + u + AHEAD))
                    if m > 0 and u == 0 and gname is not None:
                        norm_dve(dve, norm, m - 1, cols, gname)
                b = BSTART[name] + m
                dve.wait_ge(w_used, START[name] + (m + 1) * per)
                dve.tensor_tensor(h[:, m, cols], bank[b % 4][:, 0:width(cols)], h[:, m, cols],
                                  ALU.add).then_inc(evac, 1)
            if gname is not None:
                norm_dve(dve, norm, DC - 1, cols, gname)

        def hidden_pe(pe, name, cols, norm, groups):
            def group(it):
                n0, b0 = At(START[name], it, 4), At(BSTART[name], it, 4)
                for j in range(4):
                    pe.wait_ge(evac, (b0 + (j - 3)).value())
                    unit_mm(pe, n0 + j, bank[(b0 + j).mod(4)][:, 0:width(cols)], uhi, ulo, cols,
                            x=u_chunk(norm) if it is None and j == 0 else None)
                    if it is None and j == 0:
                        norm_pe(pe, norm, cols)
            group(None)
            with pe.Fori(1, groups) as it:
                group(it)

        def swiglu_pe(pe, name, cols, norm):
            hidden_pe(pe, name, cols, norm, FC1 // 2)

        def swiglu_act(act, link, name, cols):
            with act.Fori(0, FC1 // 2) as it:
                link.enter(it, 4)
                n0, b0 = At(START[name], it, 4), At(BSTART[name], it, 4)
                for j in range(2):
                    split_hi(act, n0 + (2 * j + AHEAD))
                    act.wait_ge(evac, (b0 + (2 * j + 1)).value())
                    e = egate[:, j, cols]
                    act.activation(e, gate[:, j, cols], ACT.Exp, scale=-1.0).then_inc(link.sem, 1)
                    act.wait_ge(link.sem, link.next())
                    act.activation(e, e, ACT.Ln, bias=bias[:, 1:2]).then_inc(link.sem, 1)
                    act.wait_ge(link.sem, link.next())
                    act.activation(e, e, ACT.Exp, scale=-1.0).then_inc(e_ready, 1)
                    split_hi(act, n0 + (2 * j + 1 + AHEAD))
                    act.wait_ge(evac, (b0 + (2 * j + 2)).value())
                    act.activation(hidden_at(ahi_t, At(j, it, 2), cols), mval[:, j, cols], ACT.Copy).then_inc(a_hi, 1)
                link.leave(FC1 // 2)

        def swiglu_dve(dve, name, cols, norm, i0):
            dve.wait_ge(rstd_ready, norm + 1)
            with dve.Fori(0, FC1 // 2) as it:
                n0, b0 = At(START[name], it, 4), At(BSTART[name], it, 4)
                for j in range(2):
                    i = At(i0 + j, it, 2)
                    dve.wait_ge(w_used, (n0 + (2 * j + 1)).value())
                    dve.tensor_tensor(gate[:, j, cols], bank[(b0 + 2 * j).mod(4)][:, 0:width(cols)],
                                      rstd[:, 0, cols], ALU.mult).then_inc(evac, 1)
                    split_lo(dve, n0 + (2 * j + AHEAD))
                    split_lo(dve, n0 + (2 * j + 1 + AHEAD))
                    dve.wait_ge(w_used, (n0 + (2 * j + 2)).value())
                    dve.wait_ge(t_ready, (i + 1).times(2).value())
                    dve.tensor_tensor(mval[:, j, cols], bank[(b0 + 2 * j + 1).mod(4)][:, 0:width(cols)],
                                      tgate[:, j, cols], ALU.mult).then_inc(evac, 1)

        def swiglu_pool(pool, name, cols, norm, i0):
            pool.wait_ge(rstd_ready, norm + 1)
            with pool.Fori(0, FC1 // 2) as it:
                for j in range(2):
                    i = At(i0 + j, it, 2)
                    pool.wait_ge(e_ready, (i + 1).value())
                    pool.tensor_tensor(tgate[:, j, cols], gate[:, j, cols], egate[:, j, cols], ALU.mult).then_inc(t_ready, 1)
                    pool.wait_ge(t_ready, (i.times(2) + 1).value())
                    pool.tensor_tensor(tgate[:, j, cols], tgate[:, j, cols], rstd[:, 0, cols], ALU.mult).then_inc(t_ready, 1)
                    pool.wait_ge(a_hi, (i + 1).value())
                    pool.tensor_tensor(hidden_at(alo_t, At(j, it, 2), cols), mval[:, j, cols],
                                       hidden_at(ahi_t, At(j, it, 2), cols).bitcast(F32), ALU.subtract).then_inc(a_lo, 1)

        def sqrelu_pe(pe, name, cols, norm):
            hidden_pe(pe, name, cols, norm, FC2 // 4)

        def sqrelu_act(act, name, cols):
            with act.Fori(0, FC2 // 4) as it:
                n0, b0 = At(START[name], it, 4), At(BSTART[name], it, 4)
                for j in range(4):
                    split_hi(act, n0 + (j + AHEAD))
                    act.wait_ge(evac, (b0 + (j + 1)).value())
                    act.activation(hidden_at(ahi_t, At(j, it, 4), cols), gate[:, j % 2, cols], ACT.Square).then_inc(a_hi, 1)

        def sqrelu_dve(dve, name, cols, norm, i0):
            dve.wait_ge(rstd_ready, norm + 1)
            with dve.Fori(0, FC2 // 4) as it:
                n0, b0 = At(START[name], it, 4), At(BSTART[name], it, 4)
                for j in range(4):
                    i = At(i0 + j, it, 4)
                    dve.wait_ge(w_used, (n0 + (j + 1)).value())
                    dve.wait_ge(a_lo, (i + (-1)).value())
                    dve.scalar_tensor_tensor(out=gate[:, j % 2, cols], in0=bank[(b0 + j).mod(4)][:, 0:width(cols)],
                                             scalar=0.0, in1=rstd[:, 0, cols], op0=ALU.max,
                                             op1=ALU.mult).then_inc(evac, 1)
                    split_lo(dve, n0 + (j + AHEAD))

        def sqrelu_pool(pool, name, cols, i0, k0):
            with pool.Fori(0, FC2 // 4) as it:
                b0 = At(BSTART[name], it, 4)
                for j in range(4):
                    i, k = At(i0 + j, it, 4), At(k0 + j, it, 4)
                    pool.wait_ge(evac, (b0 + (j + 1)).value())
                    pool.tensor_tensor(mval[:, j % 2, cols], gate[:, j % 2, cols], gate[:, j % 2, cols],
                                       ALU.mult).then_inc(a_sq, 1)
                    pool.wait_ge(a_sq, (k + 1).value())
                    pool.wait_ge(a_hi, (i + 1).value())
                    pool.tensor_tensor(hidden_at(alo_t, At(j, it, 4), cols), mval[:, j % 2, cols],
                                       hidden_at(ahi_t, At(j, it, 4), cols).bitcast(F32), ALU.subtract).then_inc(a_lo, 1)


        VFIRST = {"sv": 0, "bv": 4, "dv": 12, "fv": 14}
        RFIRST = {"dk": 0, "dq": 4, "fk": 12, "fq": 20}
        OFIRST = {"ki": 0, "qi": 1, "dk": 5, "dq": 9, "fk": 17, "fq": 25}
        VTILES = {"sv": (META, META + 128, None), "bv": (META, META + 128, None), "dv": (0, 128, 256), "fv": (META, META + 128, 0)}
        COUNT = dict(PHASES)

        def in_groups(eng, name, kind, body):
            n = COUNT[name]
            if kind != "plain" or n <= 4:
                body(At(0), n, None, 1)
            else:
                with eng.Fori(0, n // 4) as it:
                    body(At(0, it, 4), 4, it, n // 4)

        def proj_pe(pe, name, kind, cols, norm, second=False, sum_norm=None):
            xhi, xlo = (ahi[:, DC:, :], alo[:, DC:, :]) if second else (uhi, ulo)
            ready = (lambda i: (u2_lo, i + 1)) if second else u_chunk(norm)
            vy = lyb if name == "sv" else yb
            n_cols = width(cols)

            def body(g, k, it, trips):
                def turn(j):
                    v = g + (VFIRST[name] + j)
                    pe.wait_ge(evac, (g + (BSTART[name] + j + 1)).value())
                    if (v + (-1)).c > 0:
                        pe.wait_ge(v_stored, (v + (-1)).value())
                    t0, t1, ta = VTILES[name]
                    dst = bank[5 + j % 2]
                    if ta is not None:
                        pe.transpose(dst[0:META, 256:384], vy[:, j % 4, ta:ta + META], const("ident"))
                    pe.transpose(dst[:, 0:128], vy[:, j % 4, t0:t0 + 128], const("ident"))
                    pe.transpose(dst[:, 128:256], vy[:, j % 4, t1:t1 + 128], const("ident")).then_inc(v_turned, 1)

                def stat(j):
                    r = g + (RFIRST[name] + j)
                    pe.wait_ge(y_sq, (r + 1).value())
                    if (r + (-1)).c > 0:
                        pe.wait_ge(y_rstd, (r + (-1)).value())
                    pe.matmul(bank[5 + j % 2][:, 0:n_cols], const("headones"), ysq[:, j % 2, cols],
                              start=True, stop=True).then_inc(y_stat, 1)

                def rot(j):
                    o = g + (OFIRST[name] + j)
                    if kind == "rope":
                        pe.wait_ge(evac, (g + (BSTART[name] + j + 1)).value())
                    else:
                        pe.wait_ge(y_norm, (g + (RFIRST[name] + j + 1)).value())
                    if o.c > 0:
                        pe.wait_ge(y_done, o.value())
                    src = yb[:, (OFIRST[name] + j) % 4, cols] if kind == "rope" else y2[:, j % 2, cols]
                    pe.matmul(bank[7][:, 0:n_cols], const("rot"), src, start=True, stop=True).then_inc(y_rot, 1)

                for j in range(k):
                    b = g + (BSTART[name] + j)
                    pe.wait_ge(evac, (b + (-3)).value())
                    unit_mm(pe, g + (START[name] + j), bank[b.mod(4)][:, 0:n_cols], xhi, xlo, cols,
                            x=ready if j == 0 else None)
                    if sum_norm is not None and it is None and j == 0:
                        norm_pe(pe, sum_norm, cols)
                    if kind == "v" and j >= 1:
                        turn(j - 1)
                    if "rms" in kind and j >= 1:
                        stat(j - 1)
                    if "rope" in kind and j >= 2:
                        rot(j - 2)
                if kind == "v":
                    turn(k - 1)
                if "rms" in kind:
                    stat(k - 1)
                if "rope" in kind:
                    for j in range(max(0, k - 2), k):
                        rot(j)
            in_groups(pe, name, kind, body)

        def proj_act(act, link, name, kind, cols):
            n_cols = width(cols)

            def body(g, k, it, trips):
                def rms(j):
                    act.wait_ge(y_stat, (g + (RFIRST[name] + j + 1)).value())
                    if kind == "rms":
                        act.wait_ge(y_done, (g + (OFIRST[name] + j - 1)).value())
                    else:
                        if (g + (RFIRST[name] + j - 1)).c > 0:
                            act.wait_ge(y_norm, (g + (RFIRST[name] + j - 1)).value())
                    if (g + (RFIRST[name] + j)).c > 0:
                        act.wait_ge(y_rstd, (g + (RFIRST[name] + j)).value())
                    act.activation(lg[:, cols], bank[5 + j % 2][:, 0:n_cols], ACT.Ln, scale=1.0 / HD, bias=bias[:, 0:1]).then_inc(link.sem, 1)
                    act.wait_ge(link.sem, link.next())
                    act.activation(hr[:, j % 2, cols], lg[:, cols], ACT.Exp, scale=-0.5).then_inc(y_rstd, 1)

                def store_v(j):
                    act.wait_ge(v_turned, (g + (VFIRST[name] + j + 1)).value())
                    if VTILES[name][2] is not None:
                        act.activation(v_cols(g + j, 256, 128, META), bank[5 + j % 2][0:META, 256:384], ACT.Copy).then_inc(link.sem, 1)
                        act.wait_ge(link.sem, link.next())
                    dst = v_cols(g + j, 0, 256, P) if name != "sv" else mv_cols(g + j)
                    act.activation(dst, bank[5 + j % 2][:, 0:256], ACT.Copy).then_inc(v_stored, 1)

                for j in range(k):
                    split_hi(act, g + (START[name] + j + AHEAD))
                    if "rms" in kind:
                        act.wait_ge(evac, (g + (BSTART[name] + j + 1)).value())
                        if (g + (RFIRST[name] + j - 1)).c > 0:
                            act.wait_ge(y_stat, (g + (RFIRST[name] + j - 1)).value())
                        act.activation(ysq[:, j % 2, cols], yb[:, j % 4, cols], ACT.Square).then_inc(y_sq, 1)
                        if j >= 1:
                            rms(j - 1)
                    if kind == "v" and j >= 1:
                        store_v(j - 1)
                if "rms" in kind:
                    rms(k - 1)
                if kind == "v":
                    store_v(k - 1)
            in_groups(act, name, kind, body)

        def v_cols(at, off, w, rows):
            if at.it is None:
                return scr[0:rows, V0 + at.c * 384 + off:V0 + at.c * 384 + off + w]
            return scr[0:rows, bass.ds(at.it * (at.m * 384) + (V0 + at.c * 384 + off), w)]

        def mv_cols(at):
            return scr[:, L0 + at.c * 256:L0 + at.c * 256 + 256]

        def proj_dve(dve, link, name, kind, cols, first=None, scale=1.0, gcol=None, norm=0, between=None):
            n_cols = width(cols)
            vy = lyb if name == "sv" else yb
            dve.wait_ge(rstd_ready, norm + 1)

            def body(g, k, it, trips):
                def normed(j):
                    r = g + (RFIRST[name] + j)
                    dve.wait_ge(y_rstd, (r + 1).value())
                    if kind == "rms":
                        dst, done = chunk_at(first, g + j, cols), y_done
                    else:
                        dst, done = y2[:, j % 2, cols], y_norm
                        dve.wait_ge(y_rot, (g + (OFIRST[name] + j - 1)).value())
                        dve.wait_ge(y_cos, (g + (OFIRST[name] + j - 1)).value())
                    dve.scalar_tensor_tensor(out=dst, in0=yb[:, j % 4, cols], scalar=gcol, in1=hr[:, j % 2, cols],
                                             op0=ALU.mult, op1=ALU.mult).then_inc(done, 1)

                def rotated(j):
                    o = g + (OFIRST[name] + j)
                    dst = chunk_at(first, g + j, cols)
                    dve.wait_ge(y_rot, (o + 1).value())
                    dve.tensor_tensor(dst, bank[7][:, 0:n_cols], const("sin")[:, cols], ALU.mult).then_inc(link.sem, 1)
                    dve.wait_ge(link.sem, link.next())
                    dve.wait_ge(y_cos, (o + 1).value())
                    dve.tensor_tensor(dst, dst, mc[:, (OFIRST[name] + j) % 2, cols], ALU.add).then_inc(y_done, 1)

                for j in range(k):
                    b = g + (BSTART[name] + j)
                    dve.wait_ge(w_used, (g + (START[name] + j + 1)).value())
                    src = bank[b.mod(4)][:, 0:n_cols]
                    if kind == "plain":
                        dve.scalar_tensor_tensor(out=chunk_at(first, g + j, cols), in0=src, scalar=scale, in1=rstd[:, 0, cols],
                                                 op0=ALU.mult, op1=ALU.mult).then_inc(evac, 1)
                        split_lo(dve, g + (START[name] + j + AHEAD))
                        continue
                    if kind == "v":
                        if (g + (VFIRST[name] + j - 3)).c > 0:
                            dve.wait_ge(v_turned, (g + (VFIRST[name] + j - 3)).value())
                        dst = vy[:, j % 4, cols]
                    elif kind == "rope":
                        if (g + (OFIRST[name] + j - 3)).c > 0:
                            dve.wait_ge(y_rot, (g + (OFIRST[name] + j - 3)).value())
                        if (g + (OFIRST[name] + j - 3)).c > 0:
                            dve.wait_ge(y_cos, (g + (OFIRST[name] + j - 3)).value())
                        dst = yb[:, (OFIRST[name] + j) % 4, cols]
                    else:
                        if (g + (RFIRST[name] + j - 3)).c > 0:
                            dve.wait_ge(y_sq, (g + (RFIRST[name] + j - 3)).value())
                        dst = yb[:, j % 4, cols]
                    dve.tensor_tensor(dst, src, rstd[:, 0, cols], ALU.mult).then_inc(evac, 1)
                    split_lo(dve, g + (START[name] + j + AHEAD))
                    if "rms" in kind and j >= 1:
                        normed(j - 1)
                    if "rope" in kind and j >= 2:
                        rotated(j - 2)
                    if between is not None:
                        between(g.c + j)
                if "rms" in kind:
                    normed(k - 1)
                if "rope" in kind:
                    for j in range(max(0, k - 2), k):
                        rotated(j)
            in_groups(dve, name, kind, body)

        def proj_pool(pool, name, kind, cols):
            def body(g, k, it, trips):
                for j in range(k):
                    o = g + (OFIRST[name] + j)
                    oo = OFIRST[name] + j
                    if kind == "rope":
                        pool.wait_ge(evac, (g + (BSTART[name] + j + 1)).value())
                    else:
                        pool.wait_ge(y_norm, (g + (RFIRST[name] + j + 1)).value())
                    if (o + (-1)).c > 0:
                        pool.wait_ge(y_done, (o + (-1)).value())
                    src = yb[:, oo % 4, cols] if kind == "rope" else y2[:, j % 2, cols]
                    pool.tensor_tensor(mc[:, oo % 2, cols], src, const("cos")[:, cols], ALU.mult).then_inc(y_cos, 1)
            in_groups(pool, name, kind, body)

        class Heads:
            def __init__(self, name, head0, pairs, pre, q, k, v, va, add, chunk0, cols, p, pt, sm, obanks=2):
                self.name, self.head0, self.pairs, self.pre = name, head0, pairs, pre
                self.q, self.k, self.v, self.va, self.add = q, k, v, va, add
                self.chunk0, self.cols, self.p, self.pt, self.obanks = chunk0, cols, p, pt, obanks
                self.nmx = sm[:, 0:4].rearrange("p (b n) -> p b n", b=2)
                self.ssum = sm[:, 4:8].rearrange("p (b n) -> p b n", b=2)
                self.rinv = sm[:, 8:12].rearrange("p (b n) -> p b n", b=2)
                self.w0, self.w1 = pre + 128, pre + 256

        def scores_pe(pe, a, i):
            hd, s = a.head0 + i, bank[4 + i % 2]
            if 2 * (hd - 1) > 0:
                pe.wait_ge(p_exp, 2 * (hd - 1))
            q, k = a.q(i), a.k(i)
            more = a.add is not None
            pe.matmul(s[:, 0:a.w0], q[:, 0:128], k[:, 0:a.w0], start=True, stop=not more, skip_group_check=True)
            mm = pe.matmul(s[:, a.w0:a.w0 + a.w1], q[:, 128:256], k[:, 0:a.w1], start=not more, stop=not more, skip_group_check=True)
            if more:
                mm = a.add(pe, i, s)
            mm.then_inc(s_ready, 1)

        def turn_pe(pe, a, i):
            hd, p, dst = a.head0 + i, a.p[:, i % 2, :], bank[6 + i % 2]
            pe.wait_ge(p_norm, 2 * (hd + 1))
            if hd - 1 > 0:
                pe.wait_ge(pt_copied, hd - 1)
            idn = const("ident")
            c0, c1 = a.pre, a.w0 + a.pre
            if a.pre:
                pe.transpose(bank[2 + i % 2][0:a.pre, 0:128], p[:, 0:a.pre], idn)
                pe.transpose(bank[2 + i % 2][0:a.pre, 128:256], p[:, a.w0:a.w0 + a.pre], idn)
            pe.transpose(dst[:, 0:128], p[:, c0:c0 + 128], idn)
            pe.transpose(dst[:, 128:256], p[:, c1:c1 + 128], idn)
            pe.transpose(dst[:, 256:384], p[:, c1 + 128:c1 + 256], idn).then_inc(pt_ready, 1)

        def values_pe(pe, a, s):
            pr = a.head0 // 2 + s
            o = bank[pr % a.obanks]
            if pr + 1 - a.obanks > 0:
                pe.wait_ge(o_lo, pr + 1 - a.obanks)
            for i in (2 * s, 2 * s + 1):
                pe.wait_ge(pt_copied, a.head0 + i + 1)
                dst, pt = o[64 * (i % 2):64 * (i % 2) + 64, :], a.pt[:, i % 2, :]
                if a.pre:
                    pe.matmul(dst[:, 0:256], a.va(i), probTA[0:META, i % 2, :], start=True, stop=False, skip_group_check=True)
                pe.matmul(dst[:, 0:256], a.v(i, 0), pt[:, 0:256], start=not a.pre, stop=False, skip_group_check=True)
                mm = pe.matmul(dst[:, 128:256], a.v(i, 1), pt[:, 256:384], start=False, stop=True, skip_group_check=True)
            mm.then_inc(o_ready, 1)

        def att_pe(pe, a, hook=None):
            for s in range(a.pairs + 2):
                if hook:
                    hook(0, s)
                for i in (2 * s, 2 * s + 1):
                    if s < a.pairs:
                        scores_pe(pe, a, i)
                    if s >= 2 and i % 2 == 0:
                        values_pe(pe, a, s - 2)
                    if 1 <= s <= a.pairs:
                        turn_pe(pe, a, i - 2)
                if hook:
                    hook(1, s)

        def att_act(act, link, a, hook=None):
            for s in range(a.pairs + 2):
                if hook:
                    hook(0, s)
                if s >= 2:
                    pr = a.head0 // 2 + s - 2
                    act.wait_ge(o_ready, pr + 1)
                    act.activation(ahi[:, a.chunk0 + s - 2, a.cols], bank[pr % a.obanks][:, 0:256], ACT.Copy).then_inc(o_hi, 1)
                for i in (2 * s, 2 * s + 1):
                    if s < a.pairs:
                        hd, sc = a.head0 + i, bank[4 + i % 2]
                        act.wait_ge(s_max, 2 * (hd + 1))
                        if hd - 1 > 0:
                            act.wait_ge(pt_ready, hd - 1)
                        for t, (c0, w) in enumerate(((0, a.w0), (a.w0, a.w1))):
                            act.activation(a.p[:, i % 2, c0:c0 + w], sc[:, c0:c0 + w], ACT.Exp, bias=a.nmx[:, i % 2, t:t + 1],
                                           accum_out=a.ssum[:, i % 2, t:t + 1]).then_inc(p_exp, 1)
                    if 1 <= s <= a.pairs:
                        hd = a.head0 + i - 2
                        act.wait_ge(pt_ready, hd + 1)
                        if a.head0 // 2 + s - 1 > 0:
                            act.wait_ge(o_ready, a.head0 // 2 + s - 1)
                        if a.pre:
                            act.activation(probTA[0:a.pre, i % 2, :], bank[2 + i % 2][0:a.pre, 0:256], ACT.Copy).then_inc(link.sem, 1)
                            act.wait_ge(link.sem, link.next())
                        act.activation(a.pt[:, i % 2, 0:384], bank[6 + i % 2][:, 0:384], ACT.Copy).then_inc(pt_copied, 1)
                if hook:
                    hook(1, s)

        def att_dve(dve, link, a, hook=None):
            for s in range(a.pairs + 2):
                if hook:
                    hook(0, s)
                for i in (2 * s, 2 * s + 1):
                    if s < a.pairs:
                        sc = bank[4 + i % 2]
                        dve.wait_ge(s_ready, a.head0 + i + 1)
                        for t, (c0, w) in enumerate(((0, a.w0), (a.w0, a.w1))):
                            dve.tensor_reduce(a.nmx[:, i % 2, t:t + 1], sc[:, c0:c0 + w], AX.X, ALU.max,
                                              negate=True).then_inc(s_max, 1)
                    if s >= 2 and i % 2 == 0:
                        out_lo(dve, a, s - 2)
                if s < a.pairs:
                    for i in (2 * s, 2 * s + 1):
                        dve.wait_ge(p_exp, 2 * (a.head0 + i + 1))
                        dve.reciprocal(a.rinv[:, i % 2, :], a.ssum[:, i % 2, :]).then_inc(link.sem, 1)
                        dve.wait_ge(link.sem, link.next())
                        for t, (c0, w) in enumerate(((0, a.w0), (a.w0, a.w1))):
                            p = a.p[:, i % 2, c0:c0 + w]
                            dve.tensor_scalar(p, p, a.rinv[:, i % 2, t:t + 1], None, ALU.mult).then_inc(p_norm, 1)
                if hook:
                    hook(1, s)

        def out_lo(dve, a, s):
            pr = a.head0 // 2 + s
            dve.wait_ge(o_hi, pr + 1)
            dst = a.chunk0 + s
            dve.tensor_tensor(alo[:, dst, a.cols], bank[pr % a.obanks][:, 0:256], ahi[:, dst, a.cols].bitcast(F32),
                              ALU.subtract).then_inc(o_lo, 1)

        def half(ap, i):
            return ap[64 * (i % 2):64 * (i % 2) + 64]

        def v_of(i, tile, rows=P):
            c = V0 + (i // 2) * 384 + tile * 128 + 64 * (i % 2)
            return scr[0:rows, c:c + 64]

        def late_mask(pe, s):
            pe.matmul(s[:, 64:128], upperb, lateb, start=False, stop=True, skip_group_check=True)
            return pe.matmul(s[:, 128 + 192:128 + 256], upperb, lateb, start=False, stop=True, skip_group_check=True)

        def band_add(pe, i, s):
            pe.wait_ge(rel_loaded[i // 2 % 2], 16 * (i // 4 + 1))
            b, rev = relb[:, (i // 2) % 2, i % 2, :], const("rev")
            pe.matmul(s[:, 0:128], b[:, 0:128], rev, start=False, stop=False, skip_group_check=True)
            pe.matmul(s[:, 128:256], b[:, 128:256], rev, start=False, stop=False, skip_group_check=True)
            pe.matmul(s[:, 256:384], b[:, 0:128], rev, start=False, stop=False, skip_group_check=True)
            return late_mask(pe, s)

        def fox_add(pe, i, s):
            pe.matmul(s[:, 0:144], selb[0:96, i, :], csplit[0:96, 0:144], start=False, stop=False, skip_group_check=True)
            pe.matmul(s[:, 144:416], selb[0:96, i, :], csplit[0:96, 0:272], start=False, stop=False, skip_group_check=True)
            pe.matmul(s[:, 16:144], identb[:, :], causalb[:, :], start=False, stop=True, skip_group_check=True)
            return pe.matmul(s[:, 144 + 144:416], identb[:, :], causalb[:, :], start=False, stop=True, skip_group_check=True)

        def dsa_add(pe, i, s):
            pe.matmul(s[:, 0:128], identb[:, :], selmask[:, 0:128], start=False, stop=True, skip_group_check=True)
            return pe.matmul(s[:, 128:384], identb[:, :], selmask[:, 128:384], start=False, stop=True, skip_group_check=True)

        mla = Heads("mla", 0, 4, 0, lambda i: mq[0:96, i, :], lambda i: mk[0:96, i, :],
                    lambda i, t: scr[:, L0 + (4 + i // 2) * 256 + t * 128 + 64 * (i % 2):][:, 0:64], None,
                    lambda pe, i, s: late_mask(pe, s), 0, FIRST, mprob, mprobT, msmall, obanks=1)
        band = Heads("band", 8, 8, 0, lambda i: half(q_all[:, i // 2, FIRST], i), lambda i: half(k_all[:, i // 2, FIRST], i),
                     v_of, None, band_add, 0, FIRST, prob, probT, small)
        dsa = Heads("dsa", 24, 8, 0, lambda i: half(q_all[:, i // 2, 0:256], i), lambda i: half(k_all[:, i // 4, 0:256], i),
                    lambda i, t: scr[:, V0 + (i // 8) * 384 + t * 128 + 64 * ((i // 4) % 2):][:, 0:64], None,
                    dsa_add, 0, slice(0, 256), prob, probT, small, obanks=1)
        fox = Heads("fox", 40, 8, META, lambda i: half(q_all[:, i // 2, FIRST], i), lambda i: half(k_all[:, i // 2, WHOLE], i),
                    v_of, lambda i: v_of(i, 2, META), fox_add, 0, FIRST, prob, probT, small)

        SCALE_A = (NOPE + ROPE) ** -0.5

        def first_pe(pe):
            for i in range(QC + KVC + 1):
                if i - 3 > 0:
                    pe.wait_ge(evac, i - 3)
                unit_mm(pe, At(i), bank[i % 4][:, 0:SEQ], uhi, ulo, FIRST, x=u_chunk(0) if i == 0 else None)
                if i == 0:
                    norm_pe(pe, 0, FIRST)
            pe.wait_ge(consts_loaded, 16)
            for s, (a, k) in enumerate(((0, QC), (QC, KVC))):
                pe.wait_ge(lat_sq, a + k)
                for i in range(k):
                    mm = pe.matmul(bank[5 + s][:, 0:SEQ], ones[:, :], latsq[:, a + i, FIRST], start=i == 0, stop=i == k - 1)
                mm.then_inc(lat_stat, 1)
            pe.wait_ge(evac, BSTART["kr"] + 1)
            pe.matmul(bank[7][:, 0:SEQ], const("rotm"), lyb[:, 0, FIRST], start=True, stop=True).then_inc(kr_rot, 1)
            pe.wait_ge(lat_rstd, 2)
            pe.wait_ge(kr_done, 1)
            proj_pe(pe, "sv", "v", FIRST, 0)
            proj_pe(pe, "sq", "plain", FIRST, 0)
            proj_pe(pe, "sk", "plain", FIRST, 0)
            pe.wait_ge(v_stored, 4)
            pe.wait_ge(lat_lo, QC + KVC)

            def turn_and_rotate(i):
                b = BSTART["mla"] + 2 * i
                pe.wait_ge(evac, b + 1)
                if i > 0:
                    pe.wait_ge(m_qdone, i)
                pe.matmul(bank[7][:, 0:SEQ], const("rotm"), mq[:, i, :], start=True, stop=True).then_inc(m_rot, 1)
                pe.wait_ge(evac, b + 2)
                if i - 1 > 0:
                    pe.wait_ge(m_vstored, i - 1)
                for t in range(2):
                    mm = pe.transpose(bank[5 + i % 2][:, 64 * t:64 * t + 64], mk[64:128, i, 128 * t:128 * t + 128],
                                      const("ident")[64:128, 64:128])
                mm.then_inc(m_turned, 1)

            for i in range(8):
                b, n = BSTART["mla"] + 2 * i, At(START["mla"] + i)
                pe.wait_ge(evac, b - 2)
                unit_mm(pe, n, bank[b % 4][:, 0:SEQ], ahi[:, 16:, :], alo[:, 16:, :], FIRST, chunks=QC, used=False)
                unit_mm(pe, n, bank[(b + 1) % 4][:, 0:SEQ], ahi[:, 16 + QC:, :], alo[:, 16 + QC:, :], FIRST, chunks=KVC, at=QC)
                if i:
                    turn_and_rotate(i - 1)
            turn_and_rotate(7)

        def first_act(act, link):
            act.wait_ge(gains_loaded, 16)
            act.wait_ge(bias_set, 3)
            for m in range(DC):
                if m % 2 == 0:
                    act.wait_ge(x_loaded[m // 2], 16)
                if m >= 5:
                    split_hi(act, At(m - 5))
                norm_act(act, 0, m, FIRST, "mix0")
            norm_rstd(act, link, 0, FIRST)
            for i in range(QC + KVC + 1):
                split_hi(act, At(i + AHEAD))
                if i < QC + KVC:
                    act.wait_ge(evac, i + 1)
                    act.activation(latsq[:, i, FIRST], lat[:, i, FIRST], ACT.Square).then_inc(lat_sq, 1)
                    g = gain("cq", i) if i < QC else gain("ckv", i - QC)
                    act.activation(ahi[:, 16 + i, FIRST], lat[:, i, FIRST], ACT.Copy, scale=g).then_inc(lat_hi, 1)
            for s, w in enumerate((QL, KVL)):
                act.wait_ge(lat_stat, s + 1)
                act.wait_ge(rstd_ready, 1)
                if s > 0:
                    act.wait_ge(lat_rstd, s)
                act.activation(lg[:, FIRST], bank[5 + s][:, 0:SEQ], ACT.Ln, scale=1.0 / w, bias=bias[:, 0:1]).then_inc(link.sem, 1)
                act.wait_ge(link.sem, link.next())
                act.activation(rstd[:, 1 + s, FIRST], lg[:, FIRST], ACT.Exp, scale=-0.5).then_inc(lat_rstd, 1)
            proj_act(act, link, "sv", "v", FIRST)
            proj_act(act, link, "sq", "plain", FIRST)
            proj_act(act, link, "sk", "plain", FIRST)

            def store(i):
                act.wait_ge(m_turned, i + 1)
                c = L0 + (4 + i // 2) * 256 + 64 * (i % 2)
                for t in range(2):
                    ins = act.activation(scr[:, c + 128 * t:c + 128 * t + 64], bank[5 + i % 2][:, 64 * t:64 * t + 64], ACT.Copy)
                ins.then_inc(m_vstored, 1)
                act.wait_ge(kr_done, 1)
                act.activation(mk[64:96, i, :], kro[64:96, FIRST], ACT.Copy).then_inc(m_kdone, 1)

            for i in range(8):
                split_hi(act, At(START["mla"] + i + AHEAD))
                if i:
                    store(i - 1)
            store(7)

        def first_dve(dve, link):
            for m in range(DC):
                norm_dve(dve, 0, m, FIRST, "mix0")
                if m >= DC - AHEAD:
                    split_lo(dve, At(m - (DC - AHEAD)))
            dve.tensor_scalar(gains8[:, 0:1], gain("aq"), HD ** -0.5, None, ALU.mult).then_inc(consts_cast, 1)
            dve.tensor_scalar(gains8[:, 1:2], gain("bq"), HD ** -0.5, None, ALU.mult).then_inc(consts_cast, 1)

            def latent_lo(i):
                g = gain("cq", i) if i < QC else gain("ckv", i - QC)
                dve.wait_ge(lat_hi, i + 1)
                dve.scalar_tensor_tensor(out=alo[:, 16 + i, FIRST], in0=lat[:, i, FIRST], scalar=g,
                                         in1=ahi[:, 16 + i, FIRST].bitcast(F32), op0=ALU.mult, op1=ALU.subtract).then_inc(lat_lo, 1)

            dve.wait_ge(rstd_ready, 1)
            for i in range(QC + KVC + 1):
                dve.wait_ge(w_used, i + 1)
                dst = lat[:, i, FIRST] if i < QC + KVC else lyb[:, 0, FIRST]
                dve.tensor_tensor(dst, bank[i % 4][:, 0:SEQ], rstd[:, 0, FIRST], ALU.mult).then_inc(evac, 1)
                split_lo(dve, At(i + AHEAD))
                if i:
                    latent_lo(i - 1)
            dve.wait_ge(consts_loaded, 16)
            for dst, name in ((identb[:, :], "ident"), (causalb[:, :], "causal")):
                dve.tensor_copy(dst, const(name)).then_inc(consts_cast, 1)
            dve.tensor_copy(rowsb[:, :], c_t[:, CCOL["upper"][0]:CCOL["rep"][1]]).then_inc(consts_cast, 1)
            dve.wait_ge(kr_rot, 1)
            dve.tensor_tensor(kro[64:96, FIRST], bank[7][64:96, 0:SEQ], const("sinm")[64:96, :], ALU.mult).then_inc(link.sem, 1)
            dve.wait_ge(link.sem, link.next())
            dve.tensor_tensor(lyb[64:96, 1, FIRST], lyb[64:96, 0, FIRST], const("cosm")[64:96, :], ALU.mult).then_inc(link.sem, 1)
            dve.wait_ge(link.sem, link.next())
            dve.tensor_tensor(kro[64:96, FIRST], kro[64:96, FIRST], lyb[64:96, 1, FIRST], ALU.add).then_inc(kr_done, 1)
            proj_dve(dve, link, "sv", "v", FIRST)
            proj_dve(dve, link, "sq", "plain", FIRST, first=0, scale=HD ** -0.5)
            proj_dve(dve, link, "sk", "plain", FIRST, first=4 * T)

            def rotate(i):
                dve.wait_ge(m_rot, i + 1)
                dve.tensor_tensor(lyb[64:96, 0, FIRST], mq[64:96, i, :], const("cosm")[64:96, :], ALU.mult).then_inc(link.sem, 1)
                dve.wait_ge(link.sem, link.next())
                dve.tensor_tensor(mq[64:96, i, :], bank[7][64:96, 0:SEQ], const("sinm")[64:96, :], ALU.mult).then_inc(link.sem, 1)
                dve.wait_ge(link.sem, link.next())
                dve.tensor_tensor(mq[64:96, i, :], mq[64:96, i, :], lyb[64:96, 0, FIRST], ALU.add).then_inc(m_qdone, 1)

            dve.wait_ge(lat_rstd, 2)
            for i in range(8):
                n, b = START["mla"] + i, BSTART["mla"] + 2 * i
                dve.wait_ge(w_used, n + 1)
                dve.scalar_tensor_tensor(out=mq[:, i, :], in0=bank[b % 4][:, 0:SEQ], scalar=SCALE_A, in1=rstd[:, 1, FIRST],
                                         op0=ALU.mult, op1=ALU.mult).then_inc(evac, 1)
                dve.tensor_tensor(mk[:, i, :], bank[(b + 1) % 4][:, 0:SEQ], rstd[:, 2, FIRST], ALU.mult).then_inc(evac, 1)
                split_lo(dve, At(n + AHEAD))
                if i:
                    rotate(i - 1)
            rotate(7)

        def stick_pe(pe):
            def z(s):
                for b in range(2):
                    q, k = half(sbq[:, s, FIRST], b), half(sbk[:, s, FIRST], b)
                    if s > 0:
                        pe.wait_ge(z_arg, 2 * s)
                    pe.matmul(bank[2 + b][:, 0:256], k[:, 0:128], q, start=True, stop=True)
                    mm = pe.matmul(bank[2 + b][:, 256:384], k[:, 128:256], q[:, 128:256], start=True, stop=True)
                mm.then_inc(z_ready, 1)

            def sums(s):
                pe.wait_ge(z_masked, 4 * (s + 1))
                pe.wait_ge(z_split, 4 * (s + 1))
                for b in range(2):
                    dst, x = bank[2 + b], nlk[:, b, :]
                    pe.matmul(dst[:, 0:256], const("laterneg"), x[:, 0:256], start=True, stop=False, skip_group_check=True)
                    pe.matmul(dst[:, 128:256], const("allneg"), x[:, 256:384], start=False, stop=True, skip_group_check=True)
                    mm = pe.matmul(dst[:, 256:384], const("laterneg"), x[:, 256:384], start=True, stop=True, skip_group_check=True)
                mm.then_inc(z_sum, 1)

            def values(s):
                pe.wait_ge(z_w, 4 * (s + 1))
                if s > 0:
                    pe.wait_ge(z_olo, s)
                for b in range(2):
                    v = [scr[:, L0 + s * 256 + t * 128 + 64 * b:][:, 0:64] for t in range(2)]
                    dst, w = bank[1][64 * b:64 * b + 64, :], zlog[:, b, :]
                    pe.matmul(dst[:, 0:256], v[0], w[:, 0:256], start=True, stop=False, skip_group_check=True)
                    mm = pe.matmul(dst[:, 128:256], v[1], w[:, 256:384], start=False, stop=True, skip_group_check=True)
                mm.then_inc(z_o, 1)

            def step(at, s):
                if at == 0 and s < 4:
                    z(s)
                if at == 0 and 1 <= s <= 4:
                    values(s - 1)
                if at == 1 and s < 4:
                    sums(s)
            return step

        def stick_act(act, link):
            def logs(s):
                for b in range(2):
                    act.wait_ge(z_ready, s + 1)
                    z = zlog[:, b, :]
                    if s > 0:
                        act.wait_ge(z_o, s)
                    act.activation(z, bank[2 + b][:, 0:384], ACT.Abs).then_inc(link.sem, 1)
                    act.wait_ge(link.sem, link.next())
                    act.activation(z, z, ACT.Exp, scale=-1.0).then_inc(link.sem, 1)
                    act.wait_ge(link.sem, link.next())
                    act.activation(z, z, ACT.Ln, bias=bias[:, 1:2]).then_inc(z_log, 1)

            def step(at, s):
                if at == 0 and 1 <= s <= 4:
                    act.wait_ge(z_o, s)
                    act.activation(ahi[:, 3 + s, FIRST], bank[1][:, 0:256], ACT.Copy).then_inc(z_ohi, 1)
                if at == 0 and s < 4:
                    logs(s)
                if at == 1 and s < 4:
                    for b in range(2):
                        act.wait_ge(z_arg, 2 * s + b + 1)
                        act.activation(zlog[:, b, :], ls[:, b, :], ACT.Exp).then_inc(z_exp, 1)
            return step

        def stick_dve(dve):
            before = const("before")

            def step(at, s):
                if at == 0 and 1 <= s <= 4:
                    dve.wait_ge(z_ohi, s)
                    dve.tensor_tensor(alo[:, 3 + s, FIRST], bank[1][:, 0:256], ahi[:, 3 + s, FIRST].bitcast(F32),
                                      ALU.subtract).then_inc(z_olo, 1)
                if at == 0 and s < 4:
                    for b in range(2):
                        dve.wait_ge(z_log, 2 * s + b + 1)
                        z = bank[2 + b][:, 0:384]
                        dve.scalar_tensor_tensor(out=nlk[:, b, :], in0=z, scalar=0.0, in1=zlog[:, b, :], op0=ALU.max,
                                                 op1=ALU.add).then_inc(z_split, 1)
                        dve.scalar_tensor_tensor(out=ls[:, b, :], in0=z, scalar=0.0, in1=zlog[:, b, :], op0=ALU.min,
                                                 op1=ALU.subtract).then_inc(z_split, 1)
                        dve.wait_ge(z_split, 4 * s + 2 * b + 1)
                        for c in (0, 256):
                            dve.tensor_tensor(nlk[:, b, c:c + 128], nlk[:, b, c:c + 128], before, ALU.mult).then_inc(z_masked, 1)
                if at == 1 and s < 4:
                    dve.wait_ge(z_sum, s + 1)
                    for b in range(2):
                        dve.tensor_tensor(ls[:, b, :], ls[:, b, :], bank[2 + b][:, 0:384], ALU.add).then_inc(z_arg, 1)
                    for b in range(2):
                        dve.wait_ge(z_exp, 2 * s + b + 1)
                        for c in (0, 256):
                            dve.tensor_tensor(zlog[:, b, c:c + 128], zlog[:, b, c:c + 128], before, ALU.mult).then_inc(z_w, 1)
            return step

        def wi_pe(pe):
            n, b = START["wi"], BSTART["wi"]
            pe.wait_ge(evac, b - 3)
            unit_mm(pe, At(n), bank[b % 4][:, 0:T], uhi, ulo, WHOLE)
            pe.wait_ge(evac, b + 1)
            for t in range(3):
                w = min(128, T - 128 * t)
                mm = pe.transpose(bank[6][0:w, 8 * t:8 * t + 8], relu_t[0:8, 0, 128 * t:128 * t + w], const("ident")[0:8, 0:8])
            mm.then_inc(wi_turned, 1)

        def wi_dve(dve):
            n, b = START["wi"], BSTART["wi"]
            split_lo(dve, At(n + AHEAD))
            dve.wait_ge(w_used, n + 1)
            dve.tensor_tensor(relu_t[0:8, 0, :], bank[b % 4][0:8, 0:T], rstd[0:8, 0, :], ALU.mult).then_inc(evac, 1)
            dve.wait_ge(wi_turned, 1)
            k = 8 ** -0.5 * HD ** -0.5
            dve.tensor_scalar(wi[:, 0:16], bank[6][:, 0:16], k, None, ALU.mult).then_inc(wi_done, 1)
            dve.tensor_scalar(wi[0:META, 16:24], bank[6][0:META, 16:24], k, None, ALU.mult).then_inc(wi_done, 1)

        def index_pe(pe):
            pe.wait_ge(y_done, 5)
            pe.wait_ge(wi_done, 2)
            for i in range(8):
                q, k = half(q_all[:, i // 2, :], i), half(q_all[:, 4, :], i)
                big, tail = (bank[5], bank[7]) if i % 2 == 0 else (bank[6], bank[4])
                if 2 * (i - 1) > 0:
                    pe.wait_ge(ix_relu, 2 * (i - 1))
                pe.matmul(big[:, 0:128], q[:, 0:128], k[:, 0:128], start=True, stop=True)
                pe.matmul(big[:, 128:384], q[:, 128:256], k[:, 0:256], start=True, stop=True)
                pe.matmul(tail[0:META, 0:T], q[:, 256:T], k[:, 0:T], start=True, stop=True).then_inc(ix_ready, 1)

        def index_act(act):
            for i in range(8):
                big, tail = (bank[5], bank[7]) if i % 2 == 0 else (bank[6], bank[4])
                act.wait_ge(ix_ready, i + 1)
                if 3 * (i - 1) > 0:
                    act.wait_ge(ix_acc, 3 * (i - 1))
                act.activation(relu[:, i % 2, 0:384], big[:, 0:384], ACT.Relu).then_inc(ix_relu, 1)
                act.activation(relu_t[0:META, i % 2, :], tail[0:META, 0:T], ACT.Relu).then_inc(ix_relu, 1)

        def index_dve(dve):
            for i in range(8):
                dve.wait_ge(ix_relu, 2 * (i + 1))
                for t, (src, rows) in enumerate(((relu[:, i % 2, 0:128], P), (relu[:, i % 2, 128:384], P), (relu_t[0:META, i % 2, :], META))):
                    w, dst = wi[0:rows, 8 * t + i:8 * t + i + 1], score[t][0:rows]
                    if i == 0:
                        dve.tensor_scalar(dst, src, w, None, ALU.mult).then_inc(ix_acc, 1)
                    else:
                        dve.wait_ge(ix_acc, 3 * (i - 1) + t + 1)
                        dve.scalar_tensor_tensor(out=dst, in0=src, scalar=w, in1=dst, op0=ALU.mult, op1=ALU.add).then_inc(ix_acc, 1)

        TOPK_STEPS = TOPK // 8 + 2

        def topk_step(dve, link, t, n):
            rows, w = (P, P, META)[t], (128, 256, T)[t]
            sc = score[t][0:rows]
            d0 = w - rows
            cm = const("causal")[0:rows, 0:rows]
            if n == 0:
                dve.wait_ge(ix_acc, 24)
                dve.tensor_tensor(sc[:, d0:w], sc[:, d0:w], cm, ALU.add).then_inc(link.sem, 1)
                dve.wait_ge(link.sem, link.next())
            elif n < TOPK_STEPS - 1:
                dve.max(out=best[0:rows], in_=sc).then_inc(link.sem, 1)
                dve.wait_ge(link.sem, link.next())
                dve.match_replace(out=sc, in_to_replace=best[0:rows], in_values=sc, imm_value=TAKEN).then_inc(link.sem, 1)
                dve.wait_ge(link.sem, link.next())
            else:
                dve.tensor_scalar(sc, sc, TAKEN * 0.9, NEG, ALU.is_gt, ALU.mult).then_inc(link.sem, 1)
                dve.wait_ge(link.sem, link.next())
                dve.tensor_tensor(sc[:, d0:w], sc[:, d0:w], cm, ALU.add).then_inc(link.sem, 1)
                dve.wait_ge(link.sem, link.next())
                c0 = (0, 128, 384)[t]
                dve.tensor_copy(selmask[0:rows, c0:c0 + w], sc).then_inc(ix_mask, 1)

        def topk_between(dve, link, first):
            def between(j):
                for n in range(2 * TOPK_STEPS * (first + j) // 14, 2 * TOPK_STEPS * (first + j + 1) // 14):
                    topk_step(dve, link, n // TOPK_STEPS, n % TOPK_STEPS)
            return between

        tailq = area(E0 + 1760, 128)
        tprob = area(E0 + 664, T)
        tprobT = area(E0 + 664 + T, 384)

        def tail_pe(pe):
            idn = const("ident")
            s, pt, o = bank[2], bank[3], bank[1]

            def scores(t):
                pe.wait_ge(t_q, 1)
                pe.wait_ge(ix_mask, 3)
                if t > 0:
                    pe.wait_ge(t_exp, t)
                for r in range(4):
                    g, par = 2 * t + r // 2, r % 2
                    q = tailq[64 * par:64 * par + 64, 32 * g:32 * g + 32]
                    pe.matmul(s[32 * r:32 * r + 32, 0:T], q, k_all[64 * par:64 * par + 64, g, 0:T], start=True, stop=False,
                              skip_group_check=True)
                pe.matmul(s[:, 0:T], repb, selmask[0:META, 384:384 + T], start=False, stop=True,
                          skip_group_check=True).then_inc(t_s, 1)

            def turn(t):
                pe.wait_ge(t_p, t + 1)
                if t > 0:
                    pe.wait_ge(t_pts, 2 * t)
                pe.transpose(pt[0:META, 256:384], tprob[:, 256:T], idn)
                pe.transpose(pt[:, 0:128], tprob[:, 0:128], idn)
                pe.transpose(pt[:, 128:256], tprob[:, 128:256], idn).then_inc(t_pt, 1)

            def values(t):
                pe.wait_ge(t_pts, 2 * (t + 1))
                if t > 0:
                    pe.wait_ge(t_olo, t)
                for r in range(4):
                    g, par = 2 * t + r // 2, r % 2
                    dst = o[64 * par:64 * par + 64, 32 * (r // 2):32 * (r // 2) + 32]
                    for tile, rows in ((0, P), (1, P), (2, META)):
                        c = V0 + (g // 2) * 384 + tile * 128 + 64 * (g % 2)
                        mm = pe.matmul(dst, scr[0:rows, c:c + 64], tprobT[0:rows, 128 * tile + 32 * r:128 * tile + 32 * r + 32],
                                       start=tile == 0, stop=tile == 2, skip_group_check=True)
                mm.then_inc(t_o, 1)

            def step(at, n):
                if (at, n) == (1, 5):
                    scores(0)
                if (at, n) == (0, 7):
                    turn(0)
                if (at, n) == (1, 7):
                    values(0)
                    scores(1)
                if (at, n) == (0, 9):
                    turn(1)
                if (at, n) == (1, 9):
                    values(1)
            return step

        def tail_act(act):
            def exp(t):
                act.wait_ge(t_max, t + 1)
                if t > 0:
                    act.wait_ge(t_pt, t)
                act.activation(tprob, bank[2][:, 0:T], ACT.Exp, bias=small[:, 16:17], accum_out=small[:, 17:18]).then_inc(t_exp, 1)

            def copy(t):
                act.wait_ge(t_pt, t + 1)
                if t > 0:
                    act.wait_ge(t_o, t)
                act.activation(tprobT[0:META, 256:384], bank[3][0:META, 256:384], ACT.Copy).then_inc(t_pts, 1)
                act.activation(tprobT[:, 0:256], bank[3][:, 0:256], ACT.Copy).then_inc(t_pts, 1)

            def out_hi(t):
                act.wait_ge(t_o, t + 1)
                act.activation(ahi[:, 4 * t:4 * t + 4, 256:T], bank[1][:, 0:64].rearrange("p (c n) -> p c n", n=META),
                               ACT.Copy).then_inc(t_ohi, 1)

            def step(at, n):
                if (at, n) == (0, 6):
                    exp(0)
                if (at, n) == (0, 7):
                    copy(0)
                if (at, n) == (0, 8):
                    out_hi(0)
                    exp(1)
                if (at, n) == (0, 9):
                    copy(1)
                if (at, n) == (1, 9):
                    out_hi(1)
            return step

        def tail_dve(dve, link):
            def row_max(t):
                dve.wait_ge(t_s, t + 1)
                dve.tensor_reduce(small[:, 16:17], bank[2][:, 0:T], AX.X, ALU.max, negate=True).then_inc(t_max, 1)

            def norm(t):
                dve.wait_ge(t_exp, t + 1)
                dve.reciprocal(small[:, 18:19], small[:, 17:18]).then_inc(link.sem, 1)
                dve.wait_ge(link.sem, link.next())
                dve.tensor_scalar(tprob, tprob, small[:, 18:19], None, ALU.mult).then_inc(t_p, 1)

            def tail_lo(t):
                dve.wait_ge(t_ohi, t + 1)
                dve.tensor_tensor(alo[:, 4 * t:4 * t + 4, 256:T], bank[1][:, 0:64].rearrange("p (c n) -> p c n", n=META),
                                  ahi[:, 4 * t:4 * t + 4, 256:T].bitcast(F32), ALU.subtract).then_inc(t_olo, 1)

            def step(at, n):
                if at == 0 and n == 0:
                    dve.wait_ge(y_done, 17)
                    dve.tensor_copy(tailq.rearrange("p (c n) -> p c n", n=META), q_all[:, :, 256:T]).then_inc(t_q, 1)
                if n < 5:
                    topk_step(dve, link, 2, 2 * n + at)
                if (at, n) == (1, 5):
                    row_max(0)
                if (at, n) == (1, 6):
                    norm(0)
                if (at, n) == (1, 7):
                    row_max(1)
                if (at, n) == (1, 8):
                    tail_lo(0)
                    norm(1)
                if (at, n) == (1, 9):
                    tail_lo(1)
            return step

        fx, fe, fc = area(E0 + 1760, T), area(E0 + 1760 + T, T), area(S0, T)

        def forget_pe(pe):
            n, b = START["ff"], BSTART["ff"]
            pe.wait_ge(evac, b - 3)
            unit_mm(pe, At(n), bank[b % 4][:, 0:T], uhi, ulo, WHOLE, x=u_chunk(7))
            norm_pe(pe, 7, WHOLE)

        def forget_act(act, link):
            split_hi(act, At(START["ff"] + AHEAD))
            x = fx[0:16]
            act.wait_ge(f_exp, 1)
            act.activation(fe[0:16], x, ACT.Abs).then_inc(link.sem, 1)
            act.wait_ge(link.sem, link.next())
            act.activation(fe[0:16], fe[0:16], ACT.Exp, scale=-1.0).then_inc(link.sem, 1)
            act.wait_ge(link.sem, link.next())
            act.activation(fe[0:16], fe[0:16], ACT.Ln, bias=bias[0:16, 1:2]).then_inc(f_log, 1)

        def forget_dve(dve, link):
            n, b = START["ff"], BSTART["ff"]
            split_lo(dve, At(n + AHEAD))
            dve.wait_ge(rstd_ready, 8)
            dve.wait_ge(w_used, n + 1)
            dve.memset(csplit[:, :], 0.0).then_inc(link.sem, 1)
            dve.wait_ge(link.sem, link.next())
            x, l = fx[0:16], fe[0:16]
            dve.tensor_tensor(x, bank[b % 4][0:16, 0:T], rstd[0:16, 0, :], ALU.mult).then_inc(evac, 1)
            dve.wait_ge(evac, b + 1)
            dve.tensor_scalar(x, x, gain("fb")[0:16], None, ALU.add).then_inc(f_exp, 1)
            dve.wait_ge(f_log, 1)
            dve.scalar_tensor_tensor(out=x, in0=x, scalar=0.0, in1=l, op0=ALU.min, op1=ALU.subtract).then_inc(link.sem, 1)
            dve.wait_ge(link.sem, link.next())
            dve.memset(l, 1.0).then_inc(link.sem, 1)
            dve.wait_ge(link.sem, link.next())
            c = fc[0:16]
            dve.tensor_tensor_scan(c, l, x, 0.0, ALU.mult, ALU.add).then_inc(link.sem, 1)
            dve.wait_ge(link.sem, link.next())
            dve.tensor_scalar(c, c, -1.0, None, ALU.mult).then_inc(link.sem, 1)
            dve.wait_ge(link.sem, link.next())
            for k in range(3):
                part = csplit[32 * k:32 * k + 16, :]
                dve.tensor_copy(part, c).then_inc(f_split, 1)
                dve.wait_ge(f_split, k + 1)
                if k < 2:
                    dve.tensor_copy(l, part).then_inc(link.sem, 1)
                    dve.wait_ge(link.sem, link.next())
                    dve.tensor_tensor(c, c, l, ALU.subtract).then_inc(link.sem, 1)
                    dve.wait_ge(link.sem, link.next())

        def second_u_act(act):
            for m in range(DC):
                act.activation(ahi[:, 8 + m, :], h[:, m, :], ACT.Copy, scale=gain("attn1", m)).then_inc(u2_hi, 1)

        def second_u_dve(dve):
            for m in range(DC):
                dve.wait_ge(u2_hi, m + 1)
                dve.scalar_tensor_tensor(out=alo[:, 8 + m, :], in0=h[:, m, :], scalar=gain("attn1", m),
                                         in1=ahi[:, 8 + m, :].bitcast(F32), op0=ALU.mult, op1=ALU.subtract).then_inc(u2_lo, 1)

        block = ctx.enter_context(nc.Block())

        @block.sync
        def _(sp):
            sp.dma_start(g_t[:, :], gains).then_inc(gains_loaded, 16)
            for i in range(4):
                sp.dma_start(h[:, 2 * i:2 * i + 2, FIRST], xT[:, 2 * i:2 * i + 2, :]).then_inc(x_loaded[i], 16)
            for s in range(RING):
                sp.dma_start(raw[:, s, :], stream[s]).then_inc(w_loaded[s], 16)
            sp.dma_start(c_t[:, :], consts).then_inc(consts_loaded, 16)
            sp.dma_start(h[:, :, 0:META], metaT).then_inc(meta_loaded, 16)
            with sp.Fori(1, UNITS // RING) as it:
                for s in range(RING):
                    sp.wait_ge(w_lo, it * RING + (s - RING + 1))
                    sp.dma_start(raw[:, s, :], stream[bass.ds(it * RING + s, 1)].rearrange("a p n -> (a p) n")).then_inc(w_loaded[s], 16)
            for s in range(UNITS % RING):
                n = UNITS // RING * RING + s
                sp.wait_ge(w_lo, n - RING + 1)
                sp.dma_start(raw[:, s, :], stream[n]).then_inc(w_loaded[s], 16)
            for m in range(DC):
                sp.wait_ge(evac, BSTART["dn3"] + m + 1)
                sp.dma_start(out[:, m, :], h[:, m, META:T]).then_inc(stored, 16)
            sp.wait_ge(stored, 16 * DC)

        @block.tensor
        def _(pe):
            pe.wait_ge(bias_set, 3)
            first_pe(pe)
            pe.wait_ge(consts_cast, 5)
            pe.wait_ge(m_qdone, 8)
            pe.wait_ge(m_kdone, 8)
            pe.wait_ge(evac, BSTART["out0"])
            att_pe(pe, mla, stick_pe(pe))
            resid_pe(pe, "out0", DC, FIRST, lambda i: (o_lo, i + 1) if i < 4 else (z_olo, i - 3))
            swiglu_pe(pe, "gu0", FIRST, 1)
            resid_pe(pe, "dn0", FC1, FIRST, lambda i: (a_lo, i + 1))
            proj_pe(pe, "bv", "v", FIRST, 2, sum_norm=2)
            proj_pe(pe, "bq", "plain", FIRST, 2)
            proj_pe(pe, "bk", "plain", FIRST, 2)
            pe.wait_ge(evac, BSTART["out1"])
            pe.wait_ge(v_stored, VFIRST["dv"])
            att_pe(pe, band)
            resid_pe(pe, "out1", DC, FIRST, lambda i: (o_lo, 4 + i + 1))
            swiglu_pe(pe, "gu1", FIRST, 3)
            resid_pe(pe, "dn1", FC1, FIRST, lambda i: (a_lo, FC1 + i + 1))
            norm_pe(pe, 4, FIRST)
            proj_pe(pe, "ki", "rope", WHOLE, 5, sum_norm=5)
            wi_pe(pe)
            proj_pe(pe, "qi", "rope", WHOLE, 5)
            index_pe(pe)
            pe.wait_ge(ix_relu, 16)
            proj_pe(pe, "dk", "rmsrope", WHOLE, 5)
            pe.wait_ge(y_done, 9)
            pe.wait_ge(y_rstd, 4)
            proj_pe(pe, "dv", "v", WHOLE, 5)
            pe.wait_ge(v_stored, VFIRST["fv"])
            proj_pe(pe, "dq", "rmsrope", WHOLE, 5)
            pe.wait_ge(y_done, 17)
            pe.wait_ge(ix_mask, 2)
            att_pe(pe, dsa, tail_pe(pe))
            pe.wait_ge(t_olo, 2)
            resid_pe(pe, "out2", DC, WHOLE, lambda i: (o_lo, 12 + i + 1))
            sqrelu_pe(pe, "up2", WHOLE, 6)
            resid_pe(pe, "dn2", FC2, WHOLE, lambda i: (a_lo, 2 * FC1 + i + 1))
            forget_pe(pe)
            proj_pe(pe, "fv", "v", WHOLE, 7)
            pe.wait_ge(v_stored, 22)
            proj_pe(pe, "fk", "rms", WHOLE, 7)
            proj_pe(pe, "fq", "rms", FIRST, 7, second=True)
            pe.wait_ge(y_done, 33)
            pe.wait_ge(f_split, 3)
            pe.wait_ge(sel_loaded, 16)
            att_pe(pe, fox)
            resid_pe(pe, "out3", DC, FIRST, lambda i: (o_lo, 20 + i + 1))
            sqrelu_pe(pe, "up3", FIRST, 8)
            resid_pe(pe, "dn3", FC2, FIRST, lambda i: (a_lo, 2 * FC1 + FC2 + i + 1))

        @block.scalar
        def _(act):
            act.preload_act_table_set("natural_log_exp_and_others")
            link = Chain(act_chain)
            first_act(act, link)
            att_act(act, link, mla, stick_act(act, link))
            resid_act(act, link, "out0", DC, FIRST, 1, "ffn0")
            swiglu_act(act, link, "gu0", FIRST)
            resid_act(act, link, "dn0", FC1, FIRST, 2, "mix1")
            proj_act(act, link, "bv", "v", FIRST)
            proj_act(act, link, "bq", "plain", FIRST)
            proj_act(act, link, "bk", "plain", FIRST)

            def relh_load(where, s):
                if where == 0 and s < band.pairs:
                    if s == 0:
                        act.wait_ge(evac, BSTART["out1"])
                        for n in (0, 1):
                            act.dma_start(relb[:, n, :, :], relh[n]).then_inc(rel_loaded[n], 16)
                if where == 1 and s + 2 < band.pairs:
                    act.wait_ge(s_ready, band.head0 + 2 * s + 2)
                    act.dma_start(relb[:, s % 2, :, :], relh[s + 2]).then_inc(rel_loaded[s % 2], 16)
            att_act(act, link, band, relh_load)
            resid_act(act, link, "out1", DC, FIRST, 3, "ffn1")
            swiglu_act(act, link, "gu1", FIRST)
            resid_act(act, link, "dn1", FC1, FIRST, 4, "final")
            act.wait_ge(meta_loaded, 16)
            for m in range(DC):
                act.wait_ge(x2_ready, m + 1)
                norm_act(act, 5, m, WHOLE, "attn0")
            norm_rstd(act, link, 5, WHOLE)
            proj_act(act, link, "ki", "rope", WHOLE)
            split_hi(act, At(START["wi"] + AHEAD))
            proj_act(act, link, "qi", "rope", WHOLE)
            index_act(act)
            proj_act(act, link, "dk", "rmsrope", WHOLE)
            proj_act(act, link, "dv", "v", WHOLE)
            proj_act(act, link, "dq", "rmsrope", WHOLE)
            att_act(act, link, dsa, tail_act(act))
            resid_act(act, link, "out2", DC, WHOLE, 6, "mlp0")
            sqrelu_act(act, "up2", WHOLE)
            resid_act(act, link, "dn2", FC2, WHOLE, 7, "kvn")
            act.dma_start(area(E0, 1024)[0:96, :], sel).then_inc(sel_loaded, 16)
            forget_act(act, link)
            proj_act(act, link, "fv", "v", WHOLE)
            second_u_act(act)
            proj_act(act, link, "fk", "rms", WHOLE)
            proj_act(act, link, "fq", "rms", FIRST)
            att_act(act, link, fox)
            resid_act(act, link, "out3", DC, FIRST, 8, "mlp1")
            sqrelu_act(act, "up3", FIRST)
            resid_act(act, link, "dn3", FC2, FIRST, None, None)

        @block.vector
        def _(dve):
            link = Chain(dve_chain)
            first_dve(dve, link)
            att_dve(dve, link, mla, stick_dve(dve))
            resid_dve(dve, "out0", DC, FIRST, 1, "ffn0")
            swiglu_dve(dve, "gu0", FIRST, 1, 0)
            resid_dve(dve, "dn0", FC1, FIRST, 2, "mix1")
            proj_dve(dve, link, "bv", "v", FIRST, norm=2)
            proj_dve(dve, link, "bq", "plain", FIRST, first=Q0, scale=HD ** -0.5, norm=2)
            proj_dve(dve, link, "bk", "plain", FIRST, first=K0, norm=2)
            att_dve(dve, link, band)
            resid_dve(dve, "out1", DC, FIRST, 3, "ffn1")
            swiglu_dve(dve, "gu1", FIRST, 3, FC1)
            resid_dve(dve, "dn1", FC1, FIRST, 4, "final")
            dve.wait_ge(rstd_ready, 5)
            for m in range(DC):
                dve.scalar_tensor_tensor(out=h[:, m, FIRST], in0=h[:, m, FIRST], scalar=gain("final", m), in1=rstd[:, 0, FIRST],
                                         op0=ALU.mult, op1=ALU.mult).then_inc(x2_ready, 1)
            for m in range(DC):
                norm_dve(dve, 5, m, WHOLE, "attn0")
            proj_dve(dve, link, "ki", "rope", WHOLE, first=4 * T, norm=5)
            wi_dve(dve)
            proj_dve(dve, link, "qi", "rope", WHOLE, first=0, norm=5)
            index_dve(dve)
            proj_dve(dve, link, "dk", "rmsrope", WHOLE, first=K0, gcol=gain("ak"), norm=5, between=topk_between(dve, link, 0))
            proj_dve(dve, link, "dv", "v", WHOLE, norm=5, between=topk_between(dve, link, 4))
            proj_dve(dve, link, "dq", "rmsrope", WHOLE, first=Q0, gcol=gains8[:, 0:1], norm=5,
                     between=topk_between(dve, link, 6))
            att_dve(dve, link, dsa, tail_dve(dve, link))
            resid_dve(dve, "out2", DC, WHOLE, 6, "mlp0")
            sqrelu_dve(dve, "up2", WHOLE, 6, 2 * FC1)
            resid_dve(dve, "dn2", FC2, WHOLE, 7, "kvn")
            forget_dve(dve, link)
            proj_dve(dve, link, "fv", "v", WHOLE, norm=7)
            second_u_dve(dve)
            proj_dve(dve, link, "fk", "rms", WHOLE, first=K0, gcol=gain("kk"), norm=7)
            proj_dve(dve, link, "fq", "rms", FIRST, first=Q0, gcol=gains8[:, 1:2], norm=7)
            att_dve(dve, link, fox)
            resid_dve(dve, "out3", DC, FIRST, 8, "mlp1")
            sqrelu_dve(dve, "up3", FIRST, 8, 2 * FC1 + FC2)
            resid_dve(dve, "dn3", FC2, FIRST, None, None)

        @block.gpsimd
        def _(pool):
            pool.memset(bias[:, 0:1], EPS).then_inc(bias_set, 1)
            pool.memset(bias[:, 1:2], 1.0).then_inc(bias_set, 1)
            pool.memset(ones[:, :], 1.0).then_inc(bias_set, 1)
            norm_pool(pool, 0, FIRST)
            norm_pool(pool, 1, FIRST)
            swiglu_pool(pool, "gu0", FIRST, 1, 0)
            norm_pool(pool, 2, FIRST)
            norm_pool(pool, 3, FIRST)
            swiglu_pool(pool, "gu1", FIRST, 3, FC1)
            norm_pool(pool, 4, FIRST)
            norm_pool(pool, 5, WHOLE)
            proj_pool(pool, "ki", "rope", WHOLE)
            proj_pool(pool, "qi", "rope", WHOLE)
            proj_pool(pool, "dk", "rmsrope", WHOLE)
            proj_pool(pool, "dq", "rmsrope", WHOLE)
            norm_pool(pool, 6, WHOLE)
            sqrelu_pool(pool, "up2", WHOLE, 2 * FC1, 0)
            norm_pool(pool, 7, WHOLE)
            norm_pool(pool, 8, FIRST)
            sqrelu_pool(pool, "up3", FIRST, 2 * FC1 + FC2, FC2)


def unit_of(w, cols, chunks=None):
    u = np.zeros((P, DC, P), w.dtype)
    k = w.shape[0] // P
    u[:, :k, :len(cols)] = w[:, cols].reshape(k, P, len(cols)).transpose(1, 0, 2)
    return u.reshape(P, UNIT)


def blocks_of(w, first, last):
    units = []
    for c in range(first, last, P):
        for r in range(0, w.shape[0], UNIT):
            units.append(unit_of(w[r:r + UNIT], np.arange(c, c + P)))
    return units


def stream_of(a):
    w_in = a["ev_w_in"][0]
    o = QL + KVL + ROPE
    nb = 8 * HD
    s = blocks_of(w_in, 0, QL) + blocks_of(w_in, QL, QL + KVL)
    kr = unit_of(w_in, np.arange(QL + KVL, o)).reshape(P, DC, P)
    moved = np.zeros_like(kr)
    moved[:, :, NOPE:NOPE + ROPE] = kr[:, :, 0:ROPE]
    s.append(moved.reshape(P, UNIT))
    s += blocks_of(w_in, o + 2 * nb, o + 3 * nb) + blocks_of(w_in, o, o + nb) + blocks_of(w_in, o + nb, o + 2 * nb)
    uq, ukv = a["ev_w_uq"][0], a["ev_w_ukv"][0]
    for i in range(8):
        u = np.zeros((P, DC, P), uq.dtype)
        u[:, :QC] = unit_of(uq, np.arange(96 * i, 96 * i + 96)).reshape(P, DC, P)[:, :QC]
        u[:, QC:QC + KVC] = unit_of(ukv, np.arange(128 * i, 128 * i + 128)).reshape(P, DC, P)[:, :KVC]
        s.append(u.reshape(P, UNIT))
    s += blocks_of(a["ev_w_out"][0], 0, D)

    def swiglu(layer):
        g, u = blocks_of(a["w_gate"][layer], 0, FF1), blocks_of(a["w_up"][layer], 0, FF1)
        return [x for pair in zip(g, u) for x in pair] + blocks_of(a["w_down"][layer], 0, D)

    s += swiglu(0)
    qkv = a["od_w_qkv"][0]
    s += blocks_of(qkv, 2 * D, 3 * D) + blocks_of(qkv, 0, D) + blocks_of(qkv, D, 2 * D) + blocks_of(a["od_w_out"][0], 0, D)
    s += swiglu(1)
    w = a["a_w_in_2"][0]
    q, k, v, qi, ki = D, D + 256, D + 512, D + 1024, D + 1088
    two = np.arange(HD)
    s.append(unit_of(w, np.concatenate([qi + two, qi + two])))
    s.append(unit_of(w, np.arange(ki, ki + 8)))
    s += blocks_of(w, v, qi)
    for g in range(4):
        s.append(unit_of(w, np.concatenate([q + HD * g + two, q + HD * g + two])))
    s += blocks_of(w, k, v) + blocks_of(w, 0, D)
    s += blocks_of(a["a_w_out_2"][0], 0, D) + blocks_of(a["mlp_w1_2"][0], 0, FF2) + blocks_of(a["mlp_w2_2"][0], 0, D)
    w = a["kv_w_2"]
    s.append(unit_of(w, np.arange(2 * D, 2 * D + 16)))
    s += blocks_of(w, D, 2 * D) + blocks_of(w, 0, D) + blocks_of(a["b_w_q_2"][0], 0, D)
    s += blocks_of(a["b_w_out_2"][0], 0, D) + blocks_of(a["mlp_w1_2"][1], 0, FF2) + blocks_of(a["mlp_w2_2"][1], 0, D)
    s += [np.zeros((P, UNIT), w.dtype)] * AHEAD
    assert len(s) == UNITS
    return np.stack(s)


def gains_of(a):
    g = np.zeros((P, NG), np.float32)

    def put(name, v):
        v = np.asarray(v)
        g[:, GCOL[name]:GCOL[name] + v.size // P] = v.reshape(-1, P).T

    for name, v in (("mix0", a["g_mix"][0]), ("ffn0", a["g_ffn"][0]), ("mix1", a["g_mix"][1]), ("ffn1", a["g_ffn"][1]),
                    ("final", a["g_final"]), ("attn0", a["attn_norm_2"][0]), ("mlp0", a["mlp_norm_2"][0]), ("kvn", a["kv_norm_2"]),
                    ("attn1", a["attn_norm_2"][1]), ("mlp1", a["mlp_norm_2"][1]), ("cq", a["ev_g_cq"][0]), ("ckv", a["ev_g_ckv"][0])):
        put(name, v)
    for name, v in (("aq", a["a_q_gain_2"][0]), ("ak", a["a_k_gain_2"][0]), ("kk", a["kv_k_gain_2"]), ("bq", a["b_q_gain_2"][0])):
        put(name, np.concatenate([v, v]))
    g[0:16, GCOL["fb"]] = a["kv_f_bias_2"]
    return g


def constants():
    c = np.zeros((P, NCONST), np.float32)

    def put(name, v):
        v = np.asarray(v, np.float32)
        c[:v.shape[0], CCOL[name][0]:CCOL[name][0] + v.shape[1]] = v

    i, j = np.arange(P)[:, None], np.arange(P)[None, :]
    put("ident", i == j)
    put("rev", i + j == P - 1)
    put("headones", i // HD == j // HD)
    put("laterneg", -(i > j).astype(np.float32))
    put("allneg", -np.ones((P, P)))
    put("before", i < j)
    put("causal", np.where(j > i, NEG, 0.0))

    def rotation(first, heads, dim):
        r = np.zeros((P, P), np.float32)
        for hd in range(heads):
            for d in range(dim // 2):
                lo = first + hd * dim + d
                r[lo + dim // 2, lo] = -1.0
                r[lo, lo + dim // 2] = 1.0
        return r

    put("rot", rotation(0, 2, HD))
    put("rotm", rotation(NOPE, 1, ROPE))

    def tables(n, dim, inv):
        ang = np.arange(n, dtype=np.float32)[:, None] * inv[None, :]
        return np.cos(ang).T.astype(np.float32), np.sin(ang).T.astype(np.float32)

    e = np.arange(0, HD, 2, dtype=np.float32) / np.float32(HD)
    cos, sin = tables(T, HD, (np.float32(1.0) / (np.float32(10000.0) ** e)).astype(np.float32))
    put("cos", np.tile(cos, (4, 1)))
    put("sin", np.tile(sin, (4, 1)))
    e = -np.arange(0, ROPE, 2, dtype=np.float32) / np.float32(ROPE)
    cos, sin = tables(SEQ, ROPE, (np.float32(10000.0) ** e).astype(np.float32))
    z = np.zeros((NOPE, SEQ), np.float32)
    put("cosm", np.concatenate([z, cos, cos]))
    put("sinm", np.concatenate([z, sin, sin]))
    put("upper", (np.arange(P) < 64)[None, :])
    put("late", np.full((1, 64), NEG))
    put("rep", (np.arange(P)[None, :] % META) == np.arange(META)[:, None])
    return c


def selection():
    s = np.zeros((96, 16, P), np.uint16)
    for k in range(3):
        for hd in range(16):
            s[32 * k + hd, hd, :] = 0x3F80
    return s.reshape(96, -1).view(np.float32)


def bias_tiles(rb):
    at = 129 + np.arange(P)[:, None] + np.arange(2 * P)[None, :]
    return np.ascontiguousarray(rb[:, at].reshape(8, 2, P, 2 * P).transpose(0, 2, 1, 3))


def kernel(**inputs):
    from concourse import bacc
    from concourse.bass_utils import run_bass_kernel_spmd

    a = {k: np.asarray(v) for k, v in inputs.items()}
    nc = bacc.Bacc("TRN2", target_bir_lowering=False, num_devices=1)

    def chunked(x):
        return np.ascontiguousarray(x.T.reshape(DC, P, x.shape[0]).transpose(1, 0, 2))

    arrays = {
        "stream": stream_of(a), "xT": chunked(a["x"][0]), "metaT": chunked(a["meta_tokens_2"]),
        "gains": gains_of(a), "consts": constants(), "relh": bias_tiles(a["od_rel_bias"][0]), "sel": selection(),
    }
    aps = [nc.dram_tensor(n, v.shape, mybir.dt.from_np(v.dtype), kind="ExternalInput").ap() for n, v in arrays.items()]
    out = nc.dram_tensor("out", (P, DC, SEQ), F32, kind="ExternalOutput").ap()
    program(nc, *aps, out)
    r = run_bass_kernel_spmd(nc, [arrays], core_ids=[0])
    got = np.asarray(r.results[0]["out"])
    return np.ascontiguousarray(got.transpose(1, 0, 2).reshape(D, SEQ).T)[None]
```

```python
from contextlib import ExitStack

import concourse.bass as bass
import numpy as np
from concourse import mybir

ALU = mybir.AluOpType
ACT = mybir.ActivationFunctionType
AX = mybir.AxisListType
F32 = mybir.dt.float32
F32R = mybir.dt.float32r
BF16 = mybir.dt.bfloat16

P = 128
D = 1024
DC = D // P
META = 16
SEQ = 256
T = META + SEQ
QL, KVL = 384, 256
QC, KVC = QL // P, KVL // P
ROPE = 32
NOPE = 64
HD = 64
FF1 = 2816
FC1 = FF1 // P
FF2 = 4096
FC2 = FF2 // P
TOPK = 64
EPS = 1e-6
NEG = -1e30
TAKEN = -3e38
RING = 4
AHEAD = RING - 1
UNIT = DC * P

PHASES = [
    ("cq", 3), ("ckv", 2), ("kr", 1), ("sv", 4), ("sq", 4), ("sk", 4), ("mla", 8), ("out0", 8),
    ("gu0", 44), ("dn0", 24),
    ("bv", 8), ("bq", 8), ("bk", 8), ("out1", 8), ("gu1", 44), ("dn1", 24),
    ("ki", 1), ("wi", 1), ("qi", 4), ("dk", 4), ("dv", 2), ("dq", 8), ("out2", 8), ("up2", 32), ("dn2", 32),
    ("ff", 1), ("fv", 8), ("fk", 8), ("fq", 8), ("out3", 8), ("up3", 32), ("dn3", 32),
    ("end", AHEAD),
]
START = {}
_n = 0
for _name, _k in PHASES:
    START[_name] = _n
    _n += _k
UNITS = _n

BSTART = {}
_n = 0
for _name, _k in PHASES:
    BSTART[_name] = _n
    _n += {"dn": 8, "ml": 16, "en": 0}.get(_name[:2], _k)

GAINS = ["mix0", "ffn0", "mix1", "ffn1", "final", "attn0", "mlp0", "kvn", "attn1", "mlp1"]
GCOL = {name: DC * i for i, name in enumerate(GAINS)}
GCOL.update(cq=80, ckv=83, aq=85, ak=86, kk=87, bq=88, fb=89)
NG = 90

CONSTS = [("ident", 128), ("rev", 128), ("headones", 128), ("laterneg", 128), ("allneg", 128),
          ("rot", 128), ("rotm", 128), ("before", 128), ("causal", 128), ("cos", T), ("sin", T),
          ("cosm", SEQ), ("sinm", SEQ), ("upper", 128), ("late", 64), ("rep", 128)]
CCOL = {}
_n = 0
for _name, _k in CONSTS:
    CCOL[_name] = (_n, _n + _k)
    _n += _k
NCONST = _n


class At:

    def __init__(self, c, it=None, m=0):
        self.c, self.it, self.m = c, it, m

    def __add__(self, k):
        return At(self.c + k, self.it, self.m)

    def times(self, k):
        return At(self.c * k, self.it, self.m * k)

    def mod(self, k):
        assert self.m % k == 0
        return self.c % k

    def div(self, k):
        assert self.m % k == 0
        return At(self.c // k, self.it, self.m // k)

    def value(self):
        assert self.c > 0
        return self.c if self.it is None else self.it * self.m + self.c


class Chain:

    def __init__(self, sem):
        self.sem, self.done, self.it, self.per, self.here = sem, 0, None, 0, 0

    def enter(self, it, per):
        self.it, self.per, self.here = it, per, 0

    def leave(self, trips):
        assert self.here == self.per, (self.here, self.per)
        self.done += self.per * trips
        self.it, self.per, self.here = None, 0, 0

    def next(self):
        if self.it is None:
            self.done += 1
            return self.done
        self.here += 1
        return At(self.done + self.here, self.it, self.per).value()


def program(nc, stream, xT, metaT, gains, consts, relh, sel, out):
    with ExitStack() as ctx:
        def sb(name, cols, dt=F32):
            return ctx.enter_context(nc.sbuf_tensor(name, [P, cols], dt))

        def sem(name):
            return ctx.enter_context(nc.semaphore(name))

        def sems(names):
            return [sem(name) for name in names.split()]

        raw = sb("raw", RING * UNIT)[:, :].rearrange("p (s n) -> p s n", s=RING)
        whi = sb("whi", RING * UNIT, F32R)[:, :].rearrange("p (s n) -> p s n", s=RING)
        wlo = sb("wlo", RING * UNIT, F32R)[:, :].rearrange("p (s n) -> p s n", s=RING)
        uhi = sb("uhi", DC * T, F32R)[:, :].rearrange("p (c t) -> p c t", t=T)
        ulo = sb("ulo", DC * T, F32R)[:, :].rearrange("p (c t) -> p c t", t=T)
        ahi_t = sb("ahi", FC2 * T, F32R)
        alo_t = sb("alo", FC2 * T, F32R)
        ahi = ahi_t[:, :].rearrange("p (c t) -> p c t", t=T)
        alo = alo_t[:, :].rearrange("p (c t) -> p c t", t=T)
        h = sb("h", DC * T)[:, :].rearrange("p (c t) -> p c t", t=T)
        g_t = sb("gain_columns", NG)
        c_t = sb("constants", NCONST)
        rstd = sb("rstd", 3 * T)[:, :].rearrange("p (c t) -> p c t", t=T)
        lg = sb("log_mean", T)
        acc = sb("sum_of_squares", T)
        bias = sb("bias_columns", 2)
        gains8 = sb("gains_over_8", 2)
        ones = sb("ones", 128)
        two_gains = sb("two_gains", DC)
        identb = sb("identb", 128, BF16)
        causalb = sb("causalb", 128, BF16)
        rowsb = sb("rowsb", 128 + 64 + 128, BF16)
        selmask = sb("selmask", 128 + 256 + T, BF16)
        wi = sb("wi", 3 * 8)
        SCR = 12208
        scr = sb("scratch", SCR)
        upperb, lateb, repb = rowsb[0:1, 0:128], rowsb[0:1, 128:192], rowsb[0:16, 192:320]

        def area(at, cols):
            assert at + cols <= SCR, (at, cols)
            return scr[:, at:at + cols]

        Q0, K0, V0 = 0, DC * T, 2 * DC * T
        q_all = area(Q0, DC * T).rearrange("p (c t) -> p c t", t=T)
        k_all = area(K0, DC * T).rearrange("p (c t) -> p c t", t=T)
        sq_all = q_all
        x2_sq = k_all
        x2_sum = area(V0, T)
        x2_t = area(V0 + T, 3 * T).rearrange("p (b t) -> p b t", b=3)
        S0 = V0 + 3 * D
        prob = area(S0, 832).rearrange("p (b n) -> p b n", b=2)
        probT = area(S0 + 832, 768).rearrange("p (b n) -> p b n", b=2)
        probTA = area(S0 + 1600, 512).rearrange("p (b n) -> p b n", b=2)
        small = area(S0 + 2112, 64)
        yb = area(S0, 4 * T).rearrange("p (b t) -> p b t", b=4)
        y2 = area(S0 + 4 * T, 2 * T).rearrange("p (b t) -> p b t", b=2)
        ysq = area(S0 + 6 * T, 2 * T).rearrange("p (b t) -> p b t", b=2)
        E0 = S0 + 8 * T
        hr = area(E0 + 1760, 2 * T).rearrange("p (b t) -> p b t", b=2)
        relb = area(E0, 1024).rearrange("p (s b n) -> p s b n", s=2, b=2)
        selb = area(E0, 1024).bitcast(BF16).rearrange("p (h n) -> p h n", n=128)
        csplit = area(E0 + 1024, T // 2).bitcast(BF16)
        score = [area(E0, T), area(E0 + T, 256)]
        best = area(E0 + T + 256, 8)
        relu_t = area(E0 + 664, 2 * T).rearrange("p (b t) -> p b t", b=2)
        mc = area(E0 + 664 + 2 * T, 2 * T).rearrange("p (b t) -> p b t", b=2)
        relu = area(K0 + 4 * T, 768).rearrange("p (b n) -> p b n", b=2)
        gate, egate, tgate, mval = (
            area(K0 + 2 * T * i, 2 * T).rearrange("p (b t) -> p b t", b=2) for i in range(4))
        mq = area(8 * T, 8 * SEQ).rearrange("p (c t) -> p c t", t=SEQ)
        mk = area(8 * T + 8 * SEQ, 8 * SEQ).rearrange("p (c t) -> p c t", t=SEQ)
        sbq, sbk = q_all[:, 0:4, :], q_all[:, 4:8, :]
        L0 = 8 * T + 16 * SEQ
        zlog, nlk, ls = (area(L0 + 2048 + 768 * i, 768).rearrange("p (b n) -> p b n", b=2) for i in range(3))
        kro = area(L0 + 2048 + 2304, T)
        mprob = area(L0 + 2048 + 2304, 768).rearrange("p (b n) -> p b n", b=2)
        mprobT = area(L0 + 2048 + 2304 + 768, 768).rearrange("p (b n) -> p b n", b=2)
        msmall = area(L0 + 2048 + 2304 + 1536, 16)
        turned = area(L0 + 2048 + 2304 + 768, SEQ)
        lyb = area(L0 + 2048, 4 * T).rearrange("p (b t) -> p b t", b=4)
        lat = area(8 * T, 5 * T).rearrange("p (b t) -> p b t", b=5)
        latsq = area(8 * T + 5 * T, 5 * T).rearrange("p (b t) -> p b t", b=5)

        def const(name):
            a, b = CCOL[name]
            return c_t[:, a:b]

        def gain(name, m=0):
            return g_t[:, GCOL[name] + m:GCOL[name] + m + 1]

        def chunk_at(first, at, cols):
            w = cols.stop - cols.start
            if at.it is None:
                return scr[:, first + at.c * T + cols.start:first + at.c * T + cols.stop]
            return scr[:, bass.ds(at.it * (at.m * T) + (first + at.c * T + cols.start), w)]

        def hidden_at(t, at, cols):
            w = cols.stop - cols.start
            if at.it is None:
                return t[:, at.c * T + cols.start:at.c * T + cols.stop]
            return t[:, bass.ds(at.it * (at.m * T) + (at.c * T + cols.start), w)]

        bank = [ctx.enter_context(nc.psum_tensor(f"bank{i}", [P, 512], F32)) for i in range(8)]
        STAT = 4

        gains_loaded, consts_loaded, meta_loaded = sems("gains_loaded consts_loaded meta_loaded")
        x_loaded = sems("x_loaded0 x_loaded1 x_loaded2 x_loaded3")
        consts_cast, bias_set, stored = sems("consts_cast bias_set stored")
        w_loaded = sems("w_loaded0 w_loaded1 w_loaded2 w_loaded3")
        w_hi, w_lo, w_used, evac = sems("w_hi w_lo w_used evacuated")
        u_hi, u_lo, squares, acc_done, stat_ready, rstd_ready = sems(
            "u_hi u_lo squares acc_done stat_ready rstd_ready")
        u2_hi, u2_lo = sems("u2_hi u2_lo")
        two_gains_ready, meta_hi, meta_lo, meta_squares, x2_squares, x2_acc = sems(
            "two_gains_ready meta_hi meta_lo meta_squares x2_squares x2_acc")
        x2_factor, x2_mean, x2_log, x2_logs, x2_done = sems("x2_factor x2_mean x2_log x2_logs x2_done")
        e_ready, t_ready, a_hi, a_lo, a_sq = sems("e_ready t_ready a_hi a_lo a_sq")
        v_turned, v_stored = sems("v_turned v_stored")
        y_sq, y_stat, y_rstd, y_norm, y_rot, y_cos, y_sin, y_turned, y_done = sems(
            "y_sq y_stat y_rstd y_norm y_rot y_cos y_sin y_turned y_done")
        s_ready, s_max, p_exp, p_norm, pt_ready, pt_copied, o_ready, o_hi, o_lo = sems(
            "s_ready s_max p_exp p_norm pt_ready pt_copied o_ready o_hi o_lo")
        z_ready, z_log, z_split, z_masked, z_sum, z_arg, z_exp, z_w, z_o, z_ohi, z_olo = sems(
            "z_ready z_log z_split z_masked z_sum z_arg z_exp z_w z_o z_ohi z_olo")
        sel_loaded = sem("sel_loaded")
        rel_loaded = sems("rel_loaded0 rel_loaded1")
        lat_hi, lat_lo, lat_sq, lat_stat, lat_rstd, kr_rot, kr_done = sems(
            "lat_hi lat_lo lat_sq lat_stat lat_rstd kr_rot kr_done")
        m_rot, m_cos, m_sin, m_qdone, m_turned, m_vstored, m_kdone = sems(
            "m_rot m_cos m_sin m_qdone m_turned m_vstored m_kdone")
        wi_turned, wi_done, ix_ready, ix_relu, ix_acc, ix_mask, ix_clear = sems(
            "wi_turned wi_done ix_ready ix_relu ix_acc ix_mask ix_clear")
        f_exp, f_log, f_split = sems("f_exp f_log f_split")
        t_q, t_s, t_max, t_exp, t_p, t_pt, t_pts, t_o, t_ohi, t_olo = sems(
            "t_q t_s t_max t_exp t_p t_pt t_pts t_o t_ohi t_olo")
        dve_chain, act_chain = sems("dve_chain act_chain")

        FIRST, WHOLE = slice(META, T), slice(0, T)

        def width(cols):
            return cols.stop - cols.start

        def split_hi(act, n):
            s = n.mod(RING)
            act.wait_ge(w_loaded[s], (n.div(RING) + 1).times(16).value())
            if (n + (1 - RING)).c > 0:
                act.wait_ge(w_used, (n + (1 - RING)).value())
            act.activation(whi[:, s, :], raw[:, s, :], ACT.Copy).then_inc(w_hi, 1)

        def split_lo(dve, n):
            s = n.mod(RING)
            dve.wait_ge(w_hi, (n + 1).value())
            dve.tensor_tensor(wlo[:, s, :], raw[:, s, :], whi[:, s, :].bitcast(F32),
                              ALU.subtract).then_inc(w_lo, 1)

        def unit_mm(pe, n, dst, xhi, xlo, cols, chunks=DC, at=0, first=True, last=True, x=None, used=True):
            s = n.mod(RING)
            pe.wait_ge(w_lo, (n + 1).value())
            for i in range(chunks):
                if x is not None:
                    ready, count = x(i)
                    pe.wait_ge(ready, count)
                hi, lo = (w[:, s, (at + i) * P:(at + i + 1) * P] for w in (whi, wlo))
                a, b = xhi[:, i, cols], xlo[:, i, cols]
                pe.matmul(dst, hi, a, start=first and i == 0, stop=False)
                pe.matmul(dst, hi, b, start=False, stop=False)
                mm = pe.matmul(dst, lo, a, start=False, stop=last and i == chunks - 1)
            if used:
                mm.then_inc(w_used, 1)

        def u_chunk(norm):
            return lambda i: (u_lo, 8 * norm + i + 1)

        BETWEEN = 4

        def meta_act(act, m):
            if m == 0:
                act.wait_ge(meta_loaded, 16)
            x = h[:, m, 0:META]
            act.activation(uhi[:, m, 0:META], x, ACT.Copy, scale=gain("attn0", m)).then_inc(meta_hi, 1)
            act.activation(x2_sq[:, m, 0:META], x, ACT.Square).then_inc(meta_squares, 1)

        def meta_dve(dve, m):
            dve.wait_ge(meta_hi, m + 1)
            dve.scalar_tensor_tensor(out=ulo[:, m, 0:META], in0=h[:, m, 0:META], scalar=gain("attn0", m),
                                     in1=uhi[:, m, 0:META].bitcast(F32), op0=ALU.mult,
                                     op1=ALU.subtract).then_inc(meta_lo, 1)

        def u_gain(k, name, m):
            return two_gains[:, m:m + 1] if k == BETWEEN else gain(name, m)

        def norm_act(act, k, m, cols, name):
            if k == BETWEEN:
                if m == 0:
                    act.wait_ge(two_gains_ready, 1)
                    meta_act(act, 0)
                if m + 1 < DC:
                    meta_act(act, m + 1)
            act.activation(uhi[:, m, cols], h[:, m, cols], ACT.Copy, scale=u_gain(k, name, m)).then_inc(u_hi, 1)
            if m == 0 and k > 0:
                act.wait_ge(acc_done, 7 * k)
            act.activation(sq_all[:, m, cols], h[:, m, cols], ACT.Square).then_inc(squares, 1)
            if k == BETWEEN:
                act.activation(x2_sq[:, m, cols], h[:, m, cols], ACT.Square, scale=gain(name, m)).then_inc(x2_squares, 1)

        def norm_dve(dve, k, m, cols, name):
            if k == BETWEEN:
                for i in ((0, 1) if m == 0 else (m + 1,)):
                    if i < DC:
                        meta_dve(dve, i)
            dve.wait_ge(u_hi, 8 * k + m + 1)
            dve.scalar_tensor_tensor(out=ulo[:, m, cols], in0=h[:, m, cols], scalar=u_gain(k, name, m),
                                     in1=uhi[:, m, cols].bitcast(F32), op0=ALU.mult,
                                     op1=ALU.subtract).then_inc(u_lo, 1)

        def norm_pool(pool, k, cols):
            for m in range(1, DC):
                pool.wait_ge(squares, 8 * k + m + 1)
                if m == 1:
                    if k > 0:
                        pool.wait_ge(stat_ready, k)
                else:
                    pool.wait_ge(acc_done, 7 * k + m - 1)
                first = sq_all[:, 0, cols] if m == 1 else acc[:, cols]
                pool.tensor_tensor(acc[:, cols], first, sq_all[:, m, cols], ALU.add).then_inc(acc_done, 1)
                if k == BETWEEN:
                    pool.wait_ge(x2_squares, m + 1)
                    pool.wait_ge(meta_squares, m + 1)
                    if m > 1:
                        pool.wait_ge(x2_acc, m - 1)
                    first = x2_sq[:, 0, :] if m == 1 else x2_sum
                    pool.tensor_tensor(x2_sum, first, x2_sq[:, m, :], ALU.add).then_inc(x2_acc, 1)

        def norm_pe(pe, k, cols):
            pe.wait_ge(acc_done, 7 * (k + 1))
            if k > 0:
                pe.wait_ge(rstd_ready, k)
            if k == BETWEEN:
                pe.wait_ge(x2_acc, 7)
                pe.matmul(bank[5][:, 0:T], ones[:, :], x2_sum, start=True, stop=True)
                cols = FIRST
            pe.matmul(bank[STAT][:, 0:width(cols)], ones[:, :], acc[:, cols], start=True,
                      stop=True).then_inc(stat_ready, 1)

        def norm_rstd(act, link, k, cols):
            act.wait_ge(stat_ready, k + 1)
            if k > 0:
                act.wait_ge(rstd_ready, k)
            act.activation(lg[:, cols], bank[STAT][:, 0:width(cols)], ACT.Ln, scale=1.0 / D, bias=bias[:, 0:1]).then_inc(link.sem, 1)
            act.wait_ge(link.sem, link.next())
            if k != BETWEEN:
                act.activation(rstd[:, 0, cols], lg[:, cols], ACT.Exp, scale=-0.5).then_inc(rstd_ready, 1)
                return
            act.activation(x2_t[:, 0, FIRST], lg[:, FIRST], ACT.Exp, scale=-1.0).then_inc(x2_factor, 1)
            act.activation(rstd[:, 1, FIRST], lg[:, FIRST], ACT.Exp, scale=-0.5).then_inc(x2_factor, 1)
            act.wait_ge(x2_mean, 2)
            act.activation(x2_t[:, 2, :], x2_t[:, 1, :], ACT.Ln, scale=1.0 / D, bias=bias[:, 0:1]).then_inc(x2_log, 1)
            act.wait_ge(x2_logs, 1)
            act.activation(rstd[:, 0, :], x2_t[:, 2, :], ACT.Exp, scale=-0.5).then_inc(rstd_ready, 1)

        def between_dve(dve):
            dve.wait_ge(stat_ready, BETWEEN + 1)
            dve.tensor_copy(x2_t[:, 1, 0:META], bank[5][:, 0:META]).then_inc(x2_mean, 1)
            dve.wait_ge(x2_factor, 1)
            dve.tensor_tensor(x2_t[:, 1, FIRST], bank[5][:, FIRST], x2_t[:, 0, FIRST], ALU.mult).then_inc(x2_mean, 1)
            dve.wait_ge(x2_log, 1)
            dve.tensor_tensor(x2_t[:, 2, FIRST], x2_t[:, 2, FIRST], lg[:, FIRST], ALU.add).then_inc(x2_logs, 1)

        def x2_dve(dve):
            dve.wait_ge(x2_factor, 2)
            for m in range(DC):
                dve.scalar_tensor_tensor(out=h[:, m, FIRST], in0=h[:, m, FIRST], scalar=gain("final", m), in1=rstd[:, 1, FIRST],
                                         op0=ALU.mult, op1=ALU.mult).then_inc(x2_done, 1)

        def resid_pe(pe, name, kc, cols, x):
            per = -(-kc // DC)

            def group(it):
                n0, b0 = At(START[name], it, 4 * per), At(BSTART[name], it, 4)
                for j in range(4):
                    pe.wait_ge(evac, (b0 + (j - 3)).value())
                    dst = bank[(b0 + j).mod(4)][:, 0:width(cols)]
                    for u in range(per):
                        wait_x = it is None and j == 0
                        unit_mm(pe, n0 + (j * per + u), dst, ahi[:, u * DC:, :], alo[:, u * DC:, :], cols,
                                chunks=min(DC, kc - u * DC), first=u == 0, last=u == per - 1,
                                x=(lambda i, u=u: x(u * DC + i)) if wait_x else None)
            group(None)
            with pe.Fori(1, DC // 4) as it:
                group(it)

        def resid_act(act, link, name, kc, cols, norm, gname):
            per = -(-kc // DC)
            for m in range(DC + 1):
                for u in range(per if m < DC else 1):
                    if m < DC:
                        split_hi(act, At(START[name] + m * per + u + AHEAD))
                    if u == 0 and m > 0 and gname is not None:
                        act.wait_ge(evac, BSTART[name] + m)
                        norm_act(act, norm, m - 1, cols, gname)
            if norm is not None:
                norm_rstd(act, link, norm, cols)

        def resid_dve(dve, name, kc, cols, norm, gname):
            per = -(-kc // DC)
            for m in range(DC):
                for u in range(per):
                    split_lo(dve, At(START[name] + m * per + u + AHEAD))
                    if m > 0 and u == 0 and gname is not None:
                        norm_dve(dve, norm, m - 1, cols, gname)
                b = BSTART[name] + m
                dve.wait_ge(w_used, START[name] + (m + 1) * per)
                dve.tensor_tensor(h[:, m, cols], bank[b % 4][:, 0:width(cols)], h[:, m, cols],
                                  ALU.add).then_inc(evac, 1)
            if gname is not None:
                norm_dve(dve, norm, DC - 1, cols, gname)

        def hidden_pe(pe, name, cols, norm, groups):
            def group(it):
                n0, b0 = At(START[name], it, 4), At(BSTART[name], it, 4)
                for j in range(4):
                    pe.wait_ge(evac, (b0 + (j - 3)).value())
                    unit_mm(pe, n0 + j, bank[(b0 + j).mod(4)][:, 0:width(cols)], uhi, ulo, cols,
                            x=u_chunk(norm) if it is None and j == 0 else None)
                    if it is None and j == 0:
                        norm_pe(pe, norm, cols)
            group(None)
            with pe.Fori(1, groups) as it:
                group(it)

        def swiglu_pe(pe, name, cols, norm):
            hidden_pe(pe, name, cols, norm, FC1 // 2)

        def swiglu_act(act, link, name, cols):
            with act.Fori(0, FC1 // 2) as it:
                link.enter(it, 4)
                n0, b0 = At(START[name], it, 4), At(BSTART[name], it, 4)
                for j in range(2):
                    split_hi(act, n0 + (2 * j + AHEAD))
                    act.wait_ge(evac, (b0 + (2 * j + 1)).value())
                    e = egate[:, j, cols]
                    act.activation(e, gate[:, j, cols], ACT.Exp, scale=-1.0).then_inc(link.sem, 1)
                    act.wait_ge(link.sem, link.next())
                    act.activation(e, e, ACT.Ln, bias=bias[:, 1:2]).then_inc(link.sem, 1)
                    act.wait_ge(link.sem, link.next())
                    act.activation(e, e, ACT.Exp, scale=-1.0).then_inc(e_ready, 1)
                    split_hi(act, n0 + (2 * j + 1 + AHEAD))
                    act.wait_ge(evac, (b0 + (2 * j + 2)).value())
                    act.activation(hidden_at(ahi_t, At(j, it, 2), cols), mval[:, j, cols], ACT.Copy).then_inc(a_hi, 1)
                link.leave(FC1 // 2)

        def swiglu_dve(dve, name, cols, norm, i0):
            dve.wait_ge(rstd_ready, norm + 1)
            with dve.Fori(0, FC1 // 2) as it:
                n0, b0 = At(START[name], it, 4), At(BSTART[name], it, 4)
                for j in range(2):
                    i = At(i0 + j, it, 2)
                    dve.wait_ge(w_used, (n0 + (2 * j + 1)).value())
                    dve.tensor_tensor(gate[:, j, cols], bank[(b0 + 2 * j).mod(4)][:, 0:width(cols)],
                                      rstd[:, 0, cols], ALU.mult).then_inc(evac, 1)
                    split_lo(dve, n0 + (2 * j + AHEAD))
                    dve.wait_ge(w_used, (n0 + (2 * j + 2)).value())
                    dve.wait_ge(t_ready, (i + 1).times(2).value())
                    dve.tensor_tensor(mval[:, j, cols], bank[(b0 + 2 * j + 1).mod(4)][:, 0:width(cols)],
                                      tgate[:, j, cols], ALU.mult).then_inc(evac, 1)
                    split_lo(dve, n0 + (2 * j + 1 + AHEAD))

        def swiglu_pool(pool, name, cols, norm, i0):
            pool.wait_ge(rstd_ready, norm + 1)
            with pool.Fori(0, FC1 // 2) as it:
                for j in range(2):
                    i = At(i0 + j, it, 2)
                    pool.wait_ge(e_ready, (i + 1).value())
                    pool.tensor_tensor(tgate[:, j, cols], gate[:, j, cols], egate[:, j, cols], ALU.mult).then_inc(t_ready, 1)
                    pool.wait_ge(t_ready, (i.times(2) + 1).value())
                    pool.tensor_tensor(tgate[:, j, cols], tgate[:, j, cols], rstd[:, 0, cols], ALU.mult).then_inc(t_ready, 1)
                    pool.wait_ge(a_hi, (i + 1).value())
                    pool.tensor_tensor(hidden_at(alo_t, At(j, it, 2), cols), mval[:, j, cols],
                                       hidden_at(ahi_t, At(j, it, 2), cols).bitcast(F32), ALU.subtract).then_inc(a_lo, 1)

        def sqrelu_pe(pe, name, cols, norm):
            hidden_pe(pe, name, cols, norm, FC2 // 4)

        def sqrelu_act(act, name, cols):
            with act.Fori(0, FC2 // 4) as it:
                n0, b0 = At(START[name], it, 4), At(BSTART[name], it, 4)
                for j in range(4):
                    split_hi(act, n0 + (j + AHEAD))
                    act.wait_ge(evac, (b0 + (j + 1)).value())
                    act.activation(hidden_at(ahi_t, At(j, it, 4), cols), gate[:, j % 2, cols], ACT.Square).then_inc(a_hi, 1)

        def sqrelu_dve(dve, name, cols, norm, i0):
            dve.wait_ge(rstd_ready, norm + 1)
            with dve.Fori(0, FC2 // 4) as it:
                n0, b0 = At(START[name], it, 4), At(BSTART[name], it, 4)
                for j in range(4):
                    i = At(i0 + j, it, 4)
                    dve.wait_ge(w_used, (n0 + (j + 1)).value())
                    dve.wait_ge(a_lo, (i + (-1)).value())
                    dve.scalar_tensor_tensor(out=gate[:, j % 2, cols], in0=bank[(b0 + j).mod(4)][:, 0:width(cols)],
                                             scalar=0.0, in1=rstd[:, 0, cols], op0=ALU.max,
                                             op1=ALU.mult).then_inc(evac, 1)
                    split_lo(dve, n0 + (j + AHEAD))

        def sqrelu_pool(pool, name, cols, i0, k0):
            with pool.Fori(0, FC2 // 4) as it:
                b0 = At(BSTART[name], it, 4)
                for j in range(4):
                    i, k = At(i0 + j, it, 4), At(k0 + j, it, 4)
                    pool.wait_ge(evac, (b0 + (j + 1)).value())
                    pool.tensor_tensor(mval[:, j % 2, cols], gate[:, j % 2, cols], gate[:, j % 2, cols],
                                       ALU.mult).then_inc(a_sq, 1)
                    pool.wait_ge(a_sq, (k + 1).value())
                    pool.wait_ge(a_hi, (i + 1).value())
                    pool.tensor_tensor(hidden_at(alo_t, At(j, it, 4), cols), mval[:, j % 2, cols],
                                       hidden_at(ahi_t, At(j, it, 4), cols).bitcast(F32), ALU.subtract).then_inc(a_lo, 1)

        VFIRST = {"sv": 0, "bv": 4, "dv": 12, "fv": 14}
        RFIRST = {"dk": 0, "dq": 4, "fk": 12, "fq": 20}
        OFIRST = {"ki": 0, "qi": 1, "dk": 5, "dq": 9, "fk": 0, "fq": 8}
        VTILES = {"sv": (META, META + 128, None), "bv": (META, META + 128, None), "dv": (0, 128, 256), "fv": (META, META + 128, 0)}
        COUNT = dict(PHASES)

        def in_groups(eng, name, kind, body):
            n = COUNT[name]
            if kind != "plain" or n <= 4:
                body(At(0), n, None, 1)
            else:
                with eng.Fori(0, n // 4) as it:
                    body(At(0, it, 4), 4, it, n // 4)

        def early_unit_pe(pe, name, j, cols, second=False):
            b = BSTART[name] + j
            xhi, xlo = (ahi[:, DC:, :], alo[:, DC:, :]) if second else (uhi, ulo)
            pe.wait_ge(evac, b - 3)
            unit_mm(pe, At(START[name] + j), bank[b % 4][:, 0:width(cols)], xhi, xlo, cols,
                    x=(lambda i: (u2_lo, i + 1)) if second and j == 0 else None)

        def proj_pe(pe, name, kind, cols, norm, second=False, sum_norm=None, meanwhile=(), done=0):
            xhi, xlo = (ahi[:, DC:, :], alo[:, DC:, :]) if second else (uhi, ulo)
            ready = (lambda i: (u2_lo, i + 1)) if second else u_chunk(norm)
            vy = lyb if name == "sv" else yb
            n_cols = width(cols)

            def body(g, k, it, trips):
                def turn(j):
                    v = g + (VFIRST[name] + j)
                    pe.wait_ge(evac, (g + (BSTART[name] + j + 1)).value())
                    if (v + (-1)).c > 0:
                        pe.wait_ge(v_stored, (v + (-1)).value())
                    t0, t1, ta = VTILES[name]
                    dst = bank[5 + j % 2]
                    if ta is not None:
                        pe.transpose(dst[0:META, 256:384], vy[:, j % 4, ta:ta + META], const("ident"))
                    pe.transpose(dst[:, 0:128], vy[:, j % 4, t0:t0 + 128], const("ident"))
                    pe.transpose(dst[:, 128:256], vy[:, j % 4, t1:t1 + 128], const("ident")).then_inc(v_turned, 1)

                def stat(j):
                    r = g + (RFIRST[name] + j)
                    pe.wait_ge(y_sq, (r + 1).value())
                    if (r + (-1)).c > 0:
                        pe.wait_ge(y_rstd, (r + (-1)).value())
                    pe.matmul(bank[5 + j % 2][:, 0:n_cols], const("headones"), ysq[:, j % 2, cols],
                              start=True, stop=True).then_inc(y_stat, 1)

                def rot(j):
                    o = g + (OFIRST[name] + j)
                    if kind == "rope":
                        pe.wait_ge(evac, (g + (BSTART[name] + j + 1)).value())
                    else:
                        pe.wait_ge(y_norm, (g + (RFIRST[name] + j + 1)).value())
                    if o.c > 0:
                        pe.wait_ge(y_sin, o.value())
                    src = yb[:, (OFIRST[name] + j) % 4, cols] if kind == "rope" else y2[:, j % 2, cols]
                    pe.matmul(bank[7][:, 0:n_cols], const("rot"), src, start=True, stop=True).then_inc(y_rot, 1)

                for j in range(k):
                    b = g + (BSTART[name] + j)
                    if it is not None or j >= done:
                        pe.wait_ge(evac, (b + (-3)).value())
                        unit_mm(pe, g + (START[name] + j), bank[b.mod(4)][:, 0:n_cols], xhi, xlo, cols,
                                x=ready if j == 0 else None)
                    if sum_norm is not None and it is None and j == 0:
                        norm_pe(pe, sum_norm, cols)
                    if kind == "v" and j >= 1:
                        turn(j - 1)
                    if "rms" in kind and j >= 1:
                        stat(j - 1)
                    if "rope" in kind and j >= 2:
                        rot(j - 2)
                for early in meanwhile[0:1]:
                    early_unit_pe(pe, *early)
                if kind == "v":
                    turn(k - 1)
                if "rms" in kind:
                    stat(k - 1)
                if "rope" in kind and k >= 2:
                    rot(k - 2)
                for early in meanwhile[1:2]:
                    early_unit_pe(pe, *early)
                if "rope" in kind:
                    rot(k - 1)
                for early in meanwhile[2:3]:
                    early_unit_pe(pe, *early)
            in_groups(pe, name, kind, body)

        def proj_act(act, link, name, kind, cols, between=None):
            n_cols = width(cols)

            def body(g, k, it, trips):
                def rms(j):
                    act.wait_ge(y_stat, (g + (RFIRST[name] + j + 1)).value())
                    if kind == "rms":
                        if (g + (OFIRST[name] + j - 1)).c > 0:
                            act.wait_ge(y_done, (g + (OFIRST[name] + j - 1)).value())
                    else:
                        if (g + (RFIRST[name] + j - 1)).c > 0:
                            act.wait_ge(y_norm, (g + (RFIRST[name] + j - 1)).value())
                    if (g + (RFIRST[name] + j)).c > 0:
                        act.wait_ge(y_rstd, (g + (RFIRST[name] + j)).value())
                    act.activation(lg[:, cols], bank[5 + j % 2][:, 0:n_cols], ACT.Ln, scale=1.0 / HD, bias=bias[:, 0:1]).then_inc(link.sem, 1)
                    act.wait_ge(link.sem, link.next())
                    act.activation(hr[:, j % 2, cols], lg[:, cols], ACT.Exp, scale=-0.5).then_inc(y_rstd, 1)

                def store_v(j):
                    act.wait_ge(v_turned, (g + (VFIRST[name] + j + 1)).value())
                    if VTILES[name][2] is not None:
                        act.activation(v_cols(g + j, 256, 128, META), bank[5 + j % 2][0:META, 256:384], ACT.Copy).then_inc(link.sem, 1)
                        act.wait_ge(link.sem, link.next())
                    dst = v_cols(g + j, 0, 256, P) if name != "sv" else mv_cols(g + j)
                    act.activation(dst, bank[5 + j % 2][:, 0:256], ACT.Copy).then_inc(v_stored, 1)

                for j in range(k):
                    split_hi(act, g + (START[name] + j + AHEAD))
                    if "rms" in kind:
                        act.wait_ge(evac, (g + (BSTART[name] + j + 1)).value())
                        if (g + (RFIRST[name] + j - 1)).c > 0:
                            act.wait_ge(y_stat, (g + (RFIRST[name] + j - 1)).value())
                        act.activation(ysq[:, j % 2, cols], yb[:, j % 4, cols], ACT.Square).then_inc(y_sq, 1)
                        if j >= 1:
                            rms(j - 1)
                    if kind == "v" and j >= 1:
                        store_v(j - 1)
                    if between is not None:
                        between(j)
                if "rms" in kind:
                    rms(k - 1)
                if kind == "v":
                    store_v(k - 1)
            in_groups(act, name, kind, body)

        def v_cols(at, off, w, rows):
            if at.it is None:
                return scr[0:rows, V0 + at.c * 384 + off:V0 + at.c * 384 + off + w]
            return scr[0:rows, bass.ds(at.it * (at.m * 384) + (V0 + at.c * 384 + off), w)]

        def mv_cols(at):
            return scr[:, L0 + at.c * 256:L0 + at.c * 256 + 256]

        def proj_dve(dve, link, name, kind, cols, first=None, scale=1.0, gcol=None, norm=0, between=None):
            n_cols = width(cols)
            vy = lyb if name == "sv" else yb
            dve.wait_ge(rstd_ready, norm + 1)

            def body(g, k, it, trips):
                def normed(j):
                    r = g + (RFIRST[name] + j)
                    dve.wait_ge(y_rstd, (r + 1).value())
                    if kind == "rms":
                        dst, done = chunk_at(first, g + j, cols), y_done
                    else:
                        dst, done = y2[:, j % 2, cols], y_norm
                        dve.wait_ge(y_rot, (g + (OFIRST[name] + j - 1)).value())
                        dve.wait_ge(y_cos, (g + (OFIRST[name] + j - 1)).value())
                    dve.scalar_tensor_tensor(out=dst, in0=yb[:, j % 4, cols], scalar=gcol, in1=hr[:, j % 2, cols],
                                             op0=ALU.mult, op1=ALU.mult).then_inc(done, 1)

                def rotated(j):
                    o = g + (OFIRST[name] + j)
                    dst = chunk_at(first, g + j, cols)
                    dve.wait_ge(y_rot, (o + 1).value())
                    dve.tensor_tensor(dst, bank[7][:, 0:n_cols], const("sin")[:, cols], ALU.mult).then_inc(y_sin, 1)

                for j in range(k):
                    b = g + (BSTART[name] + j)
                    dve.wait_ge(w_used, (g + (START[name] + j + 1)).value())
                    src = bank[b.mod(4)][:, 0:n_cols]
                    if kind == "plain":
                        dve.scalar_tensor_tensor(out=chunk_at(first, g + j, cols), in0=src, scalar=scale, in1=rstd[:, 0, cols],
                                                 op0=ALU.mult, op1=ALU.mult).then_inc(evac, 1)
                        split_lo(dve, g + (START[name] + j + AHEAD))
                        continue
                    if kind == "v":
                        if (g + (VFIRST[name] + j - 3)).c > 0:
                            dve.wait_ge(v_turned, (g + (VFIRST[name] + j - 3)).value())
                        dst = vy[:, j % 4, cols]
                    elif kind == "rope":
                        if (g + (OFIRST[name] + j - 3)).c > 0:
                            dve.wait_ge(y_rot, (g + (OFIRST[name] + j - 3)).value())
                        if (g + (OFIRST[name] + j - 3)).c > 0:
                            dve.wait_ge(y_cos, (g + (OFIRST[name] + j - 3)).value())
                        dst = yb[:, (OFIRST[name] + j) % 4, cols]
                    else:
                        if (g + (RFIRST[name] + j - 3)).c > 0:
                            dve.wait_ge(y_sq, (g + (RFIRST[name] + j - 3)).value())
                        dst = yb[:, j % 4, cols]
                    dve.tensor_tensor(dst, src, rstd[:, 0, cols], ALU.mult).then_inc(evac, 1)
                    split_lo(dve, g + (START[name] + j + AHEAD))
                    if "rms" in kind and j >= 1:
                        normed(j - 1)
                    if "rope" in kind and j >= 2:
                        rotated(j - 2)
                    if between is not None:
                        between(g.c + j)
                if "rms" in kind:
                    normed(k - 1)
                if "rope" in kind:
                    for j in range(max(0, k - 2), k):
                        rotated(j)
            in_groups(dve, name, kind, body)

        def proj_pool(pool, name, kind, cols, first):
            def add(j):
                o = OFIRST[name] + j
                pool.wait_ge(y_sin, o + 1)
                pool.wait_ge(y_cos, o + 1)
                dst = chunk_at(first, At(j), cols)
                pool.tensor_tensor(dst, dst, mc[:, o % 2, cols], ALU.add).then_inc(y_turned, 1)

            k = COUNT[name]
            for j in range(k):
                o = OFIRST[name] + j
                if j >= 2:
                    add(j - 2)
                if kind == "rope":
                    pool.wait_ge(evac, BSTART[name] + j + 1)
                else:
                    pool.wait_ge(y_norm, RFIRST[name] + j + 1)
                if o >= 2:
                    pool.wait_ge(y_turned, o - 1)
                src = yb[:, o % 4, cols] if kind == "rope" else y2[:, j % 2, cols]
                pool.tensor_tensor(mc[:, o % 2, cols], src, const("cos")[:, cols], ALU.mult).then_inc(y_cos, 1)
            for j in range(max(0, k - 2), k):
                add(j)

        class Heads:
            def __init__(self, name, head0, pairs, pre, q, k, v, va, add, chunk0, cols, p, pt, sm, obanks=2):
                self.name, self.head0, self.pairs, self.pre = name, head0, pairs, pre
                self.q, self.k, self.v, self.va, self.add = q, k, v, va, add
                self.chunk0, self.cols, self.p, self.pt, self.obanks = chunk0, cols, p, pt, obanks
                self.nmx = sm[:, 0:4].rearrange("p (b n) -> p b n", b=2)
                self.ssum = sm[:, 4:8].rearrange("p (b n) -> p b n", b=2)
                self.rinv = sm[:, 8:12].rearrange("p (b n) -> p b n", b=2)
                self.w0, self.w1 = pre + 128, pre + 256

        def scores_pe(pe, a, i):
            hd, s = a.head0 + i, bank[4 + i % 2]
            if 2 * (hd - 1) > 0:
                pe.wait_ge(p_exp, 2 * (hd - 1))
            if a.name == "mla":
                pe.wait_ge(m_qdone, i + 1)
                pe.wait_ge(m_kdone, 1 if i == 0 else 8)
            if a.name == "dsa":
                pe.wait_ge(y_turned, OFIRST["dq"] + i // 2 + 1)
            q, k = a.q(i), a.k(i)
            more = a.add is not None
            pe.matmul(s[:, 0:a.w0], q[:, 0:128], k[:, 0:a.w0], start=True, stop=not more, skip_group_check=True)
            mm = pe.matmul(s[:, a.w0:a.w0 + a.w1], q[:, 128:256], k[:, 0:a.w1], start=not more, stop=not more, skip_group_check=True)
            if more:
                mm = a.add(pe, i, s)
            mm.then_inc(s_ready, 1)

        def turn_pe(pe, a, i):
            hd, p, dst = a.head0 + i, a.p[:, i % 2, :], bank[6 + i % 2]
            pe.wait_ge(p_norm, 2 * (hd + 1))
            if hd - 1 > 0:
                pe.wait_ge(pt_copied, hd - 1)
            idn = const("ident")
            c0, c1 = a.pre, a.w0 + a.pre
            if a.pre:
                pe.transpose(bank[2 + i % 2][0:a.pre, 0:128], p[:, 0:a.pre], idn)
                pe.transpose(bank[2 + i % 2][0:a.pre, 128:256], p[:, a.w0:a.w0 + a.pre], idn)
            pe.transpose(dst[:, 0:128], p[:, c0:c0 + 128], idn)
            pe.transpose(dst[:, 128:256], p[:, c1:c1 + 128], idn)
            pe.transpose(dst[:, 256:384], p[:, c1 + 128:c1 + 256], idn).then_inc(pt_ready, 1)

        def values_pe(pe, a, s):
            pr = a.head0 // 2 + s
            o = bank[pr % a.obanks]
            if pr + 1 - a.obanks > 0:
                pe.wait_ge(o_lo, pr + 1 - a.obanks)
            for i in (2 * s, 2 * s + 1):
                pe.wait_ge(pt_copied, a.head0 + i + 1)
                dst, pt = o[64 * (i % 2):64 * (i % 2) + 64, :], a.pt[:, i % 2, :]
                if a.pre:
                    pe.matmul(dst[:, 0:256], a.va(i), probTA[0:META, i % 2, :], start=True, stop=False, skip_group_check=True)
                pe.matmul(dst[:, 0:256], a.v(i, 0), pt[:, 0:256], start=not a.pre, stop=False, skip_group_check=True)
                mm = pe.matmul(dst[:, 128:256], a.v(i, 1), pt[:, 256:384], start=False, stop=True, skip_group_check=True)
            mm.then_inc(o_ready, 1)

        def att_pe(pe, a, hook=None):
            for s in range(a.pairs + 2):
                if hook:
                    hook(0, s)
                for i in (2 * s, 2 * s + 1):
                    if s < a.pairs:
                        scores_pe(pe, a, i)
                    if s >= 2 and i % 2 == 0:
                        values_pe(pe, a, s - 2)
                    if 1 <= s <= a.pairs:
                        turn_pe(pe, a, i - 2)
                if hook:
                    hook(1, s)

        def att_act(act, link, a, hook=None):
            for s in range(a.pairs + 2):
                if hook:
                    hook(0, s)
                if s >= 2:
                    pr = a.head0 // 2 + s - 2
                    act.wait_ge(o_ready, pr + 1)
                    act.activation(ahi[:, a.chunk0 + s - 2, a.cols], bank[pr % a.obanks][:, 0:256], ACT.Copy).then_inc(o_hi, 1)
                for i in (2 * s, 2 * s + 1):
                    if s < a.pairs:
                        hd, sc = a.head0 + i, bank[4 + i % 2]
                        act.wait_ge(s_max, 2 * (hd + 1))
                        if hd - 1 > 0:
                            act.wait_ge(pt_ready, hd - 1)
                        for t, (c0, w) in enumerate(((0, a.w0), (a.w0, a.w1))):
                            act.activation(a.p[:, i % 2, c0:c0 + w], sc[:, c0:c0 + w], ACT.Exp, bias=a.nmx[:, i % 2, t:t + 1],
                                           accum_out=a.ssum[:, i % 2, t:t + 1]).then_inc(p_exp, 1)
                    if 1 <= s <= a.pairs:
                        hd = a.head0 + i - 2
                        act.wait_ge(pt_ready, hd + 1)
                        if a.head0 // 2 + s - 1 > 0:
                            act.wait_ge(o_ready, a.head0 // 2 + s - 1)
                        if a.pre:
                            act.activation(probTA[0:a.pre, i % 2, :], bank[2 + i % 2][0:a.pre, 0:256], ACT.Copy).then_inc(link.sem, 1)
                            act.wait_ge(link.sem, link.next())
                        act.activation(a.pt[:, i % 2, 0:384], bank[6 + i % 2][:, 0:384], ACT.Copy).then_inc(pt_copied, 1)
                if hook:
                    hook(1, s)

        def att_dve(dve, link, a, hook=None):
            for s in range(a.pairs + 2):
                if hook:
                    hook(0, s)
                for i in (2 * s, 2 * s + 1):
                    if s < a.pairs:
                        sc = bank[4 + i % 2]
                        dve.wait_ge(s_ready, a.head0 + i + 1)
                        for t, (c0, w) in enumerate(((0, a.w0), (a.w0, a.w1))):
                            dve.tensor_reduce(a.nmx[:, i % 2, t:t + 1], sc[:, c0:c0 + w], AX.X, ALU.max,
                                              negate=True).then_inc(s_max, 1)
                    if s >= 2 and i % 2 == 0:
                        out_lo(dve, a, s - 2)
                if s < a.pairs:
                    for i in (2 * s, 2 * s + 1):
                        dve.wait_ge(p_exp, 2 * (a.head0 + i + 1))
                        dve.reciprocal(a.rinv[:, i % 2, :], a.ssum[:, i % 2, :]).then_inc(link.sem, 1)
                        dve.wait_ge(link.sem, link.next())
                        for t, (c0, w) in enumerate(((0, a.w0), (a.w0, a.w1))):
                            p = a.p[:, i % 2, c0:c0 + w]
                            dve.tensor_scalar(p, p, a.rinv[:, i % 2, t:t + 1], None, ALU.mult).then_inc(p_norm, 1)
                if hook:
                    hook(1, s)

        def out_lo(dve, a, s):
            pr = a.head0 // 2 + s
            dve.wait_ge(o_hi, pr + 1)
            dst = a.chunk0 + s
            dve.tensor_tensor(alo[:, dst, a.cols], bank[pr % a.obanks][:, 0:256], ahi[:, dst, a.cols].bitcast(F32),
                              ALU.subtract).then_inc(o_lo, 1)

        def half(ap, i):
            return ap[64 * (i % 2):64 * (i % 2) + 64]

        def v_of(i, tile, rows=P):
            c = V0 + (i // 2) * 384 + tile * 128 + 64 * (i % 2)
            return scr[0:rows, c:c + 64]

        def late_mask(pe, s):
            pe.matmul(s[:, 64:128], upperb, lateb, start=False, stop=True, skip_group_check=True)
            return pe.matmul(s[:, 128 + 192:128 + 256], upperb, lateb, start=False, stop=True, skip_group_check=True)

        def band_add(pe, i, s):
            pe.wait_ge(rel_loaded[i // 2 % 2], 16 * (i // 4 + 1))
            b, rev = relb[:, (i // 2) % 2, i % 2, :], const("rev")
            pe.matmul(s[:, 0:128], b[:, 0:128], rev, start=False, stop=False, skip_group_check=True)
            pe.matmul(s[:, 128:256], b[:, 128:256], rev, start=False, stop=False, skip_group_check=True)
            pe.matmul(s[:, 256:384], b[:, 0:128], rev, start=False, stop=False, skip_group_check=True)
            return late_mask(pe, s)

        def fox_add(pe, i, s):
            pe.matmul(s[:, 0:144], selb[0:96, i, :], csplit[0:96, 0:144], start=False, stop=False, skip_group_check=True)
            pe.matmul(s[:, 144:416], selb[0:96, i, :], csplit[0:96, 0:272], start=False, stop=False, skip_group_check=True)
            pe.matmul(s[:, 16:144], identb[:, :], causalb[:, :], start=False, stop=True, skip_group_check=True)
            return pe.matmul(s[:, 144 + 144:416], identb[:, :], causalb[:, :], start=False, stop=True, skip_group_check=True)

        def dsa_add(pe, i, s):
            pe.matmul(s[:, 0:128], identb[:, :], selmask[:, 0:128], start=False, stop=True, skip_group_check=True)
            return pe.matmul(s[:, 128:384], identb[:, :], selmask[:, 128:384], start=False, stop=True, skip_group_check=True)

        mla = Heads("mla", 0, 4, 0, lambda i: mq[0:96, i, :], lambda i: mk[0:96, i, :],
                    lambda i, t: scr[:, L0 + (4 + i // 2) * 256 + t * 128 + 64 * (i % 2):][:, 0:64], None,
                    lambda pe, i, s: late_mask(pe, s), 0, FIRST, mprob, mprobT, msmall, obanks=1)
        band = Heads("band", 8, 8, 0, lambda i: half(q_all[:, i // 2, FIRST], i), lambda i: half(k_all[:, i // 2, FIRST], i),
                     v_of, None, band_add, 0, FIRST, prob, probT, small)
        dsa = Heads("dsa", 24, 8, 0, lambda i: half(q_all[:, i // 2, 0:256], i), lambda i: half(k_all[:, i // 4, 0:256], i),
                    lambda i, t: scr[:, V0 + (i // 8) * 384 + t * 128 + 64 * ((i // 4) % 2):][:, 0:64], None,
                    dsa_add, 0, slice(0, 256), prob, probT, small, obanks=1)
        fox = Heads("fox", 40, 8, META, lambda i: half(q_all[:, i // 2, FIRST], i), lambda i: half(k_all[:, i // 2, WHOLE], i),
                    v_of, lambda i: v_of(i, 2, META), fox_add, 0, FIRST, prob, probT, small)

        SCALE_A = (NOPE + ROPE) ** -0.5

        def first_pe(pe):
            for i in range(QC + KVC + 1):
                if i - 3 > 0:
                    pe.wait_ge(evac, i - 3)
                unit_mm(pe, At(i), bank[i % 4][:, 0:SEQ], uhi, ulo, FIRST, x=u_chunk(0) if i == 0 else None)
                if i == 0:
                    norm_pe(pe, 0, FIRST)
            pe.wait_ge(consts_loaded, 16)
            for s, (a, k) in enumerate(((0, QC), (QC, KVC))):
                pe.wait_ge(lat_sq, a + k)
                for i in range(k):
                    mm = pe.matmul(bank[5 + s][:, 0:SEQ], ones[:, :], latsq[:, a + i, FIRST], start=i == 0, stop=i == k - 1)
                mm.then_inc(lat_stat, 1)
            pe.wait_ge(evac, BSTART["kr"] + 1)
            pe.matmul(bank[7][:, 0:SEQ], const("rotm"), lyb[:, 0, FIRST], start=True, stop=True).then_inc(kr_rot, 1)
            pe.wait_ge(lat_rstd, 2)
            pe.wait_ge(kr_done, 1)
            proj_pe(pe, "sv", "v", FIRST, 0)
            proj_pe(pe, "sq", "plain", FIRST, 0)
            proj_pe(pe, "sk", "plain", FIRST, 0)
            pe.wait_ge(v_stored, 4)
            pe.wait_ge(lat_lo, QC + KVC)

            def turn_and_rotate(i):
                b = BSTART["mla"] + 2 * i
                pe.wait_ge(evac, b + 1)
                if i > 0:
                    pe.wait_ge(m_sin, i)
                pe.matmul(bank[7][:, 0:SEQ], const("rotm"), mq[:, i, :], start=True, stop=True).then_inc(m_rot, 1)
                pe.wait_ge(evac, b + 2)
                if i - 1 > 0:
                    pe.wait_ge(m_vstored, i - 1)
                for t in range(2):
                    mm = pe.transpose(bank[5 + i % 2][:, 64 * t:64 * t + 64], mk[64:128, i, 128 * t:128 * t + 128],
                                      const("ident")[64:128, 64:128])
                mm.then_inc(m_turned, 1)

            stick = stick_pe(pe)
            pe.wait_ge(rstd_ready, 1)
            for i in range(8):
                b, n = BSTART["mla"] + 2 * i, At(START["mla"] + i)
                pe.wait_ge(evac, b)
                if i % 2 == 0:
                    stick(0, i // 2)
                unit_mm(pe, n, bank[0][:, 0:SEQ], ahi[:, 16:, :], alo[:, 16:, :], FIRST, chunks=QC, used=False)
                unit_mm(pe, n, bank[4][:, 0:SEQ], ahi[:, 16 + QC:, :], alo[:, 16 + QC:, :], FIRST, chunks=KVC, at=QC)
                if i:
                    turn_and_rotate(i - 1)
                if i % 2 == 0:
                    stick(1, i // 2)
            turn_and_rotate(7)

        def first_act(act, link):
            act.wait_ge(gains_loaded, 16)
            act.wait_ge(bias_set, 3)
            for m in range(DC):
                if m % 2 == 0:
                    act.wait_ge(x_loaded[m // 2], 16)
                if m >= 5:
                    split_hi(act, At(m - 5))
                norm_act(act, 0, m, FIRST, "mix0")
            norm_rstd(act, link, 0, FIRST)
            for i in range(QC + KVC + 1):
                split_hi(act, At(i + AHEAD))
                if i < QC + KVC:
                    act.wait_ge(evac, i + 1)
                    act.activation(latsq[:, i, FIRST], lat[:, i, FIRST], ACT.Square).then_inc(lat_sq, 1)
                    g = gain("cq", i) if i < QC else gain("ckv", i - QC)
                    act.activation(ahi[:, 16 + i, FIRST], lat[:, i, FIRST], ACT.Copy, scale=g).then_inc(lat_hi, 1)
            for s, w in enumerate((QL, KVL)):
                act.wait_ge(lat_stat, s + 1)
                act.wait_ge(rstd_ready, 1)
                if s > 0:
                    act.wait_ge(lat_rstd, s)
                act.activation(lg[:, FIRST], bank[5 + s][:, 0:SEQ], ACT.Ln, scale=1.0 / w, bias=bias[:, 0:1]).then_inc(link.sem, 1)
                act.wait_ge(link.sem, link.next())
                act.activation(rstd[:, 1 + s, FIRST], lg[:, FIRST], ACT.Exp, scale=-0.5).then_inc(lat_rstd, 1)
            proj_act(act, link, "sv", "v", FIRST)
            proj_act(act, link, "sq", "plain", FIRST)
            proj_act(act, link, "sk", "plain", FIRST)

            def store(i):
                act.wait_ge(m_turned, i + 1)
                c = L0 + (4 + i // 2) * 256 + 64 * (i % 2)
                for t in range(2):
                    ins = act.activation(scr[:, c + 128 * t:c + 128 * t + 64], bank[5 + i % 2][:, 64 * t:64 * t + 64], ACT.Copy)
                ins.then_inc(m_vstored, 1)
                act.wait_ge(kr_done, 1)
                act.activation(mk[64:96, i, :], kro[64:96, FIRST], ACT.Copy).then_inc(m_kdone, 1)

            stick = stick_act(act, link)
            for i in range(8):
                if i % 2 == 0:
                    stick(0, i // 2)
                split_hi(act, At(START["mla"] + i + AHEAD))
                if i:
                    store(i - 1)
                if i % 2 == 0:
                    stick(1, i // 2)
            store(7)

        def first_dve(dve, link):
            for m in range(DC):
                norm_dve(dve, 0, m, FIRST, "mix0")
                if m >= DC - AHEAD:
                    split_lo(dve, At(m - (DC - AHEAD)))
            dve.tensor_tensor(two_gains[:, :], g_t[:, GCOL["final"]:GCOL["final"] + DC], g_t[:, GCOL["attn0"]:GCOL["attn0"] + DC],
                              ALU.mult).then_inc(two_gains_ready, 1)
            dve.tensor_scalar(gains8[:, 0:1], gain("aq"), HD ** -0.5, None, ALU.mult).then_inc(consts_cast, 1)
            dve.tensor_scalar(gains8[:, 1:2], gain("bq"), HD ** -0.5, None, ALU.mult).then_inc(consts_cast, 1)

            def latent_lo(i):
                g = gain("cq", i) if i < QC else gain("ckv", i - QC)
                dve.wait_ge(lat_hi, i + 1)
                dve.scalar_tensor_tensor(out=alo[:, 16 + i, FIRST], in0=lat[:, i, FIRST], scalar=g,
                                         in1=ahi[:, 16 + i, FIRST].bitcast(F32), op0=ALU.mult, op1=ALU.subtract).then_inc(lat_lo, 1)

            dve.wait_ge(rstd_ready, 1)
            for i in range(QC + KVC + 1):
                dve.wait_ge(w_used, i + 1)
                dst = lat[:, i, FIRST] if i < QC + KVC else lyb[:, 0, FIRST]
                dve.tensor_tensor(dst, bank[i % 4][:, 0:SEQ], rstd[:, 0, FIRST], ALU.mult).then_inc(evac, 1)
                split_lo(dve, At(i + AHEAD))
                if i:
                    latent_lo(i - 1)
            dve.wait_ge(consts_loaded, 16)
            for dst, name in ((identb[:, :], "ident"), (causalb[:, :], "causal")):
                dve.tensor_copy(dst, const(name)).then_inc(consts_cast, 1)
            dve.tensor_copy(rowsb[:, :], c_t[:, CCOL["upper"][0]:CCOL["rep"][1]]).then_inc(consts_cast, 1)
            dve.wait_ge(kr_rot, 1)
            dve.tensor_tensor(kro[64:96, FIRST], bank[7][64:96, 0:SEQ], const("sinm")[64:96, :], ALU.mult).then_inc(link.sem, 1)
            dve.wait_ge(link.sem, link.next())
            dve.tensor_tensor(lyb[64:96, 1, FIRST], lyb[64:96, 0, FIRST], const("cosm")[64:96, :], ALU.mult).then_inc(link.sem, 1)
            dve.wait_ge(link.sem, link.next())
            dve.tensor_tensor(kro[64:96, FIRST], kro[64:96, FIRST], lyb[64:96, 1, FIRST], ALU.add).then_inc(kr_done, 1)
            proj_dve(dve, link, "sv", "v", FIRST)
            proj_dve(dve, link, "sq", "plain", FIRST, first=0, scale=HD ** -0.5)
            proj_dve(dve, link, "sk", "plain", FIRST, first=4 * T)

            def rotate(i):
                dve.wait_ge(m_rot, i + 1)
                dve.wait_ge(m_cos, i + 1)
                dve.tensor_tensor(mq[64:96, i, :], bank[7][64:96, 0:SEQ], const("sinm")[64:96, :], ALU.mult).then_inc(m_sin, 1)

            dve.wait_ge(lat_rstd, 2)
            stick = stick_dve(dve)
            for i in range(8):
                n = START["mla"] + i
                if i % 2 == 0:
                    stick(0, i // 2)
                dve.wait_ge(w_used, n + 1)
                dve.scalar_tensor_tensor(out=mq[:, i, :], in0=bank[0][:, 0:SEQ], scalar=SCALE_A, in1=rstd[:, 1, FIRST],
                                         op0=ALU.mult, op1=ALU.mult).then_inc(evac, 1)
                dve.tensor_tensor(mk[:, i, :], bank[4][:, 0:SEQ], rstd[:, 2, FIRST], ALU.mult).then_inc(evac, 1)
                split_lo(dve, At(n + AHEAD))
                if i:
                    rotate(i - 1)
                if i % 2 == 0:
                    stick(1, i // 2)
            rotate(7)

        def first_pool(pool):
            for i in range(8):
                pool.wait_ge(evac, BSTART["mla"] + 2 * i + 1)
                if i > 0:
                    pool.wait_ge(m_qdone, i)
                pool.tensor_tensor(turned[64:96], mq[64:96, i, :], const("cosm")[64:96, :], ALU.mult).then_inc(m_cos, 1)
                pool.wait_ge(m_sin, i + 1)
                pool.wait_ge(m_cos, i + 1)
                pool.tensor_tensor(mq[64:96, i, :], mq[64:96, i, :], turned[64:96], ALU.add).then_inc(m_qdone, 1)

        def stick_pe(pe):
            def z(s):
                for b in range(2):
                    q, k = half(sbq[:, s, FIRST], b), half(sbk[:, s, FIRST], b)
                    if s > 0:
                        pe.wait_ge(z_arg, 2 * s)
                    pe.matmul(bank[2 + b][:, 0:256], k[:, 0:128], q, start=True, stop=True)
                    mm = pe.matmul(bank[2 + b][:, 256:384], k[:, 128:256], q[:, 128:256], start=True, stop=True)
                mm.then_inc(z_ready, 1)

            def sums(s):
                pe.wait_ge(z_masked, 4 * (s + 1))
                pe.wait_ge(z_split, 4 * (s + 1))
                for b in range(2):
                    dst, x = bank[2 + b], nlk[:, b, :]
                    pe.matmul(dst[:, 0:256], const("laterneg"), x[:, 0:256], start=True, stop=False, skip_group_check=True)
                    pe.matmul(dst[:, 128:256], const("allneg"), x[:, 256:384], start=False, stop=True, skip_group_check=True)
                    mm = pe.matmul(dst[:, 256:384], const("laterneg"), x[:, 256:384], start=True, stop=True, skip_group_check=True)
                mm.then_inc(z_sum, 1)

            def values(s):
                pe.wait_ge(z_w, 4 * (s + 1))
                if s > 0:
                    pe.wait_ge(z_olo, s)
                for b in range(2):
                    v = [scr[:, L0 + s * 256 + t * 128 + 64 * b:][:, 0:64] for t in range(2)]
                    dst, w = bank[1][64 * b:64 * b + 64, :], zlog[:, b, :]
                    pe.matmul(dst[:, 0:256], v[0], w[:, 0:256], start=True, stop=False, skip_group_check=True)
                    mm = pe.matmul(dst[:, 128:256], v[1], w[:, 256:384], start=False, stop=True, skip_group_check=True)
                mm.then_inc(z_o, 1)

            def step(at, s):
                if at == 0 and s < 4:
                    z(s)
                if at == 0 and 1 <= s <= 4:
                    values(s - 1)
                if at == 1 and s < 4:
                    sums(s)
            return step

        def stick_act(act, link):
            def logs(s):
                for b in range(2):
                    act.wait_ge(z_ready, s + 1)
                    z = zlog[:, b, :]
                    if s > 0:
                        act.wait_ge(z_o, s)
                    act.activation(z, bank[2 + b][:, 0:384], ACT.Abs).then_inc(link.sem, 1)
                    act.wait_ge(link.sem, link.next())
                    act.activation(z, z, ACT.Exp, scale=-1.0).then_inc(link.sem, 1)
                    act.wait_ge(link.sem, link.next())
                    act.activation(z, z, ACT.Ln, bias=bias[:, 1:2]).then_inc(z_log, 1)

            def step(at, s):
                if at == 0 and 1 <= s <= 4:
                    act.wait_ge(z_o, s)
                    act.activation(ahi[:, 3 + s, FIRST], bank[1][:, 0:256], ACT.Copy).then_inc(z_ohi, 1)
                if at == 0 and s < 4:
                    logs(s)
                if at == 1 and s < 4:
                    for b in range(2):
                        act.wait_ge(z_arg, 2 * s + b + 1)
                        act.activation(zlog[:, b, :], ls[:, b, :], ACT.Exp).then_inc(z_exp, 1)
            return step

        def stick_dve(dve):
            before = const("before")

            def step(at, s):
                if at == 0 and 1 <= s <= 4:
                    dve.wait_ge(z_ohi, s)
                    dve.tensor_tensor(alo[:, 3 + s, FIRST], bank[1][:, 0:256], ahi[:, 3 + s, FIRST].bitcast(F32),
                                      ALU.subtract).then_inc(z_olo, 1)
                if at == 0 and s < 4:
                    for b in range(2):
                        dve.wait_ge(z_log, 2 * s + b + 1)
                        z = bank[2 + b][:, 0:384]
                        dve.scalar_tensor_tensor(out=nlk[:, b, :], in0=z, scalar=0.0, in1=zlog[:, b, :], op0=ALU.max,
                                                 op1=ALU.add).then_inc(z_split, 1)
                        dve.scalar_tensor_tensor(out=ls[:, b, :], in0=z, scalar=0.0, in1=zlog[:, b, :], op0=ALU.min,
                                                 op1=ALU.subtract).then_inc(z_split, 1)
                        dve.wait_ge(z_split, 4 * s + 2 * b + 1)
                        for c in (0, 256):
                            dve.tensor_tensor(nlk[:, b, c:c + 128], nlk[:, b, c:c + 128], before, ALU.mult).then_inc(z_masked, 1)
                if at == 1 and s < 4:
                    dve.wait_ge(z_sum, s + 1)
                    for b in range(2):
                        dve.tensor_tensor(ls[:, b, :], ls[:, b, :], bank[2 + b][:, 0:384], ALU.add).then_inc(z_arg, 1)
                    for b in range(2):
                        dve.wait_ge(z_exp, 2 * s + b + 1)
                        for c in (0, 256):
                            dve.tensor_tensor(zlog[:, b, c:c + 128], zlog[:, b, c:c + 128], before, ALU.mult).then_inc(z_w, 1)
            return step

        def stick_end(step):
            def hook(at, s):
                if (at, s) == (1, 0):
                    step(0, 4)
            return hook

        def wi_pe(pe):
            b = BSTART["wi"]
            pe.wait_ge(evac, b + 1)
            for t in range(3):
                w = min(128, T - 128 * t)
                mm = pe.transpose(bank[6][0:w, 8 * t:8 * t + 8], relu_t[0:8, 0, 128 * t:128 * t + w], const("ident")[0:8, 0:8])
            mm.then_inc(wi_turned, 1)

        def wi_dve(dve):
            n, b = START["wi"], BSTART["wi"]
            split_lo(dve, At(n + AHEAD))
            dve.wait_ge(w_used, n + 1)
            dve.tensor_tensor(relu_t[0:8, 0, :], bank[b % 4][0:8, 0:T], rstd[0:8, 0, :], ALU.mult).then_inc(evac, 1)
            dve.wait_ge(wi_turned, 1)
            k = 8 ** -0.5 * HD ** -0.5
            dve.tensor_scalar(wi[:, 0:16], bank[6][:, 0:16], k, None, ALU.mult).then_inc(wi_done, 1)
            dve.tensor_scalar(wi[0:META, 16:24], bank[6][0:META, 16:24], k, None, ALU.mult).then_inc(wi_done, 1)

        def index_pe(pe):
            pe.wait_ge(y_turned, 5)
            pe.wait_ge(wi_done, 2)
            for i in range(8):
                q, k = half(q_all[:, i // 2, :], i), half(q_all[:, 4, :], i)
                big, tail = (bank[5], bank[7]) if i % 2 == 0 else (bank[6], bank[4])
                if 2 * (i - 1) > 0:
                    pe.wait_ge(ix_relu, 2 * (i - 1))
                pe.matmul(big[:, 0:128], q[:, 0:128], k[:, 0:128], start=True, stop=True)
                pe.matmul(big[:, 128:384], q[:, 128:256], k[:, 0:256], start=True, stop=True)
                pe.matmul(tail[0:META, 0:T], q[:, 256:T], k[:, 0:T], start=True, stop=True).then_inc(ix_ready, 1)

        def index_act(act):
            for i in range(8):
                big, tail = (bank[5], bank[7]) if i % 2 == 0 else (bank[6], bank[4])
                act.wait_ge(ix_ready, i + 1)
                if 3 * (i - 1) > 0:
                    act.wait_ge(ix_acc, 3 * (i - 1))
                act.activation(relu[:, i % 2, 0:384], big[:, 0:384], ACT.Relu).then_inc(ix_relu, 1)
                act.activation(relu_t[0:META, i % 2, :], tail[0:META, 0:T], ACT.Relu).then_inc(ix_relu, 1)

        def index_dve(dve):
            dve.memset(score[0], NEG).then_inc(ix_clear, 1)
            dve.wait_ge(ix_clear, 1)
            for i in range(8):
                dve.wait_ge(ix_relu, 2 * (i + 1))
                for t, (src, rows, dst) in enumerate((
                        (relu[64:P, i % 2, 0:128], slice(64, P), score[0][64:P, 0:128]),
                        (relu[:, i % 2, 128:384], slice(0, P), score[1]),
                        (relu_t[0:META, i % 2, :], slice(0, META), score[0][0:META]))):
                    w = wi[rows, 8 * t + i:8 * t + i + 1]
                    if i == 0:
                        dve.tensor_scalar(dst, src, w, None, ALU.mult).then_inc(ix_acc, 1)
                    else:
                        dve.wait_ge(ix_acc, 3 * (i - 1) + t + 1)
                        dve.scalar_tensor_tensor(out=dst, in0=src, scalar=w, in1=dst, op0=ALU.mult, op1=ALU.add).then_inc(ix_acc, 1)

        TOPK_STEPS = TOPK // 8 + 2

        def add_causal(dve, link, t):
            cm = const("causal")
            for sc, m in ((score[0][64:P, 0:128], cm[64:P]), (score[0][0:META, 256:T], cm[0:META, 0:META])) if t == 0 else (
                    (score[1][:, 128:256], cm),):
                dve.tensor_tensor(sc, sc, m, ALU.add).then_inc(link.sem, 1)
                dve.wait_ge(link.sem, link.next())

        def topk_step(dve, link, t, n):
            sc = score[t]
            if n == 0:
                dve.wait_ge(ix_acc, 24)
                add_causal(dve, link, t)
            elif n < TOPK_STEPS - 1:
                dve.max(out=best, in_=sc).then_inc(link.sem, 1)
                dve.wait_ge(link.sem, link.next())
                dve.match_replace(out=sc, in_to_replace=best, in_values=sc, imm_value=TAKEN).then_inc(link.sem, 1)
                dve.wait_ge(link.sem, link.next())
            else:
                dve.tensor_scalar(sc, sc, TAKEN * 0.9, NEG, ALU.is_gt, ALU.mult).then_inc(link.sem, 1)
                dve.wait_ge(link.sem, link.next())
                add_causal(dve, link, t)
                if t == 0:
                    dve.tensor_copy(selmask[0:64, 0:128], causalb[0:64, :]).then_inc(ix_mask, 1)
                    dve.tensor_copy(selmask[64:P, 0:128], sc[64:P, 0:128]).then_inc(ix_mask, 1)
                    dve.tensor_copy(selmask[0:META, 384:384 + T], sc[0:META]).then_inc(ix_mask, 1)
                else:
                    dve.tensor_copy(selmask[:, 128:384], sc).then_inc(ix_mask, 1)

        def topk_between(dve, link, first):
            def between(j):
                for n in range(2 * TOPK_STEPS * (first + j) // 12, min(2 * TOPK_STEPS, 2 * TOPK_STEPS * (first + j + 1) // 12)):
                    topk_step(dve, link, n // TOPK_STEPS, n % TOPK_STEPS)
            return between

        tailq = area(E0 + 1760, 128)
        tprob = area(E0 + 664, T)
        tprobT = area(E0 + 664 + T, 384)

        def tail_pe(pe):
            idn = const("ident")
            s, pt, o = bank[2], bank[3], bank[1]

            def scores(t):
                pe.wait_ge(t_q, 1)
                if t > 0:
                    pe.wait_ge(t_exp, t)
                for r in range(4):
                    g, par = 2 * t + r // 2, r % 2
                    q = tailq[64 * par:64 * par + 64, 32 * g:32 * g + 32]
                    pe.matmul(s[32 * r:32 * r + 32, 0:T], q, k_all[64 * par:64 * par + 64, g, 0:T], start=True, stop=False,
                              skip_group_check=True)
                pe.matmul(s[:, 0:T], repb, selmask[0:META, 384:384 + T], start=False, stop=True,
                          skip_group_check=True).then_inc(t_s, 1)

            def turn(t):
                pe.wait_ge(t_p, t + 1)
                if t > 0:
                    pe.wait_ge(t_pts, 2 * t)
                pe.transpose(pt[0:META, 256:384], tprob[:, 256:T], idn)
                pe.transpose(pt[:, 0:128], tprob[:, 0:128], idn)
                pe.transpose(pt[:, 128:256], tprob[:, 128:256], idn).then_inc(t_pt, 1)

            def values(t):
                pe.wait_ge(t_pts, 2 * (t + 1))
                if t > 0:
                    pe.wait_ge(t_olo, t)
                for r in range(4):
                    g, par = 2 * t + r // 2, r % 2
                    dst = o[64 * par:64 * par + 64, 32 * (r // 2):32 * (r // 2) + 32]
                    for tile, rows in ((0, P), (1, P), (2, META)):
                        c = V0 + (g // 2) * 384 + tile * 128 + 64 * (g % 2)
                        mm = pe.matmul(dst, scr[0:rows, c:c + 64], tprobT[0:rows, 128 * tile + 32 * r:128 * tile + 32 * r + 32],
                                       start=tile == 0, stop=tile == 2, skip_group_check=True)
                mm.then_inc(t_o, 1)

            def step(at, n):
                if (at, n) == (1, 1):
                    scores(0)
                if (at, n) == (1, 3):
                    turn(0)
                if (at, n) == (1, 4):
                    values(0)
                    scores(1)
                if (at, n) == (1, 6):
                    turn(1)
                if (at, n) == (1, 7):
                    values(1)
            return step

        def tail_act(act):
            def exp(t):
                act.wait_ge(t_max, t + 1)
                if t > 0:
                    act.wait_ge(t_pt, t)
                act.activation(tprob, bank[2][:, 0:T], ACT.Exp, bias=small[:, 16:17], accum_out=small[:, 17:18]).then_inc(t_exp, 1)

            def copy(t):
                act.wait_ge(t_pt, t + 1)
                if t > 0:
                    act.wait_ge(t_o, t)
                act.activation(tprobT[0:META, 256:384], bank[3][0:META, 256:384], ACT.Copy).then_inc(t_pts, 1)
                act.activation(tprobT[:, 0:256], bank[3][:, 0:256], ACT.Copy).then_inc(t_pts, 1)

            def out_hi(t):
                act.wait_ge(t_o, t + 1)
                act.activation(ahi[:, 4 * t:4 * t + 4, 256:T], bank[1][:, 0:64].rearrange("p (c n) -> p c n", n=META),
                               ACT.Copy).then_inc(t_ohi, 1)

            def step(at, n):
                if (at, n) == (0, 2):
                    exp(0)
                if (at, n) == (0, 4):
                    copy(0)
                if (at, n) == (0, 5):
                    out_hi(0)
                    exp(1)
                if (at, n) == (0, 7):
                    copy(1)
                if (at, n) == (0, 8):
                    out_hi(1)
            return step

        def tail_dve(dve, link):
            def row_max(t):
                dve.wait_ge(t_s, t + 1)
                dve.tensor_reduce(small[:, 16:17], bank[2][:, 0:T], AX.X, ALU.max, negate=True).then_inc(t_max, 1)

            def norm(t):
                dve.wait_ge(t_exp, t + 1)
                dve.reciprocal(small[:, 18:19], small[:, 17:18]).then_inc(link.sem, 1)
                dve.wait_ge(link.sem, link.next())
                dve.tensor_scalar(tprob, tprob, small[:, 18:19], None, ALU.mult).then_inc(t_p, 1)

            def tail_lo(t):
                dve.wait_ge(t_ohi, t + 1)
                dve.tensor_tensor(alo[:, 4 * t:4 * t + 4, 256:T], bank[1][:, 0:64].rearrange("p (c n) -> p c n", n=META),
                                  ahi[:, 4 * t:4 * t + 4, 256:T].bitcast(F32), ALU.subtract).then_inc(t_olo, 1)

            def step(at, n):
                if (at, n) == (0, 0):
                    dve.wait_ge(y_turned, 17)
                    dve.tensor_copy(tailq.rearrange("p (c n) -> p c n", n=META), q_all[:, :, 256:T]).then_inc(t_q, 1)
                if (at, n) == (1, 1):
                    row_max(0)
                if (at, n) == (1, 2):
                    norm(0)
                if (at, n) == (1, 4):
                    row_max(1)
                if (at, n) == (1, 5):
                    tail_lo(0)
                    norm(1)
                if (at, n) == (1, 8):
                    tail_lo(1)
            return step

        fx, fe, fc = area(E0 + 1760, T), area(E0 + 1760 + T, T), area(S0 + 4 * T, T)

        def forget_pe(pe):
            n, b = START["ff"], BSTART["ff"]
            pe.wait_ge(evac, b - 3)
            unit_mm(pe, At(n), bank[b % 4][:, 0:T], uhi, ulo, WHOLE, x=u_chunk(6))
            norm_pe(pe, 6, WHOLE)

        def forget_act(act, link, j):
            if j != 1:
                return
            x, e = fx[0:16], fe[0:16]
            act.wait_ge(f_exp, 1)
            act.activation(e, x, ACT.Abs).then_inc(link.sem, 1)
            act.wait_ge(link.sem, link.next())
            act.activation(e, e, ACT.Exp, scale=-1.0).then_inc(link.sem, 1)
            act.wait_ge(link.sem, link.next())
            act.activation(e, e, ACT.Ln, bias=bias[0:16, 1:2]).then_inc(f_log, 1)

        def forget_unit_dve(dve):
            n, b = START["ff"], BSTART["ff"]
            dve.wait_ge(rstd_ready, 7)
            dve.wait_ge(w_used, n + 1)
            dve.tensor_tensor(fx[0:16], bank[b % 4][0:16, 0:T], rstd[0:16, 0, :], ALU.mult).then_inc(evac, 1)
            split_lo(dve, At(n + AHEAD))

        def forget_dve(dve, link, j):
            x, l, c = fx[0:16], fe[0:16], fc[0:16]
            if j == 0:
                dve.wait_ge(evac, BSTART["ff"] + 1)
                dve.tensor_scalar(x, x, gain("fb")[0:16], None, ALU.add).then_inc(f_exp, 1)
                dve.memset(csplit[:, :], 0.0).then_inc(link.sem, 1)
                dve.wait_ge(link.sem, link.next())
            if j == 2:
                dve.wait_ge(f_log, 1)
                dve.scalar_tensor_tensor(out=x, in0=x, scalar=0.0, in1=l, op0=ALU.min, op1=ALU.subtract).then_inc(link.sem, 1)
                dve.wait_ge(link.sem, link.next())
                dve.memset(l, 1.0).then_inc(link.sem, 1)
                dve.wait_ge(link.sem, link.next())
            if j == 3:
                dve.tensor_tensor_scan(c, l, x, 0.0, ALU.mult, ALU.add).then_inc(link.sem, 1)
                dve.wait_ge(link.sem, link.next())
                dve.tensor_scalar(c, c, -1.0, None, ALU.mult).then_inc(link.sem, 1)
                dve.wait_ge(link.sem, link.next())
            if 4 <= j < 7:
                k = j - 4
                part = csplit[32 * k:32 * k + 16, :]
                dve.tensor_copy(part, c).then_inc(f_split, 1)
                dve.wait_ge(f_split, k + 1)
                if k < 2:
                    dve.tensor_copy(l, part).then_inc(link.sem, 1)
                    dve.wait_ge(link.sem, link.next())
                    dve.tensor_tensor(c, c, l, ALU.subtract).then_inc(link.sem, 1)
                    dve.wait_ge(link.sem, link.next())

        def second_u_act(act):
            for m in range(DC):
                act.activation(ahi[:, 8 + m, :], h[:, m, :], ACT.Copy, scale=gain("attn1", m)).then_inc(u2_hi, 1)

        def second_u_dve(dve):
            for m in range(DC):
                dve.wait_ge(u2_hi, m + 1)
                dve.scalar_tensor_tensor(out=alo[:, 8 + m, :], in0=h[:, m, :], scalar=gain("attn1", m),
                                         in1=ahi[:, 8 + m, :].bitcast(F32), op0=ALU.mult, op1=ALU.subtract).then_inc(u2_lo, 1)

        block = ctx.enter_context(nc.Block())

        @block.sync
        def _(sp):
            sp.dma_start(g_t[:, :], gains).then_inc(gains_loaded, 16)
            for i in range(4):
                sp.dma_start(h[:, 2 * i:2 * i + 2, FIRST], xT[:, 2 * i:2 * i + 2, :]).then_inc(x_loaded[i], 16)
            for s in range(RING):
                sp.dma_start(raw[:, s, :], stream[s]).then_inc(w_loaded[s], 16)
            sp.dma_start(c_t[:, :], consts).then_inc(consts_loaded, 16)
            sp.dma_start(h[:, :, 0:META], metaT).then_inc(meta_loaded, 16)
            with sp.Fori(1, UNITS // RING) as it:
                for s in range(RING):
                    sp.wait_ge(w_lo, it * RING + (s - RING + 1))
                    sp.dma_start(raw[:, s, :], stream[bass.ds(it * RING + s, 1)].rearrange("a p n -> (a p) n")).then_inc(w_loaded[s], 16)
            for s in range(UNITS % RING):
                n = UNITS // RING * RING + s
                sp.wait_ge(w_lo, n - RING + 1)
                sp.dma_start(raw[:, s, :], stream[n]).then_inc(w_loaded[s], 16)
            for m in range(DC):
                sp.wait_ge(evac, BSTART["dn3"] + m + 1)
                sp.dma_start(out[:, m, :], h[:, m, META:T]).then_inc(stored, 16)
            sp.wait_ge(stored, 16 * DC)

        @block.tensor
        def _(pe):
            pe.wait_ge(bias_set, 3)
            first_pe(pe)
            pe.wait_ge(consts_cast, 5)
            pe.wait_ge(evac, BSTART["out0"])
            att_pe(pe, mla, stick_end(stick_pe(pe)))
            resid_pe(pe, "out0", DC, FIRST, lambda i: (o_lo, i + 1) if i < 4 else (z_olo, i - 3))
            swiglu_pe(pe, "gu0", FIRST, 1)
            resid_pe(pe, "dn0", FC1, FIRST, lambda i: (a_lo, i + 1))
            proj_pe(pe, "bv", "v", FIRST, 2, sum_norm=2)
            proj_pe(pe, "bq", "plain", FIRST, 2)
            proj_pe(pe, "bk", "plain", FIRST, 2)
            pe.wait_ge(evac, BSTART["out1"])
            pe.wait_ge(v_stored, VFIRST["dv"])
            att_pe(pe, band)
            resid_pe(pe, "out1", DC, FIRST, lambda i: (o_lo, 4 + i + 1))
            swiglu_pe(pe, "gu1", FIRST, 3)
            resid_pe(pe, "dn1", FC1, FIRST, lambda i: (a_lo, FC1 + i + 1))
            pe.wait_ge(meta_lo, DC)
            proj_pe(pe, "ki", "rope", WHOLE, BETWEEN, sum_norm=BETWEEN,
                    meanwhile=[("wi", 0, WHOLE), ("qi", 0, WHOLE)])
            wi_pe(pe)
            proj_pe(pe, "qi", "rope", WHOLE, BETWEEN, done=1, 
                    meanwhile=[("dk", 0, WHOLE), ("dk", 1, WHOLE), ("dk", 2, WHOLE)])
            index_pe(pe)
            pe.wait_ge(ix_relu, 16)
            proj_pe(pe, "dk", "rmsrope", WHOLE, BETWEEN, done=3, meanwhile=[("dv", 0, WHOLE), ("dv", 1, WHOLE)])
            pe.wait_ge(y_turned, 9)
            pe.wait_ge(y_rstd, 4)
            proj_pe(pe, "dv", "v", WHOLE, BETWEEN, done=2, meanwhile=[("dq", 0, WHOLE)])
            pe.wait_ge(v_stored, VFIRST["fv"])
            proj_pe(pe, "dq", "rmsrope", WHOLE, BETWEEN, done=1)
            pe.wait_ge(ix_mask, 4)
            att_pe(pe, dsa, tail_pe(pe))
            pe.wait_ge(t_olo, 2)
            resid_pe(pe, "out2", DC, WHOLE, lambda i: (o_lo, 12 + i + 1))
            sqrelu_pe(pe, "up2", WHOLE, 5)
            resid_pe(pe, "dn2", FC2, WHOLE, lambda i: (a_lo, 2 * FC1 + i + 1))
            forget_pe(pe)
            proj_pe(pe, "fv", "v", WHOLE, 6, meanwhile=[("fk", 0, WHOLE)])
            pe.wait_ge(v_stored, 22)
            proj_pe(pe, "fk", "rms", WHOLE, 6, done=1, meanwhile=[("fq", 0, FIRST, True)])
            proj_pe(pe, "fq", "rms", FIRST, 6, second=True, done=1)
            pe.wait_ge(y_done, 16)
            pe.wait_ge(f_split, 3)
            pe.wait_ge(sel_loaded, 16)
            att_pe(pe, fox)
            resid_pe(pe, "out3", DC, FIRST, lambda i: (o_lo, 20 + i + 1))
            sqrelu_pe(pe, "up3", FIRST, 7)
            resid_pe(pe, "dn3", FC2, FIRST, lambda i: (a_lo, 2 * FC1 + FC2 + i + 1))

        @block.scalar
        def _(act):
            act.preload_act_table_set("natural_log_exp_and_others")
            link = Chain(act_chain)
            first_act(act, link)
            act.wait_ge(m_kdone, 8)
            act.wait_ge(m_qdone, 8)
            att_act(act, link, mla, stick_end(stick_act(act, link)))
            resid_act(act, link, "out0", DC, FIRST, 1, "ffn0")
            swiglu_act(act, link, "gu0", FIRST)
            resid_act(act, link, "dn0", FC1, FIRST, 2, "mix1")
            proj_act(act, link, "bv", "v", FIRST)
            proj_act(act, link, "bq", "plain", FIRST)
            proj_act(act, link, "bk", "plain", FIRST)

            def relh_load(where, s):
                if where == 0 and s < band.pairs:
                    if s == 0:
                        act.wait_ge(evac, BSTART["out1"])
                        for n in (0, 1):
                            act.dma_start(relb[:, n, :, :], relh[n]).then_inc(rel_loaded[n], 16)
                if where == 1 and s + 2 < band.pairs:
                    act.wait_ge(s_ready, band.head0 + 2 * s + 2)
                    act.dma_start(relb[:, s % 2, :, :], relh[s + 2]).then_inc(rel_loaded[s % 2], 16)
            att_act(act, link, band, relh_load)
            resid_act(act, link, "out1", DC, FIRST, 3, "ffn1")
            swiglu_act(act, link, "gu1", FIRST)
            resid_act(act, link, "dn1", FC1, FIRST, 4, "final")
            proj_act(act, link, "ki", "rope", WHOLE)
            split_hi(act, At(START["wi"] + AHEAD))
            proj_act(act, link, "qi", "rope", WHOLE)
            index_act(act)
            proj_act(act, link, "dk", "rmsrope", WHOLE)
            proj_act(act, link, "dv", "v", WHOLE)
            proj_act(act, link, "dq", "rmsrope", WHOLE)
            att_act(act, link, dsa, tail_act(act))
            resid_act(act, link, "out2", DC, WHOLE, 5, "mlp0")
            sqrelu_act(act, "up2", WHOLE)
            resid_act(act, link, "dn2", FC2, WHOLE, 6, "kvn")
            act.dma_start(area(E0, 1024)[0:96, :], sel).then_inc(sel_loaded, 16)
            split_hi(act, At(START["ff"] + AHEAD))
            proj_act(act, link, "fv", "v", WHOLE, between=lambda j: forget_act(act, link, j))
            second_u_act(act)
            proj_act(act, link, "fk", "rms", WHOLE)
            proj_act(act, link, "fq", "rms", FIRST)
            att_act(act, link, fox)
            resid_act(act, link, "out3", DC, FIRST, 7, "mlp1")
            sqrelu_act(act, "up3", FIRST)
            resid_act(act, link, "dn3", FC2, FIRST, None, None)

        @block.vector
        def _(dve):
            link = Chain(dve_chain)
            first_dve(dve, link)
            att_dve(dve, link, mla, stick_end(stick_dve(dve)))
            resid_dve(dve, "out0", DC, FIRST, 1, "ffn0")
            swiglu_dve(dve, "gu0", FIRST, 1, 0)
            resid_dve(dve, "dn0", FC1, FIRST, 2, "mix1")
            proj_dve(dve, link, "bv", "v", FIRST, norm=2)
            proj_dve(dve, link, "bq", "plain", FIRST, first=Q0, scale=HD ** -0.5, norm=2)
            proj_dve(dve, link, "bk", "plain", FIRST, first=K0, norm=2)
            att_dve(dve, link, band)
            resid_dve(dve, "out1", DC, FIRST, 3, "ffn1")
            swiglu_dve(dve, "gu1", FIRST, 3, FC1)
            resid_dve(dve, "dn1", FC1, FIRST, 4, "final")
            between_dve(dve)
            proj_dve(dve, link, "ki", "rope", WHOLE, first=4 * T, norm=BETWEEN)
            wi_dve(dve)
            x2_dve(dve)
            proj_dve(dve, link, "qi", "rope", WHOLE, first=0, norm=BETWEEN)
            index_dve(dve)
            proj_dve(dve, link, "dk", "rmsrope", WHOLE, first=K0, gcol=gain("ak"), norm=BETWEEN, between=topk_between(dve, link, 0))
            proj_dve(dve, link, "dv", "v", WHOLE, norm=BETWEEN, between=topk_between(dve, link, 4))
            proj_dve(dve, link, "dq", "rmsrope", WHOLE, first=Q0, gcol=gains8[:, 0:1], norm=BETWEEN,
                     between=topk_between(dve, link, 6))
            att_dve(dve, link, dsa, tail_dve(dve, link))
            dve.wait_ge(x2_done, DC)
            resid_dve(dve, "out2", DC, WHOLE, 5, "mlp0")
            sqrelu_dve(dve, "up2", WHOLE, 5, 2 * FC1)
            resid_dve(dve, "dn2", FC2, WHOLE, 6, "kvn")
            forget_unit_dve(dve)
            proj_dve(dve, link, "fv", "v", WHOLE, norm=6, between=lambda j: forget_dve(dve, link, j))
            second_u_dve(dve)
            proj_dve(dve, link, "fk", "rms", WHOLE, first=K0, gcol=gain("kk"), norm=6)
            proj_dve(dve, link, "fq", "rms", FIRST, first=Q0, gcol=gains8[:, 1:2], norm=6)
            att_dve(dve, link, fox)
            resid_dve(dve, "out3", DC, FIRST, 7, "mlp1")
            sqrelu_dve(dve, "up3", FIRST, 7, 2 * FC1 + FC2)
            resid_dve(dve, "dn3", FC2, FIRST, None, None)

        @block.gpsimd
        def _(pool):
            pool.memset(bias[:, 0:1], EPS).then_inc(bias_set, 1)
            pool.memset(bias[:, 1:2], 1.0).then_inc(bias_set, 1)
            pool.memset(ones[:, :], 1.0).then_inc(bias_set, 1)
            norm_pool(pool, 0, FIRST)
            first_pool(pool)
            norm_pool(pool, 1, FIRST)
            swiglu_pool(pool, "gu0", FIRST, 1, 0)
            norm_pool(pool, 2, FIRST)
            norm_pool(pool, 3, FIRST)
            swiglu_pool(pool, "gu1", FIRST, 3, FC1)
            norm_pool(pool, 4, FIRST)
            proj_pool(pool, "ki", "rope", WHOLE, 4 * T)
            proj_pool(pool, "qi", "rope", WHOLE, 0)
            proj_pool(pool, "dk", "rmsrope", WHOLE, K0)
            proj_pool(pool, "dq", "rmsrope", WHOLE, Q0)
            norm_pool(pool, 5, WHOLE)
            sqrelu_pool(pool, "up2", WHOLE, 2 * FC1, 0)
            norm_pool(pool, 6, WHOLE)
            norm_pool(pool, 7, FIRST)
            sqrelu_pool(pool, "up3", FIRST, 2 * FC1 + FC2, FC2)


def unit_of(w, cols, chunks=None):
    u = np.zeros((P, DC, P), w.dtype)
    k = w.shape[0] // P
    u[:, :k, :len(cols)] = w[:, cols].reshape(k, P, len(cols)).transpose(1, 0, 2)
    return u.reshape(P, UNIT)


def blocks_of(w, first, last):
    units = []
    for c in range(first, last, P):
        for r in range(0, w.shape[0], UNIT):
            units.append(unit_of(w[r:r + UNIT], np.arange(c, c + P)))
    return units


def stream_of(a):
    w_in = a["ev_w_in"][0]
    o = QL + KVL + ROPE
    nb = 8 * HD
    s = blocks_of(w_in, 0, QL) + blocks_of(w_in, QL, QL + KVL)
    kr = unit_of(w_in, np.arange(QL + KVL, o)).reshape(P, DC, P)
    moved = np.zeros_like(kr)
    moved[:, :, NOPE:NOPE + ROPE] = kr[:, :, 0:ROPE]
    s.append(moved.reshape(P, UNIT))
    s += blocks_of(w_in, o + 2 * nb, o + 3 * nb) + blocks_of(w_in, o, o + nb) + blocks_of(w_in, o + nb, o + 2 * nb)
    uq, ukv = a["ev_w_uq"][0], a["ev_w_ukv"][0]
    for i in range(8):
        u = np.zeros((P, DC, P), uq.dtype)
        u[:, :QC] = unit_of(uq, np.arange(96 * i, 96 * i + 96)).reshape(P, DC, P)[:, :QC]
        u[:, QC:QC + KVC] = unit_of(ukv, np.arange(128 * i, 128 * i + 128)).reshape(P, DC, P)[:, :KVC]
        s.append(u.reshape(P, UNIT))
    s += blocks_of(a["ev_w_out"][0], 0, D)

    def swiglu(layer):
        g, u = blocks_of(a["w_gate"][layer], 0, FF1), blocks_of(a["w_up"][layer], 0, FF1)
        return [x for pair in zip(g, u) for x in pair] + blocks_of(a["w_down"][layer], 0, D)

    s += swiglu(0)
    qkv = a["od_w_qkv"][0]
    s += blocks_of(qkv, 2 * D, 3 * D) + blocks_of(qkv, 0, D) + blocks_of(qkv, D, 2 * D) + blocks_of(a["od_w_out"][0], 0, D)
    s += swiglu(1)
    w = a["a_w_in_2"][0]
    q, k, v, qi, ki = D, D + 256, D + 512, D + 1024, D + 1088
    two = np.arange(HD)
    s.append(unit_of(w, np.concatenate([qi + two, qi + two])))
    s.append(unit_of(w, np.arange(ki, ki + 8)))
    s += blocks_of(w, v, qi)
    for g in range(4):
        s.append(unit_of(w, np.concatenate([q + HD * g + two, q + HD * g + two])))
    s += blocks_of(w, k, v) + blocks_of(w, 0, D)
    s += blocks_of(a["a_w_out_2"][0], 0, D) + blocks_of(a["mlp_w1_2"][0], 0, FF2) + blocks_of(a["mlp_w2_2"][0], 0, D)
    w = a["kv_w_2"]
    s.append(unit_of(w, np.arange(2 * D, 2 * D + 16)))
    s += blocks_of(w, D, 2 * D) + blocks_of(w, 0, D) + blocks_of(a["b_w_q_2"][0], 0, D)
    s += blocks_of(a["b_w_out_2"][0], 0, D) + blocks_of(a["mlp_w1_2"][1], 0, FF2) + blocks_of(a["mlp_w2_2"][1], 0, D)
    s += [np.zeros((P, UNIT), w.dtype)] * AHEAD
    assert len(s) == UNITS
    return np.stack(s)


def gains_of(a):
    g = np.zeros((P, NG), np.float32)

    def put(name, v):
        v = np.asarray(v)
        g[:, GCOL[name]:GCOL[name] + v.size // P] = v.reshape(-1, P).T

    for name, v in (("mix0", a["g_mix"][0]), ("ffn0", a["g_ffn"][0]), ("mix1", a["g_mix"][1]), ("ffn1", a["g_ffn"][1]),
                    ("final", a["g_final"]), ("attn0", a["attn_norm_2"][0]), ("mlp0", a["mlp_norm_2"][0]), ("kvn", a["kv_norm_2"]),
                    ("attn1", a["attn_norm_2"][1]), ("mlp1", a["mlp_norm_2"][1]), ("cq", a["ev_g_cq"][0]), ("ckv", a["ev_g_ckv"][0])):
        put(name, v)
    for name, v in (("aq", a["a_q_gain_2"][0]), ("ak", a["a_k_gain_2"][0]), ("kk", a["kv_k_gain_2"]), ("bq", a["b_q_gain_2"][0])):
        put(name, np.concatenate([v, v]))
    g[0:16, GCOL["fb"]] = a["kv_f_bias_2"]
    return g


def constants():
    c = np.zeros((P, NCONST), np.float32)

    def put(name, v):
        v = np.asarray(v, np.float32)
        c[:v.shape[0], CCOL[name][0]:CCOL[name][0] + v.shape[1]] = v

    i, j = np.arange(P)[:, None], np.arange(P)[None, :]
    put("ident", i == j)
    put("rev", i + j == P - 1)
    put("headones", i // HD == j // HD)
    put("laterneg", -(i > j).astype(np.float32))
    put("allneg", -np.ones((P, P)))
    put("before", i < j)
    put("causal", np.where(j > i, NEG, 0.0))

    def rotation(first, heads, dim):
        r = np.zeros((P, P), np.float32)
        for hd in range(heads):
            for d in range(dim // 2):
                lo = first + hd * dim + d
                r[lo + dim // 2, lo] = -1.0
                r[lo, lo + dim // 2] = 1.0
        return r

    put("rot", rotation(0, 2, HD))
    put("rotm", rotation(NOPE, 1, ROPE))

    def tables(n, dim, inv):
        ang = np.arange(n, dtype=np.float32)[:, None] * inv[None, :]
        return np.cos(ang).T.astype(np.float32), np.sin(ang).T.astype(np.float32)

    e = np.arange(0, HD, 2, dtype=np.float32) / np.float32(HD)
    cos, sin = tables(T, HD, (np.float32(1.0) / (np.float32(10000.0) ** e)).astype(np.float32))
    put("cos", np.tile(cos, (4, 1)))
    put("sin", np.tile(sin, (4, 1)))
    e = -np.arange(0, ROPE, 2, dtype=np.float32) / np.float32(ROPE)
    cos, sin = tables(SEQ, ROPE, (np.float32(10000.0) ** e).astype(np.float32))
    z = np.zeros((NOPE, SEQ), np.float32)
    put("cosm", np.concatenate([z, cos, cos]))
    put("sinm", np.concatenate([z, sin, sin]))
    put("upper", (np.arange(P) < 64)[None, :])
    put("late", np.full((1, 64), NEG))
    put("rep", (np.arange(P)[None, :] % META) == np.arange(META)[:, None])
    return c


def selection():
    s = np.zeros((96, 16, P), np.uint16)
    for k in range(3):
        for hd in range(16):
            s[32 * k + hd, hd, :] = 0x3F80
    return s.reshape(96, -1).view(np.float32)


def bias_tiles(rb):
    at = 129 + np.arange(P)[:, None] + np.arange(2 * P)[None, :]
    return np.ascontiguousarray(rb[:, at].reshape(8, 2, P, 2 * P).transpose(0, 2, 1, 3))


def kernel(**inputs):
    from concourse import bacc
    from concourse.bass_utils import run_bass_kernel_spmd

    a = {k: np.asarray(v) for k, v in inputs.items()}
    nc = bacc.Bacc("TRN2", target_bir_lowering=False, num_devices=1)

    def chunked(x):
        return np.ascontiguousarray(x.T.reshape(DC, P, x.shape[0]).transpose(1, 0, 2))

    arrays = {
        "stream": stream_of(a), "xT": chunked(a["x"][0]), "metaT": chunked(a["meta_tokens_2"]),
        "gains": gains_of(a), "consts": constants(), "relh": bias_tiles(a["od_rel_bias"][0]), "sel": selection(),
    }
    aps = [nc.dram_tensor(n, v.shape, mybir.dt.from_np(v.dtype), kind="ExternalInput").ap() for n, v in arrays.items()]
    out = nc.dram_tensor("out", (P, DC, SEQ), F32, kind="ExternalOutput").ap()
    program(nc, *aps, out)
    r = run_bass_kernel_spmd(nc, [arrays], core_ids=[0])
    got = np.asarray(r.results[0]["out"])
    return np.ascontiguousarray(got.transpose(1, 0, 2).reshape(D, SEQ).T)[None]
```
